# Optimizing a Trainium2 kernel written in Bass

```python
import math
import jax, jax.numpy as jnp
from jax import lax
import numpy as np

D_MODEL = 1024
BATCH = 1
SEQ = 256
DEPTH = 1

N_META = 16
GDN_HEADS = 8
GDN_DK = 128
GDN_DV = 128
CONV_WIDTH = 4
CHUNK = 64
ATT_HEADS = 8
ATT_KV_HEADS = 2
ATT_HD = 128
ATT_GROUP = ATT_HEADS // ATT_KV_HEADS
IDX_HEADS = 8
IDX_HD = 64
TOPK_MAX = 256
Q_BLOCK = 128
ROPE_THETA = 10000.0
D_FF = 4 * D_MODEL
EPS = 1e-6

GDN_QK_W = GDN_HEADS * GDN_DK
GDN_V_W = GDN_HEADS * GDN_DV
ATT_Q_W = ATT_HEADS * ATT_HD
ATT_KV_W = ATT_KV_HEADS * ATT_HD
SPLITS = (GDN_QK_W, GDN_QK_W, GDN_V_W, GDN_V_W, GDN_HEADS, GDN_HEADS,
          ATT_Q_W, ATT_KV_W, ATT_KV_W, IDX_HEADS * IDX_HD, IDX_HD, IDX_HEADS,
          D_MODEL, D_MODEL)
N_IN = sum(SPLITS)


def _rmsnorm(x, g):
    xf = x.astype(jnp.float32)
    y = xf * lax.rsqrt(jnp.mean(xf * xf, axis=-1, keepdims=True) + EPS)
    return (y * g.astype(jnp.float32)).astype(x.dtype)

def _l2norm(x):
    return x * lax.rsqrt(jnp.sum(x * x, axis=-1, keepdims=True) + EPS)

def _rope_tables(pos, dim):
    inv = ROPE_THETA ** (-jnp.arange(0, dim, 2, dtype=jnp.float32) / dim)
    ang = pos.astype(jnp.float32)[:, None] * inv[None, :]
    return jnp.cos(ang), jnp.sin(ang)

def _apply_rope(x, cos, sin):
    half = x.shape[-1] // 2
    xf = x.astype(jnp.float32)
    x1, x2 = xf[..., :half], xf[..., half:]
    c = cos[None, :, None, :]
    s = sin[None, :, None, :]
    return jnp.concatenate([x1 * c - x2 * s, x2 * c + x1 * s], axis=-1).astype(x.dtype)

def _causal_conv(x, w):
    K = w.shape[0]
    T = x.shape[1]
    xp = jnp.pad(x, ((0, 0), (K - 1, 0), (0, 0)))
    y = xp[:, 0:T] * w[0]
    for j in range(1, K):
        y = y + xp[:, j:j + T] * w[j]
    return y

def _gated_delta_rule(q, k, v, beta, g):
    B_, T_, H, dk = q.shape
    dv = v.shape[-1]
    C = CHUNK
    pad = (-N_META) % C
    tail = (-(T_ + pad)) % C

    def padf(a):
        return jnp.pad(a, [(0, 0), (pad, tail)] + [(0, 0)] * (a.ndim - 2))

    q, k, v, beta, g = padf(q), padf(k), padf(v), padf(beta), padf(g)
    N = (T_ + pad + tail) // C

    def vec_chunks(a):
        return a.reshape(B_, N, C, H, a.shape[-1]).transpose(0, 3, 1, 2, 4)

    def sc_chunks(a):
        return a.reshape(B_, N, C, H).transpose(0, 3, 1, 2)

    q, k, v = vec_chunks(q), vec_chunks(k), vec_chunks(v)
    beta, g = sc_chunks(beta), sc_chunks(g)
    gc = jnp.cumsum(g, axis=-1)

    tri_incl = jnp.tril(jnp.ones((C, C), dtype=bool))
    tri_strict = jnp.tril(jnp.ones((C, C), dtype=bool), -1)
    decay = jnp.exp(jnp.where(tri_incl, gc[..., :, None] - gc[..., None, :], -jnp.inf))

    kb = k * beta[..., None]
    A = jnp.where(tri_strict, jnp.einsum('bhncd,bhnsd->bhncs', kb, k) * decay, 0.0)
    eye = jnp.eye(C, dtype=jnp.float32)
    Tm = lax.linalg.triangular_solve(A + eye, jnp.broadcast_to(eye, A.shape),
                                     left_side=True, lower=True, unit_diagonal=True)
    u = jnp.einsum('bhncs,bhnse->bhnce', Tm, v * beta[..., None])
    w = jnp.einsum('bhncs,bhnsd->bhncd', Tm, kb * jnp.exp(gc)[..., None])
    attn = jnp.einsum('bhncd,bhnsd->bhncs', q, k) * decay
    q_dec = q * jnp.exp(gc)[..., None]
    k_tail = k * jnp.exp(gc[..., -1:] - gc)[..., None]
    g_last = jnp.exp(gc[..., -1])

    def to_scan(a):
        return jnp.moveaxis(a, 2, 0)

    xs = (to_scan(q_dec), to_scan(attn), to_scan(u), to_scan(w), to_scan(k_tail), to_scan(g_last))

    def step(S, inp):
        qe, at, u_i, w_i, kt, gl = inp
        v_new = u_i - jnp.einsum('bhcd,bhde->bhce', w_i, S)
        o = jnp.einsum('bhcd,bhde->bhce', qe, S) + jnp.einsum('bhcs,bhse->bhce', at, v_new)
        S = S * gl[..., None, None] + jnp.einsum('bhcd,bhce->bhde', kt, v_new)
        return S, o

    S0 = jnp.zeros((B_, H, dk, dv), jnp.float32)
    _, o = lax.scan(step, S0, xs)
    o = o.transpose(1, 0, 3, 2, 4).reshape(B_, N * C, H, dv)
    return o[:, pad:pad + T_]

def _gdn_branch(q, k, v, z, b_raw, a_raw, conv_w, a_log, dt_bias, norm_w):
    B_, T_, _ = q.shape
    dt = q.dtype
    qkv = jax.nn.silu(_causal_conv(jnp.concatenate([q, k, v], axis=-1), conv_w))
    q, k, v = jnp.split(qkv, [GDN_QK_W, 2 * GDN_QK_W], axis=-1)
    q = q.reshape(B_, T_, GDN_HEADS, GDN_DK).astype(jnp.float32)
    k = k.reshape(B_, T_, GDN_HEADS, GDN_DK).astype(jnp.float32)
    v = v.reshape(B_, T_, GDN_HEADS, GDN_DV).astype(jnp.float32)
    q = _l2norm(q) * (GDN_DK ** -0.5)
    k = _l2norm(k)
    beta = jax.nn.sigmoid(b_raw.astype(jnp.float32))
    g = -jnp.exp(a_log.astype(jnp.float32)) * jax.nn.softplus(a_raw.astype(jnp.float32) + dt_bias.astype(jnp.float32))
    o = _gated_delta_rule(q, k, v, beta, g)
    zf = z.reshape(B_, T_, GDN_HEADS, GDN_DV).astype(jnp.float32)
    o = _rmsnorm(o, norm_w) * jax.nn.silu(zf)
    return o.reshape(B_, T_, GDN_V_W).astype(dt)

def _dsa_branch(q, k, v, qi, ki, wi, rope_att, rope_idx, n_visible):
    B_, T_, _ = q.shape
    cos_a, sin_a = rope_att
    cos_i, sin_i = rope_idx
    q = _apply_rope(q.reshape(B_, T_, ATT_HEADS, ATT_HD), cos_a, sin_a)
    k = _apply_rope(k.reshape(B_, T_, ATT_KV_HEADS, ATT_HD), cos_a, sin_a)
    v = v.reshape(B_, T_, ATT_KV_HEADS, ATT_HD)
    qi = _apply_rope(qi.reshape(B_, T_, IDX_HEADS, IDX_HD), cos_i, sin_i)
    ki = _apply_rope(ki.reshape(B_, T_, 1, IDX_HD), cos_i, sin_i)[:, :, 0]
    wi = wi * ((IDX_HEADS * IDX_HD) ** -0.5)
    kv = jnp.concatenate([k, v], axis=-1)
    topk = min(TOPK_MAX, n_visible // 4)
    nb = -(-T_ // Q_BLOCK)
    Tq = nb * Q_BLOCK

    def to_blocks(a):
        a = jnp.pad(a, [(0, 0), (0, Tq - T_)] + [(0, 0)] * (a.ndim - 2))
        return jnp.moveaxis(a.reshape((B_, nb, Q_BLOCK) + a.shape[2:]), 1, 0)

    key_pos = jnp.arange(T_, dtype=jnp.int32)

    def block(args):
        qb, qib, wib, posb = args
        s = jnp.einsum('bqhd,bsd->bqhs', qib, ki)
        s = jnp.einsum('bqhs,bqh->bqs', jax.nn.relu(s), wib).astype(jnp.float32)
        s = jnp.where(key_pos[None, None, :] <= posb[None, :, None], s, -jnp.inf)
        _, idx = lax.top_k(s, topk)
        kv_sel = jax.vmap(lambda a, i: a[i])(kv, idx)
        k_sel, v_sel = jnp.split(kv_sel, 2, axis=-1)
        qg = qb.reshape(B_, Q_BLOCK, ATT_KV_HEADS, ATT_GROUP, ATT_HD)
        logits = jnp.einsum('bqgrd,bqkgd->bqgrk', qg, k_sel).astype(jnp.float32) * (ATT_HD ** -0.5)
        valid = (idx <= posb[None, :, None])[:, :, None, None, :]
        p = jax.nn.softmax(jnp.where(valid, logits, -jnp.inf), axis=-1).astype(v.dtype)
        o = jnp.einsum('bqgrk,bqkgd->bqgrd', p, v_sel)
        return o.reshape(B_, Q_BLOCK, ATT_Q_W)

    pos_blocks = jnp.arange(Tq, dtype=jnp.int32).reshape(nb, Q_BLOCK)
    out = lax.map(block, (to_blocks(q), to_blocks(qi), to_blocks(wi), pos_blocks))
    return jnp.moveaxis(out, 0, 1).reshape(B_, Tq, ATT_Q_W)[:, :T_]

def first_inputs(seed: int = 0) -> dict:
    key = jax.random.key(seed)
    ks = jax.random.split(key, 20)
    f32 = jnp.float32

    def nrm(k, shape, scale):
        return jax.random.normal(k, shape, f32) * scale

    def gain(k, shape):
        return 1.0 + 0.02 * jax.random.normal(k, shape, f32)

    dt = jnp.exp(jax.random.uniform(ks[5], (DEPTH, GDN_HEADS), f32, math.log(1e-3), math.log(1e-1)))
    return {
        "x": jax.random.normal(ks[0], (BATCH, SEQ, D_MODEL), f32),
        "meta_tokens": nrm(ks[1], (N_META, D_MODEL), 1.0),
        "pre_mix_norm": gain(ks[2], (DEPTH, D_MODEL)),
        "w_in": nrm(ks[3], (DEPTH, D_MODEL, N_IN), D_MODEL ** -0.5),
        "conv_w": nrm(ks[4], (DEPTH, CONV_WIDTH, 2 * GDN_QK_W + GDN_V_W), CONV_WIDTH ** -0.5),
        "a_log": jnp.log(jax.random.uniform(ks[6], (DEPTH, GDN_HEADS), f32, 1.0, 16.0)),
        "dt_bias": jnp.log(jnp.expm1(dt)),
        "gdn_norm": gain(ks[7], (DEPTH, GDN_DV)),
        "w_branch_gdn": nrm(ks[8], (DEPTH, GDN_V_W, D_MODEL), GDN_V_W ** -0.5),
        "w_branch_dsa": nrm(ks[9], (DEPTH, ATT_Q_W, D_MODEL), ATT_Q_W ** -0.5),
        "w_out": nrm(ks[10], (DEPTH, D_MODEL, D_MODEL), D_MODEL ** -0.5),
        "post_mix_norm": gain(ks[11], (DEPTH, D_MODEL)),
        "pre_mlp_norm": gain(ks[12], (DEPTH, D_MODEL)),
        "w_up": nrm(ks[13], (DEPTH, D_MODEL, D_FF), D_MODEL ** -0.5),
        "w_down": nrm(ks[14], (DEPTH, D_FF, D_MODEL), D_FF ** -0.5),
        "post_mlp_norm": gain(ks[15], (DEPTH, D_MODEL)),
    }

def first_block(x, meta_tokens, pre_mix_norm, w_in, conv_w, a_log, dt_bias, gdn_norm,
              w_branch_gdn, w_branch_dsa, w_out, post_mix_norm, pre_mlp_norm, w_up, w_down,
              post_mlp_norm):
    B_, L, _ = x.shape
    meta = jnp.broadcast_to(meta_tokens.astype(x.dtype)[None], (B_, N_META, D_MODEL))
    h = jnp.concatenate([meta, x], axis=1)
    T_ = h.shape[1]
    pos = jnp.arange(T_, dtype=jnp.int32)
    rope_att = _rope_tables(pos, ATT_HD)
    rope_idx = _rope_tables(pos, IDX_HD)
    split_at = [int(i) for i in np.cumsum(SPLITS)[:-1]]

    for l in range(DEPTH):
        n = _rmsnorm(h, pre_mix_norm[l])
        proj = jnp.einsum('btd,dn->btn', n, w_in[l])
        (gq, gk, gv, gz, gb, ga, aq, ak, av, iq, ik, iw, gate_a, gate_b) = jnp.split(proj, split_at, axis=-1)
        y_gdn = _gdn_branch(gq, gk, gv, gz, gb, ga, conv_w[l], a_log[l], dt_bias[l], gdn_norm[l])
        y_dsa = _dsa_branch(aq, ak, av, iq, ik, iw, rope_att, rope_idx, L)
        merged = (jax.nn.sigmoid(gate_a) * jnp.einsum('btv,vd->btd', y_gdn, w_branch_gdn[l])
                  + jax.nn.sigmoid(gate_b) * jnp.einsum('btv,vd->btd', y_dsa, w_branch_dsa[l]))
        mix = jnp.einsum('btd,de->bte', merged, w_out[l])
        h = h + _rmsnorm(mix, post_mix_norm[l])
        n2 = _rmsnorm(h, pre_mlp_norm[l])
        u = jnp.square(jax.nn.relu(jnp.einsum('btd,df->btf', n2, w_up[l])))
        h = h + _rmsnorm(jnp.einsum('btf,fd->btd', u, w_down[l]), post_mlp_norm[l])

    return h[:, N_META:]


GRID_W = 64
CTX_LEN = 256
N_HEADS = 8
HEAD_DIM = D_MODEL // 16
QK_W = N_HEADS * 2 * HEAD_DIM
V_W = N_HEADS * 2 * HEAD_DIM
ATTN_SCALE = HEAD_DIM ** -0.5
ROT_FREQS = HEAD_DIM // 4
ROPE_BASE = 10000.0
LAMBDA_STD = 0.1
F_GROUPS = 4
F_GROUP_DIM = D_MODEL // 8
F_W = F_GROUPS * F_GROUP_DIM
Q_OFF = 0
K_OFF = Q_OFF + QK_W
V_OFF = K_OFF + QK_W
F_OFF = V_OFF + V_W
GA_OFF = F_OFF + F_W
GF_OFF = GA_OFF + D_MODEL
PROJ_W = GF_OFF + D_MODEL
N_GROUPS = 4
EXPERTS_PER_GROUP = 4
N_EXPERTS = N_GROUPS * EXPERTS_PER_GROUP
TOP_K_IN_GROUP = 2
EXPERT_HIDDEN = D_MODEL // 2


def rmsnorm(x, g):
    x32 = x.astype(jnp.float32)
    y = x32 * lax.rsqrt(jnp.mean(x32 * x32, axis=-1, keepdims=True) + EPS)
    return (y * g.astype(jnp.float32)).astype(x.dtype)

def modulate(h, shift, scale):
    return h * (1 + scale) + shift

def axial_angles(rows):
    inv = 1.0 / (ROPE_BASE ** (jnp.arange(ROT_FREQS, dtype=jnp.float32) / ROT_FREQS))
    row = jnp.broadcast_to(jnp.arange(rows, dtype=jnp.float32)[:, None], (rows, GRID_W)).reshape(-1)
    col = jnp.broadcast_to(jnp.arange(GRID_W, dtype=jnp.float32)[None, :], (rows, GRID_W)).reshape(-1)
    return row[:, None] * inv[None, :], col[:, None] * inv[None, :]

def rotate(x, ang):
    cos = jnp.cos(ang)[:, None, None, :].astype(x.dtype)
    sin = jnp.sin(ang)[:, None, None, :].astype(x.dtype)
    x1, x2 = x[..., :ROT_FREQS], x[..., ROT_FREQS:]
    return jnp.concatenate([x1 * cos - x2 * sin, x2 * cos + x1 * sin], axis=-1)

def axial_rope(x, ang_row, ang_col):
    half = 2 * ROT_FREQS
    return jnp.concatenate([rotate(x[..., :half], ang_row), rotate(x[..., half:], ang_col)], axis=-1)

def split_proj(p):
    b, n = p.shape[:2]
    q = p[..., Q_OFF:K_OFF].reshape(b, n, N_HEADS, 2, HEAD_DIM)
    k = p[..., K_OFF:V_OFF].reshape(b, n, N_HEADS, 2, HEAD_DIM)
    v = p[..., V_OFF:F_OFF].reshape(b, n, N_HEADS, 2 * HEAD_DIM)
    f = p[..., F_OFF:GA_OFF]
    ga = p[..., GA_OFF:GF_OFF]
    gf = p[..., GF_OFF:PROJ_W]
    return q, k, v, f, ga, gf

def diff_attend(q, k, v, lam):
    s = jnp.einsum('bqhid,bkhid->bhiqk', q, k, preferred_element_type=jnp.float32) * ATTN_SCALE
    p = jax.nn.softmax(s, axis=-1)
    a = p[:, :, 0] - lam * p[:, :, 1]
    return jnp.einsum('bhqk,bkhe->bqhe', a.astype(v.dtype), v)

def blocked_latent_attention(q, k_all, v_all, lam):
    b, n = q.shape[:2]
    qb = q.reshape(b, n // Q_BLOCK, Q_BLOCK, N_HEADS, 2, HEAD_DIM).transpose(1, 0, 2, 3, 4, 5)
    out = lax.map(lambda qblk: diff_attend(qblk, k_all, v_all, lam), qb)
    return out.transpose(1, 0, 2, 3, 4).reshape(b, n, N_HEADS, 2 * HEAD_DIM)

def merge_branches(heads, f, ga, gf, subln_g, lam_init, w_ao, w_fo, w_o):
    b, n = heads.shape[:2]
    attn = (rmsnorm(heads, subln_g) * (1.0 - lam_init)).reshape(b, n, V_W)
    fg = f.reshape(b, n, F_GROUPS, F_GROUP_DIM).astype(jnp.float32)
    four = jnp.fft.fftn(fg, axes=(1, 3), norm='ortho').real.astype(f.dtype).reshape(b, n, F_W)
    y = jax.nn.sigmoid(ga) * (attn @ w_ao) + jax.nn.sigmoid(gf) * (four @ w_fo)
    return y @ w_o

def hier_moe(h, w_rg, b_rg, w_re, b_re, w1, w3, w2):
    b, n, d = h.shape
    t = h.reshape(-1, d)
    lg = (t @ w_rg + b_rg).astype(jnp.float32)
    g_sel = jnp.argmax(lg, axis=-1)
    w_grp = jnp.take_along_axis(jax.nn.softmax(lg, axis=-1), g_sel[:, None], axis=-1)
    le = (t @ w_re + b_re).astype(jnp.float32).reshape(-1, N_GROUPS, EXPERTS_PER_GROUP)
    le_g = jnp.take_along_axis(le, g_sel[:, None, None], axis=1)[:, 0]
    top_v, top_i = lax.top_k(le_g, TOP_K_IN_GROUP)
    w_top = jax.nn.softmax(top_v, axis=-1) * w_grp
    eid = g_sel[:, None] * EXPERTS_PER_GROUP + top_i
    gates = jnp.einsum('tk,tke->et', w_top, jax.nn.one_hot(eid, N_EXPERTS, dtype=jnp.float32)).astype(t.dtype)

    def expert_step(acc, xs):
        w1e, w3e, w2e, ge = xs
        y = (jax.nn.silu(t @ w1e) * (t @ w3e)) @ w2e
        return acc + ge[:, None] * y, None

    acc, _ = lax.scan(expert_step, jnp.zeros_like(t), (w1, w3, w2, gates))
    return acc.reshape(b, n, d)

def second_inputs(seed: int = 0) -> dict:
    key = jax.random.key(seed)
    ks = jax.random.split(key, 32)
    f32 = jnp.float32
    d = D_MODEL

    def nrm(k, shape, scale):
        return jax.random.normal(k, shape, f32) * scale

    return {
        'x': nrm(ks[0], (BATCH, SEQ, d), 1.0),
        'c': nrm(ks[1], (BATCH, d), 1.0),
        'ctx': nrm(ks[2], (BATCH, CTX_LEN, d), 1.0),
        'c_ctx': nrm(ks[3], (d,), 1.0),
        'w_mod': nrm(ks[4], (DEPTH, d, 6 * d), 0.5 * d ** -0.5),
        'b_mod': nrm(ks[5], (DEPTH, 6 * d), 0.02),
        'norm1_g': 1.0 + nrm(ks[6], (DEPTH, d), 0.02),
        'norm2_g': 1.0 + nrm(ks[7], (DEPTH, d), 0.02),
        'w_in': nrm(ks[8], (DEPTH, d, PROJ_W), d ** -0.5),
        'lam_q1': nrm(ks[9], (DEPTH, HEAD_DIM), LAMBDA_STD),
        'lam_k1': nrm(ks[10], (DEPTH, HEAD_DIM), LAMBDA_STD),
        'lam_q2': nrm(ks[11], (DEPTH, HEAD_DIM), LAMBDA_STD),
        'lam_k2': nrm(ks[12], (DEPTH, HEAD_DIM), LAMBDA_STD),
        'subln_g': 1.0 + nrm(ks[13], (DEPTH, 2 * HEAD_DIM), 0.02),
        'w_attn_out': nrm(ks[14], (DEPTH, V_W, d), V_W ** -0.5),
        'w_four_out': nrm(ks[15], (DEPTH, F_W, d), F_W ** -0.5),
        'w_out': nrm(ks[16], (DEPTH, d, d), d ** -0.5),
        'w_router_group': nrm(ks[17], (DEPTH, d, N_GROUPS), d ** -0.5),
        'b_router_group': nrm(ks[18], (DEPTH, N_GROUPS), 0.01),
        'w_router_expert': nrm(ks[19], (DEPTH, d, N_EXPERTS), d ** -0.5),
        'b_router_expert': nrm(ks[20], (DEPTH, N_EXPERTS), 0.01),
        'w_exp_gate': nrm(ks[21], (DEPTH, N_EXPERTS, d, EXPERT_HIDDEN), d ** -0.5),
        'w_exp_up': nrm(ks[22], (DEPTH, N_EXPERTS, d, EXPERT_HIDDEN), d ** -0.5),
        'w_exp_down': nrm(ks[23], (DEPTH, N_EXPERTS, EXPERT_HIDDEN, d), EXPERT_HIDDEN ** -0.5),
        'final_g': 1.0 + nrm(ks[24], (d,), 0.02),
    }

def second_block(x, c, ctx, c_ctx, w_mod, b_mod, norm1_g, norm2_g, w_in, lam_q1, lam_k1, lam_q2, lam_k2,
              subln_g, w_attn_out, w_four_out, w_out, w_router_group, b_router_group, w_router_expert,
              b_router_expert, w_exp_gate, w_exp_up, w_exp_down, final_g):
    n = x.shape[1]
    rows = n // GRID_W
    ang_row, ang_col = axial_angles(rows)
    x_lat, x_ctx = x, ctx
    for l in range(DEPTH):
        update_ctx = l < DEPTH - 1
        lam_init = 0.8 - 0.6 * math.exp(-0.3 * l)
        lam = (jnp.exp(jnp.sum(lam_q1[l].astype(jnp.float32) * lam_k1[l].astype(jnp.float32)))
               - jnp.exp(jnp.sum(lam_q2[l].astype(jnp.float32) * lam_k2[l].astype(jnp.float32)))
               + lam_init)
        sh1, sc1, g1, sh2, sc2, g2 = [m[:, None, :] for m in jnp.split(jax.nn.silu(c) @ w_mod[l] + b_mod[l], 6, axis=-1)]
        csh1, csc1, cg1, csh2, csc2, cg2 = jnp.split(jax.nn.silu(c_ctx) @ w_mod[l] + b_mod[l], 6, axis=-1)

        h_c = modulate(rmsnorm(x_ctx, norm1_g[l]), csh1, csc1)
        if update_ctx:
            q_c, k_c, v_c, f_c, ga_c, gf_c = split_proj(h_c @ w_in[l])
        else:
            kv_c = h_c @ w_in[l][:, K_OFF:F_OFF]
            k_c = kv_c[..., :QK_W].reshape(x_ctx.shape[0], x_ctx.shape[1], N_HEADS, 2, HEAD_DIM)
            v_c = kv_c[..., QK_W:].reshape(x_ctx.shape[0], x_ctx.shape[1], N_HEADS, 2 * HEAD_DIM)
        h_l = modulate(rmsnorm(x_lat, norm1_g[l]), sh1, sc1)
        q_l, k_l, v_l, f_l, ga_l, gf_l = split_proj(h_l @ w_in[l])
        q_l = axial_rope(q_l, ang_row, ang_col)
        k_l = axial_rope(k_l, ang_row, ang_col)
        k_all = jnp.concatenate([k_c, k_l], axis=1)
        v_all = jnp.concatenate([v_c, v_l], axis=1)
        heads_l = blocked_latent_attention(q_l, k_all, v_all, lam)
        mix_l = merge_branches(heads_l, f_l, ga_l, gf_l, subln_g[l], lam_init, w_attn_out[l], w_four_out[l], w_out[l])
        x_lat = x_lat + g1 * mix_l
        if update_ctx:
            heads_c = diff_attend(q_c, k_c, v_c, lam)
            mix_c = merge_branches(heads_c, f_c, ga_c, gf_c, subln_g[l], lam_init, w_attn_out[l], w_four_out[l], w_out[l])
            x_ctx = x_ctx + cg1 * mix_c

        h2_l = modulate(rmsnorm(x_lat, norm2_g[l]), sh2, sc2)
        x_lat = x_lat + g2 * hier_moe(h2_l, w_router_group[l], b_router_group[l], w_router_expert[l],
                                      b_router_expert[l], w_exp_gate[l], w_exp_up[l], w_exp_down[l])
        if update_ctx:
            h2_c = modulate(rmsnorm(x_ctx, norm2_g[l]), csh2, csc2)
            x_ctx = x_ctx + cg2 * hier_moe(h2_c, w_router_group[l], b_router_group[l], w_router_expert[l],
                                          b_router_expert[l], w_exp_gate[l], w_exp_up[l], w_exp_down[l])
    return rmsnorm(x_lat, final_g)


def setup_inputs(seed=0):
    out = dict(first_inputs(seed))
    for name, value in second_inputs(seed + 1).items():
        if name != "x":
            out[name + "_2"] = value
    return out


def reference(
    x, meta_tokens, pre_mix_norm, w_in, conv_w, a_log, dt_bias, gdn_norm, w_branch_gdn,
    w_branch_dsa, w_out, post_mix_norm, pre_mlp_norm, w_up, w_down, post_mlp_norm, c_2, ctx_2,
    c_ctx_2, w_mod_2, b_mod_2, norm1_g_2, norm2_g_2, w_in_2, lam_q1_2, lam_k1_2, lam_q2_2,
    lam_k2_2, subln_g_2, w_attn_out_2, w_four_out_2, w_out_2, w_router_group_2,
    b_router_group_2, w_router_expert_2, b_router_expert_2, w_exp_gate_2, w_exp_up_2,
    w_exp_down_2, final_g_2,
):
    x = first_block(
        x, meta_tokens, pre_mix_norm, w_in, conv_w, a_log, dt_bias, gdn_norm, w_branch_gdn,
        w_branch_dsa, w_out, post_mix_norm, pre_mlp_norm, w_up, w_down, post_mlp_norm,
    )
    return second_block(
        x, c_2, ctx_2, c_ctx_2, w_mod_2, b_mod_2, norm1_g_2, norm2_g_2, w_in_2, lam_q1_2,
        lam_k1_2, lam_q2_2, lam_k2_2, subln_g_2, w_attn_out_2, w_four_out_2, w_out_2,
        w_router_group_2, b_router_group_2, w_router_expert_2, b_router_expert_2, w_exp_gate_2,
        w_exp_up_2, w_exp_down_2, final_g_2,
    )


_drawn_inputs = setup_inputs


def setup_inputs(seed=0):
    import zlib

    import numpy as np

    out = dict(_drawn_inputs(seed))
    spreads = {}
    factors = {'gdn_norm': 3.819,
     'post_mix_norm': 3.606,
     'pre_mlp_norm': 4.044,
     'post_mlp_norm': 4.626,
     'ctx_2': 3.254,
     'b_mod_2': 4.923,
     'norm1_g_2': 8.0,
     'norm2_g_2': 8.0,
     'lam_q1_2': 64.0,
     'lam_k1_2': 8.0,
     'lam_q2_2': 8.0,
     'lam_k2_2': 7.838,
     'subln_g_2': 44.262,
     'b_router_group_2': 8.0,
     'b_router_expert_2': 25.706,
     'final_g_2': 23.389}
    for name, (base, spread) in spreads.items():
        noise = np.random.default_rng([zlib.crc32(name.encode()), seed]).standard_normal(out[name].shape)
        drawn = base * np.exp(spread * noise) if base else spread * noise
        out[name] = __import__('jax').numpy.asarray(drawn.astype(out[name].dtype))
    for name, factor in factors.items():
        out[name] = (out[name] * factor).astype(out[name].dtype)
    return out
```

```python
import math
from contextlib import ExitStack

import concourse.bass as bass
import numpy as np
from concourse import mybir

D = 1024
KT = D // 128
META = 16
SEQ = 256
T = META + SEQ
H = 8
CH = 128
NCH = SEQ // CH
NSYS = H * NCH
LEVELS = 7
META_LEVELS = 4
TOPK = SEQ // 4
KV_HEADS = 2
CTX = 256
DFF = 4096
FT = DFF // 128
EPS = 1e-6
N_EXP = 16
LAM_INIT = 0.8 - 0.6 * math.exp(-0.0)
EH = D // 2
EPG = 4
NGRP = 4
UNIT_COLS = 256
SLOTS = 6
NEG = -3.0e38
TAKEN = -3.3e38
MOD_TILES = 6 * D // 128
MOD_UNITS = MOD_TILES // 2

def _layout(widths):
    at, out = 0, {}
    for name, w in widths:
        out[name] = (at, w)
        at += w
    return out, at

C1, C1_W = _layout([("ident", 128), ("ones", 128), ("eps", 1), ("upper", 128), ("rot_att", 128), ("rot_idx", 128),
                    ("cos_att", T), ("sin_att", T), ("cos_idx", T), ("sin_idx", T),
                    ("meta_upper", 128), ("meta_last", 128), ("levels", LEVELS * 128),
                    ("causal", NCH * T), ("head_rows", H)])
C2, C2_W = _layout([("rot_ax", 128), ("cos_ax", SEQ), ("sin_ax", SEQ), ("dft_d", 256), ("dft_n", 4 * SEQ)])
SM, SM_W = _layout([("g_pre_mix", KT), ("g_post_mix", KT), ("g_pre_mlp", KT), ("g_post_mlp", KT),
                    ("g_n1", KT), ("g_n2", KT), ("g_final", KT), ("conv", 24 * 4), ("gdn_norm", 1),
                    ("subln", 1), ("b_mod", MOD_TILES), ("c", KT * 2), ("dt_bias", H), ("a_log", H),
                    ("b_router", 20)])
C2_AT = C1["upper"][0]
WS, WS_W = _layout([("gba", KT * 16), ("ik", KT * 128), ("iw", KT * 8)])

def weight_order():
    order = [("mod", u) for u in range(4)]
    order += [("gk", u) for u in range(4)] + [("gv", u) for u in range(4)] + [("gq", u) for u in range(4)]
    order += [("mod", u) for u in range(4, 16)]
    order += [("gz", u) for u in range(4)] + [("aq", u) for u in range(4)] + [("ak", 0), ("av", 0)]
    order += [("iq", u) for u in range(2)]
    for u in range(4):
        order += [("gate_a", u), ("bg", u)]
    for u in range(4):
        order += [("gate_b", u), ("bd", u)]
    order += [("wo", u) for u in range(4)]
    order += [("mod", u) for u in range(16, 20)]
    order += [("up", u) for u in range(16)]
    order += [("down", u) for u in range(16)]
    order += [("mod", u) for u in range(20, 24)]
    order += [("q2", u) for u in range(4)] + [("k2", u) for u in range(4)] + [("v2", u) for u in range(4)]
    order += [("f2", u) for u in range(2)]
    for u in range(4):
        order += [("gate2a", u), ("ao", u), ("gate2f", u)] + ([("fo", u // 2)] if u % 2 == 0 else [])
    order += [("wo2", u) for u in range(4)]
    order += [("e_up", u) for u in range(4)]
    for e in range(1, N_EXP):
        order += [("e_up", 4 * e + u) for u in range(4)] + [("e_down", 2 * (e - 1) + u) for u in range(2)]
    order += [("e_down", 2 * (N_EXP - 1) + u) for u in range(2)]
    return order

ORDER = weight_order()
FIRST_EXPERT = ORDER.index(("e_up", 0))
assert len(ORDER) % SLOTS == 0 and FIRST_EXPERT % SLOTS == 0


class Steps:

    def __init__(self, eng, sem):
        self.eng, self.sem, self.n = eng, sem, 0

    def __call__(self, ins):
        self.n += 1
        ins.then_inc(self.sem, 1)

    def settle(self):
        self.eng.wait_ge(self.sem, self.n)


class Banks:

    def __init__(self, full, free):
        self.full, self.free = full, free
        self.turn, self.filled, self.freed = 0, [0] * 8, [0] * 8
        self.at, self.full_when, self.free_when = {}, {}, {}

    def take(self, name, drains, bank=None):
        if bank is None:
            bank = self.turn % 8
            self.turn += 1
        before = self.freed[bank]
        self.freed[bank] += drains
        self.at[name] = bank
        self.free_when[name] = self.freed[bank]
        return bank, before

    def fill(self, name):
        bank = self.at[name]
        self.filled[bank] += 1
        self.full_when[name] = (self.full[bank], self.filled[bank])
        return self.full[bank]


def build(nc, stream, h_in, ctx_in, c1_in, c2_in, sm_in, ws_in, wr_in, lam_in, out):
    f32 = mybir.dt.float32
    ALU, ACT, AX = mybir.AluOpType, mybir.ActivationFunctionType, mybir.AxisListType.X
    mul, add, sub = ALU.mult, ALU.add, ALU.subtract
    top = ExitStack()
    with top:
        def sb(stack, name, *shape):
            return stack.enter_context(nc.sbuf_tensor(name, list(shape), f32))

        def sem(name):
            return top.enter_context(nc.semaphore(name))

        ring = sb(top, "ring", 128, SLOTS, KT * UNIT_COLS)
        c1 = sb(top, "c1", 128, C1_W)
        sm = sb(top, "sm", 128, SM_W)
        hT = sb(top, "hT", 128, KT, SEQ)
        modT = sb(top, "modT", 128, MOD_TILES, 2)
        silu_c = sb(top, "silu_c", 128, KT, 2)
        a1 = sb(top, "a1", 128, KT, 2)
        a2 = sb(top, "a2", 128, KT)
        rB = sb(top, "rB", 128, T)
        root = sb(top, "root", 128, T)
        lam = sb(top, "lam", 128, 8)
        wr = sb(top, "wr", 128, KT, 20)

        def cst(name, rows=128):
            a, w = C1[name]
            return c1[0:rows, a:a + w]

        def small(name):
            a, w = SM[name]
            return sm[:, a:a + w]

        ident, ones, upper, eps = cst("ident"), cst("ones"), cst("upper"), cst("eps")

        with ExitStack() as mixer:
            nT = sb(mixer, "nT", 128, KT, T)
            ws = sb(mixer, "ws", 128, WS_W)
            y_gdn = sb(mixer, "y_gdn", 128, H, SEQ)
            with ExitStack() as m:
                kc = sb(m, "kc", 128, H, T)
                vc = sb(m, "vc", 128, H, T)
                qc = sb(m, "qc", 128, H, T)
                v_beta = sb(m, "v_beta", 128, NSYS, 128)
                attn = sb(m, "attn", 128, NSYS, 128)
                k_tail = sb(m, "k_tail", 128, NSYS, 128)
                inv = sb(m, "inv", 128, NSYS, 128)
                invT = sb(m, "invT", 128, NSYS, 128)
                low = sb(m, "low", 128, NSYS, 128)
                masked = sb(m, "masked", 128, 2, 512)
                prod = sb(m, "prod", 128, 2, 512)
                state = sb(m, "state", 128, 2, H * 128)
                scr = sb(m, "scr", 128, 2, 1024)
                metas = sb(m, "metas", 128, 10, 128)
                mcol = sb(m, "mcol", 128, 4)
                egl = sb(m, "egl", 128, NSYS)
                tok = sb(m, "tok", 128, 8, 24)
            with ExitStack() as m:
                merged = sb(m, "merged", 128, KT, SEQ)
                gate = sb(m, "gate", 128, 2, 512)
                aq = sb(m, "aq", 128, H, SEQ)
                ak = sb(m, "ak", 128, KV_HEADS, T)
                av = sb(m, "av", 128, 3, KV_HEADS * 128)
                iq = sb(m, "iq", 128, 4, SEQ)
                ik = sb(m, "ik", 128, T)
                iw = sb(m, "iw", 128, NCH, H)
                rot1 = sb(m, "rot1", 128, 512)
                rot2 = sb(m, "rot2", 128, 512)
                relu = sb(m, "relu", 128, 2, T)
                score = sb(m, "score", 128, NCH, T)
                work = sb(m, "work", 128, 2, T)
                best = sb(m, "best", 128, 8)
                bias = sb(m, "bias", 128, NCH, T)
                lmask = sb(m, "lmask", 128, 2, T)
                prob = sb(m, "prob", 128, 2, T)
                probT = sb(m, "probT", 128, 2, 3 * 128)
                stat = sb(m, "stat", 128, 2, 4)
                y_dsa = sb(m, "y_dsa", 128, H, SEQ)
        with ExitStack() as rest:
            ctxT = sb(rest, "ctxT", 128, KT, CTX)
            with ExitStack() as m:
                _under = sb(m, "under_merged", 128, KT * T + WS_W + H * SEQ - KT * CTX)
                _merged = sb(m, "merged_still", 128, KT, SEQ)
                mix = sb(m, "mix", 128, KT, SEQ)
                sq = sb(m, "sq", 128, KT, SEQ)
                nM = sb(m, "nM", 128, KT, SEQ)
                up = sb(m, "up", 128, FT, SEQ)
            with ExitStack() as m:
                hcl = sb(m, "hcl", 128, KT, CTX + SEQ)
                q2 = sb(m, "q2", 128, H, SEQ)
                k2 = sb(m, "k2", 128, H, CTX + SEQ)
                v2 = sb(m, "v2", 128, 4, D)
                f2 = sb(m, "f2", 128, 4, SEQ)
                zdft = sb(m, "zdft", 128, 4, 2, 256)
                four = sb(m, "four", 128, 4, SEQ)
                sq1 = sb(m, "sq1", 128, KT, SEQ)
                heads = sb(m, "heads", 128, H, SEQ)
                esc = sb(m, "esc", 128, 2, 2, 512)
                aT = sb(m, "aT", 128, 2, 512)
                stat2 = sb(m, "stat2", 128, 2, 8)
                rot3 = sb(m, "rot3", 128, 2, 512)
                merged2 = sb(m, "merged2", 128, KT, SEQ)
                gate2 = sb(m, "gate2", 128, 2, 512)
            with ExitStack() as m:
                mix2 = sb(m, "mix2", 128, KT, SEQ)
                sq2 = sb(m, "sq2", 128, KT, SEQ)
                h2 = sb(m, "h2", 128, KT, SEQ)
                geB = sb(m, "geB", 128, N_EXP, SEQ)
                sel = sb(m, "sel", 16, N_EXP, 128)
                gT = sb(m, "gT", 16, SEQ)
                hid = sb(m, "hid", 128, 2, 4, SEQ)
                sg = sb(m, "sg", 128, 4, SEQ)
                rt = sb(m, "rt", 128, 24, 32)
        c2 = c1[:, C2_AT:C2_AT + C2_W]

        def cst2(name):
            a, w = C2[name]
            return c2[:, a:a + w]

        psum = [top.enter_context(nc.psum_tensor(f"bank{b}", [128, 512], f32)) for b in range(8)]
        banks = Banks([sem(f"bank_full{b}") for b in range(8)], [sem(f"bank_free{b}") for b in range(8)])

        unit_loaded = [sem(f"unit_loaded{s}") for s in range(SLOTS)]
        unit_used = [sem(f"unit_used{s}") for s in range(SLOTS)]
        h_loaded, c1_loaded, sm_loaded, ws_loaded = sem("h_loaded"), sem("c1_loaded"), sem("sm_loaded"), sem("ws_loaded")
        res_loaded, ctx_loaded, c2_loaded, lam_loaded, wr_loaded = (sem("res_loaded"), sem("ctx_loaded"), sem("c2_loaded"),
                                                        sem("lam_loaded"), sem("wr_loaded"))
        act_step, dve_step, out_stored = sem("act_step"), sem("dve_step"), sem("out_stored")

        block = top.enter_context(nc.Block())

        def full(eng, name):
            eng.wait_ge(*banks.full_when[name])
            return psum[banks.at[name]]

        def free(name):
            return banks.free[banks.at[name]]

        def emptied(eng, name, but=0):
            eng.wait_ge(banks.free[banks.at[name]], banks.free_when[name] - but)

        sq_ready = sem("sq_ready")
        silu_ready = sem("silu_ready")
        sig_ready = sem("sig_ready")
        nT_ready = sem("nT_ready")
        normed_ready = sem("normed_ready")
        absx_ready = sem("absx_ready")
        softplus_ready = sem("softplus_ready")
        tri_ready = sem("tri_ready")
        meta_arg_ready = sem("meta_arg_ready")
        meta_exp_ready = sem("meta_exp_ready")
        decay_arg_ready = sem("decay_arg_ready")
        decay_exp_ready = sem("decay_exp_ready")
        gated_step = sem("gated_step")
        masked_ready = sem("masked_ready")
        scan_ready = sem("scan_ready")
        y_ready = sem("y_ready")
        roped_ready = sem("roped_ready")
        score_ready = sem("score_ready")
        nmax_ready = sem("nmax_ready")
        pexp_ready = sem("pexp_ready")
        prob_ready = sem("prob_ready")
        merged_ready = sem("merged_ready")
        h1_ready = sem("h1_ready")
        nM_ready = sem("nM_ready")
        up_ready = sem("up_ready")
        lamp_ready = sem("lamp_ready")
        hcl_ready = sem("hcl_ready")
        roped2_ready = sem("roped2_ready")
        heads_ready = sem("heads_ready")
        merged2_ready = sem("merged2_ready")
        h2_ready = sem("h2_ready")
        sel_ready = sem("sel_ready")
        rexp_arg_ready = sem("rexp_arg_ready")
        rexp_ready = sem("rexp_ready")
        gates_ready = sem("gates_ready")
        w1_sig_ready = sem("w1_sig_ready")
        out_ready = sem("out_ready")
        up_full = [sem(f"up_full{b}") for b in (0, 2)]
        hid_ready = [sem(f"hid_ready{b}") for b in range(4)]

        BASE = FIRST_EXPERT // SLOTS
        LEVEL_ITEMS = [(l, g) for l in range(LEVELS) for g in (4, 0, 1, 2, 3) if g < 4 or l < META_LEVELS]

        CONV_TILES = [(kind, j) for kind in ("gk", "gv", "gq") for j in range(H)]

        def conv_dst(t):
            kind, j = CONV_TILES[t]
            return {"gk": kc, "gv": vc, "gq": qc}[kind][:, j, :]

        def raw_of(kind, j):
            if kind == "ik":
                return ik[:, :].unsqueeze(1), T
            if kind == "ak":
                return ak[:, j:j + 1, :], T
            return (aq if kind == "aq" else iq)[:, 2 * j:2 * j + 2, :], 512

        def rflat(a, n):
            return rt[:, :, :].rearrange("p a b -> p (a b)")[:, a:a + n]

        def systems(g):
            return [4 * g + s for s in range(4)] if g < 4 else [None]

        def sysview(t, meta_slot, s):
            return t[:, s, :] if s is not None else metas[:, meta_slot, :]

        def chunk(t, h, ci):
            a = META + ci * CH
            return t[:, h, a:a + CH]

        def nkeys(qt):
            return META + (qt + 1) * 128

        def key_tiles(qt):
            n = nkeys(qt)
            return [(a, min(128, n - a)) for a in range(0, n, 128)]

        ATT = [(qt, h) for qt in range(2) for h in range(H)]
        ROPES = [("aq", j) for j in range(4)] + [("ak", j) for j in range(2)] + [("iq", j) for j in range(2)] + [("ik", 0)]

        @block.tensor
        def _(pe):
            at = [0]

            def unit(kind, u):
                assert ORDER[at[0]] == (kind, u), (ORDER[at[0]], kind, u)
                s, n = at[0] % SLOTS, at[0] // SLOTS + 1
                at[0] += 1
                pe.wait_ge(unit_loaded[s], 16 * n)
                return s, n

            def by_k(s, cols=UNIT_COLS):
                return ring[:, s, :].rearrange("p (k n) -> p k n", n=cols)

            def take(name, drains=1, bank=None):
                b, before = banks.take(name, drains, bank)
                if before:
                    pe.wait_ge(banks.free[b], before)
                return psum[b]

            def done(name, ins):
                ins.then_inc(banks.fill(name), 1)

            def group(dst, pairs):
                for i, (lhs, rhs) in enumerate(pairs):
                    last = nc.tensor.matmul(dst, lhs, rhs, start=(i == 0), stop=(i == len(pairs) - 1))
                return last

            def tiles_of_unit(kind, u, rhs, n, names, kt=KT, drains=1):
                s, cnt = unit(kind, u)
                w = by_k(s)
                if len(names) == 2:
                    for j in range(2):
                        dst = take(names[j], drains)
                        last = group(dst[:, 0:n], [(w[:, k, j * 128:(j + 1) * 128], rhs[:, k, :]) for k in range(kt)])
                        if j == 0:
                            done(names[0], last)
                else:
                    dst = take(names[0], drains)
                    for j in range(2):
                        last = group(dst[:, j * n:(j + 1) * n], [(w[:, k, j * 128:(j + 1) * 128], rhs[:, k, :]) for k in range(kt)])
                last.then_inc(unit_used[s], 1)
                banks.full_when[names[-1]] = (unit_used[s], cnt)

            def mod_unit(u):
                tiles_of_unit("mod", u, silu_c, 2, [("mod", u)])

            def feature_sum(name, src, n, drains=1):
                dst = take(name, drains)
                done(name, group(dst[:, 0:n], [(ones, src[:, k, :]) for k in range(KT)]))

            pe.wait_ge(c1_loaded, 16)
            pe.wait_ge(sq_ready, 1)
            feature_sum("ss_in", vc[:, :, :], T)
            pe.wait_ge(silu_ready, 1)
            for u in range(4):
                mod_unit(u)

            pe.wait_ge(nT_ready, 1)
            pe.wait_ge(ws_loaded, 16)
            gba = ws[:, 0:KT * 16].rearrange("p (k n) -> p k n", n=16)
            dst = take("gba", 2)
            for g, a in enumerate((0, META, META + CH)):
                last = group(dst[:, g * 16:(g + 1) * 16], [(nT[:, k, a:a + 128], gba[:, k, :]) for k in range(KT)])
            done("gba", last)

            for kind in ("gk", "gv", "gq"):
                for u in range(4):
                    tiles_of_unit(kind, u, nT, T, [(kind, 2 * u), (kind, 2 * u + 1)])

            for i in range(12):
                n = T if i < 8 else 512
                pe.wait_ge(sq_ready, 2 + i)
                dst = take(("l2", i), 1)
                done(("l2", i), nc.tensor.matmul(dst[:, 0:n], ones, scr[:, i % 2, 0:n], start=True, stop=True))
                if i % 4 == 3:
                    mod_unit(4 + i // 4)

            pe.wait_ge(tri_ready, 1)
            dst = take("gct", 2)
            for ci in range(NCH):
                last = nc.tensor.matmul(dst[:, ci * 8:(ci + 1) * 8], upper, tok[:, 3, (1 + ci) * 8:(2 + ci) * 8], start=True, stop=True)
            done("gct", last)
            dst = take("metaGB", 1)
            nc.tensor.matmul(dst[:, 0:128], ones[0:META, :], metas[0:META, 0, :], start=True, stop=True)
            done("metaGB", nc.tensor.matmul(dst[:, 128:256], ones[0:META, :], metas[0:META, 1, :], start=True, stop=True))
            dst = take("metaK", 1)
            nc.tensor.matmul(dst[:, 0:128], metas[:, 2, :], metas[:, 2, :], start=True, stop=True)
            nc.tensor.transpose(dst[:, 128:256], metas[:, 2, :], ident)
            done("metaK", nc.tensor.transpose(dst[:, 256:384], metas[:, 3, :], ident))

            for h in range(H):
                dst = take(("GB", h), 2)
                for ci in range(NCH):
                    sy = h * NCH + ci
                    nc.tensor.matmul(dst[:, ci * 128:(ci + 1) * 128], inv[:, sy, :], upper, start=True, stop=True)
                    last = nc.tensor.matmul(dst[:, 256 + ci * 128:384 + ci * 128], invT[:, sy, :], ident, start=True, stop=True)
                done(("GB", h), last)
                dst = take(("KQ", h), 1)
                for ci in range(NCH):
                    k_c, q_c = chunk(kc, h, ci), chunk(qc, h, ci)
                    nc.tensor.matmul(dst[:, ci * 128:(ci + 1) * 128], k_c, k_c, start=True, stop=True)
                    last = nc.tensor.matmul(dst[:, 256 + ci * 128:384 + ci * 128], k_c, q_c, start=True, stop=True)
                done(("KQ", h), last)
                dst = take(("TR", h), 1)
                for ci in range(NCH):
                    nc.tensor.transpose(dst[:, ci * 128:(ci + 1) * 128], chunk(kc, h, ci), ident)
                    last = nc.tensor.transpose(dst[:, 256 + ci * 128:384 + ci * 128], chunk(vc, h, ci), ident)
                done(("TR", h), last)

            def level_p(n):
                l, g = LEVEL_ITEMS[n]
                pe.wait_ge(masked_ready, n + 1)
                if l > 0:
                    emptied(pe, ("QT", LEVEL_ITEMS.index((l - 1, g))))
                dst = take(("P", n))
                for j, s in enumerate(systems(g)):
                    rhs = ident if l == 0 else sysview(inv, 8, s)
                    last = nc.tensor.matmul(dst[:, j * 128:(j + 1) * 128], masked[:, n % 2, j * 128:(j + 1) * 128], rhs, start=True, stop=True)
                done(("P", n), last)

            def level_q(n):
                l, g = LEVEL_ITEMS[n]
                emptied(pe, ("P", n))
                end = META_LEVELS - 1 if g == 4 else LEVELS - 1
                if 0 < l < end:
                    dst = take(("Q", n), 1)
                    for j, s in enumerate(systems(g)):
                        last = nc.tensor.matmul(dst[:, j * 128:(j + 1) * 128], sysview(invT, 9, s), prod[:, n % 2, j * 128:(j + 1) * 128], start=True, stop=True)
                    done(("Q", n), last)
                dst = take(("QT", n), 1)
                for j, s in enumerate(systems(g)):
                    rhs = ident if l == 0 else sysview(invT, 9, s)
                    last = nc.tensor.matmul(dst[:, j * 128:(j + 1) * 128], prod[:, n % 2, j * 128:(j + 1) * 128], rhs, start=True, stop=True)
                done(("QT", n), last)

            for n in range(len(LEVEL_ITEMS)):
                level_p(n)
                if n >= 1:
                    level_q(n - 1)
                if n % 4 == 3 and 7 + n // 4 < 16:
                    mod_unit(7 + n // 4)
            level_q(len(LEVEL_ITEMS) - 1)
            mod_unit(15)
            assert ORDER[at[0]] == ("gz", 0), ORDER[at[0]]

            pe.wait_ge(scan_ready, 1)
            dst = take("meta_v", 1)
            emptied(pe, ("QT", LEVEL_ITEMS.index((META_LEVELS - 1, 4))))
            done("meta_v", nc.tensor.matmul(dst[:, 0:128], metas[:, 9, :], metas[:, 7, :], start=True, stop=True))
            emptied(pe, "meta_v")
            for hg in range(2):
                dst = take(("S0", hg), 1)
                for j in range(4):
                    h = hg * 4 + j
                    last = nc.tensor.matmul(dst[:, j * 128:(j + 1) * 128], scr[:, 0, h * 128:(h + 1) * 128], metas[:, 3, :], start=True, stop=True)
                done(("S0", hg), last)
            emptied(pe, ("QT", len(LEVEL_ITEMS) - 1))
            for ci in range(NCH):
                for hg in range(2):
                    emptied(pe, ("S0", hg) if ci == 0 else ("dS", ci - 1, hg))
                    dst = take(("kS", ci, hg), 1)
                    for j in range(4):
                        h = hg * 4 + j
                        last = nc.tensor.matmul(dst[:, j * 128:(j + 1) * 128], chunk(kc, h, ci), state[:, ci, h * 128:(h + 1) * 128], start=True, stop=True)
                    done(("kS", ci, hg), last)
                for hg in range(2):
                    emptied(pe, ("kS", ci, hg))
                    dst = take(("vn", ci, hg), 1)
                    for j in range(4):
                        sy = (hg * 4 + j) * NCH + ci
                        last = nc.tensor.matmul(dst[:, j * 128:(j + 1) * 128], invT[:, sy, :], scr[:, hg, j * 128:(j + 1) * 128], start=True, stop=True)
                    done(("vn", ci, hg), last)
                for hg in range(2):
                    emptied(pe, ("vn", ci, hg))
                    if ci + 1 < NCH:
                        dst = take(("dS", ci, hg), 1)
                        for j in range(4):
                            sy = (hg * 4 + j) * NCH + ci
                            last = nc.tensor.matmul(dst[:, j * 128:(j + 1) * 128], k_tail[:, sy, :], scr[:, hg, 512 + j * 128:640 + j * 128], start=True, stop=True)
                        done(("dS", ci, hg), last)
                    dst = take(("o", ci, hg), 1)
                    for j in range(4):
                        h = hg * 4 + j
                        last = group(dst[:, j * 128:(j + 1) * 128],
                                     [(state[:, ci, h * 128:(h + 1) * 128], chunk(qc, h, ci)),
                                      (scr[:, hg, 512 + j * 128:640 + j * 128], attn[:, h * NCH + ci, :])])
                    done(("o", ci, hg), last)
            for u in range(4):
                tiles_of_unit("gz", u, nT[:, :, META:T], SEQ, [("gz", u)])
            pe.wait_ge(sq_ready, 14)
            for j in range(4):
                dst = take(("yss", j), 1)
                done(("yss", j), nc.tensor.matmul(dst[:, :], ones, low[:, 4 * j:4 * j + 4, :], start=True, stop=True))

            def rope(i):
                kind, j = ROPES[i]
                emptied(pe, "ik" if kind == "ik" else ROPES[i])
                dst = take(("rot", i), 1)
                src, n = raw_of(kind, j)
                r = "rot_att" if kind in ("aq", "ak") else "rot_idx"
                done(("rot", i), nc.tensor.matmul(dst[:, 0:n], cst(r), src, start=True, stop=True))

            real = nT[:, :, META:T]
            for u in range(4):
                tiles_of_unit("aq", u, real, SEQ, [("aq", u)])
                if u:
                    rope(u - 1)
            tiles_of_unit("ak", 0, nT, T, [("ak", 0), ("ak", 1)])
            rope(3)
            s, cnt = unit("av", 0)
            for g, (a, m) in enumerate(((0, 128), (128, 128), (256, META))):
                dst = take(("av", g), 1)
                last = group(dst[0:m, 0:256], [(nT[:, k, a:a + m], by_k(s)[:, k, :]) for k in range(KT)])
                if g < 2:
                    done(("av", g), last)
            last.then_inc(unit_used[s], 1)
            banks.full_when[("av", 2)] = (unit_used[s], cnt)
            rope(4)
            rope(5)
            tiles_of_unit("iq", 0, real, SEQ, [("iq", 0)])
            tiles_of_unit("iq", 1, real, SEQ, [("iq", 1)])
            rope(6)
            wik = ws[:, WS["ik"][0]:WS["ik"][0] + KT * 128].rearrange("p (k n) -> p k n", n=128)
            wiw = ws[:, WS["iw"][0]:WS["iw"][0] + KT * 8].rearrange("p (k n) -> p k n", n=8)
            dst = take("ik")
            done("ik", group(dst[:, 0:T], [(wik[:, k, :], nT[:, k, :]) for k in range(KT)]))
            dst = take("iw")
            for qt in range(2):
                a = META + qt * 128
                last = group(dst[:, qt * 8:(qt + 1) * 8], [(nT[:, k, a:a + 128], wiw[:, k, :]) for k in range(KT)])
            done("iw", last)
            rope(7)
            rope(8)

            pe.wait_ge(roped_ready, 9)
            for qt, h in ATT:
                a = 64 * (h % 2)
                dst = take(("ix", qt, h))
                done(("ix", qt, h), nc.tensor.matmul(dst[:, 0:nkeys(qt)], iq[a:a + 64, h // 2, qt * 128:(qt + 1) * 128],
                                                     ik[a:a + 64, 0:nkeys(qt)], start=True, stop=True))
            pe.wait_ge(y_ready, 1)
            for u in range(4):
                tiles_of_unit("gate_a", u, real, SEQ, [("gate_a", u)])
                tiles_of_unit("bg", u, y_gdn, SEQ, [("bg", u)])

            def att_logits(n):
                qt, h = ATT[n]
                dst = take(("lg", n))
                done(("lg", n), nc.tensor.matmul(dst[:, 0:nkeys(qt)], aq[:, h, qt * 128:(qt + 1) * 128],
                                                 ak[:, h // 4, 0:nkeys(qt)], start=True, stop=True))

            def att_transpose(n):
                qt, h = ATT[n]
                pe.wait_ge(prob_ready, n + 1)
                dst = take(("pt", n), 1)
                for i, (a, m) in enumerate(key_tiles(qt)):
                    last = nc.tensor.transpose(dst[0:m, i * 128:(i + 1) * 128], prob[:, n % 2, a:a + m], ident)
                done(("pt", n), last)

            def att_values(n):
                qt, h = ATT[n]
                emptied(pe, ("pt", n))
                dst = take(("ao", n), 1)
                g = h // 4
                done(("ao", n), group(dst[:, 0:128], [(av[0:m, i, g * 128:(g + 1) * 128], probT[0:m, n % 2, i * 128:(i + 1) * 128])
                                                      for i, (a, m) in enumerate(key_tiles(qt))]))

            for n in range(len(ATT) + 2):
                if n < len(ATT):
                    att_logits(n)
                if 1 <= n <= len(ATT):
                    att_transpose(n - 1)
                if n >= 2:
                    att_values(n - 2)
            for u in range(4):
                tiles_of_unit("gate_b", u, real, SEQ, [("gate_b", u)])
                if u == 0:
                    emptied(pe, ("ao", len(ATT) - 1))
                tiles_of_unit("bd", u, y_dsa, SEQ, [("bd", u)])
            pe.wait_ge(merged_ready, 4)
            for u in range(4):
                tiles_of_unit("wo", u, merged, SEQ, [("wo", u)])
            for u in range(16, 20):
                mod_unit(u)
            pe.wait_ge(sq_ready, 15)
            feature_sum("ss_mix", sq, SEQ)
            pe.wait_ge(sq_ready, 16)
            feature_sum("ss_h1", sq, SEQ)
            pe.wait_ge(nM_ready, 1)
            for u in range(16):
                tiles_of_unit("up", u, nM, SEQ, [("up", u)])
            pe.wait_ge(sq_ready, 17)
            feature_sum("ss_ctx", sq, CTX)
            pe.wait_ge(up_ready, 16)
            for cp in range(4):
                dst = take(("down", cp))
                for kg in range(4):
                    s, cnt = unit("down", cp * 4 + kg)
                    for j in range(2):
                        for k in range(KT):
                            last = nc.tensor.matmul(dst[:, j * SEQ:(j + 1) * SEQ], by_k(s)[:, k, j * 128:(j + 1) * 128],
                                                    up[:, kg * KT + k, :], start=(kg == 0 and j == 0 and k == 0),
                                                    stop=(kg == 3 and k == KT - 1), skip_group_check=True)
                    last.then_inc(unit_used[s], 1)
                banks.full_when[("down", cp)] = (unit_used[s], cnt)
            for u in range(20, 24):
                mod_unit(u)
            pe.wait_ge(lamp_ready, 1)
            dst = take("lam")
            done("lam", nc.tensor.matmul(dst[:, 0:2], ones[0:64, :], lam[0:64, 4:6], start=True, stop=True))
            pe.wait_ge(sq_ready, 18)
            feature_sum("ss_mlp", sq, SEQ)

            pe.wait_ge(sq_ready, 19)
            feature_sum("ss_x", sq1, SEQ)
            pe.wait_ge(hcl_ready, 1)
            lat = hcl[:, :, CTX:CTX + SEQ]
            for u in range(4):
                tiles_of_unit("q2", u, lat, SEQ, [("q2", u)])

            def rope2(i):
                emptied(pe, ("q2", i) if i < 4 else ("k2", 2 * (i - 4) + 1))
                src = q2[:, 2 * i:2 * i + 2, :] if i < 4 else k2[:, 2 * (i - 4):2 * (i - 4) + 2, CTX:CTX + SEQ]
                dst = take(("rot2", i))
                done(("rot2", i), nc.tensor.matmul(dst[:, :], cst2("rot_ax"), src, start=True, stop=True))

            pe.wait_ge(c2_loaded, 16)
            for u in range(4):
                tiles_of_unit("k2", u, hcl, 512, [("k2", 2 * u), ("k2", 2 * u + 1)])
                rope2(u)
            for u in range(4):
                s, cnt = unit("v2", u)
                for tp in range(2):
                    dst = take(("v2", u, tp))
                    for j in range(2):
                        a = (2 * tp + j) * 128
                        last = group(dst[:, j * 256:(j + 1) * 256], [(hcl[:, k, a:a + 128], by_k(s)[:, k, :]) for k in range(KT)])
                    if tp == 0:
                        done(("v2", u, 0), last)
                last.then_inc(unit_used[s], 1)
                banks.full_when[("v2", u, 1)] = (unit_used[s], cnt)
                rope2(4 + u)
            for u in range(2):
                tiles_of_unit("f2", u, lat, SEQ, [("f2", u)])

            def scores2(n):
                qt, h = ATT[n]
                for i in range(2):
                    dst = take(("s2", n, i), 2)
                    done(("s2", n, i), nc.tensor.matmul(dst[:, :], q2[64 * i:64 * i + 64, h, qt * 128:(qt + 1) * 128],
                                                        k2[64 * i:64 * i + 64, h, :], start=True, stop=True))

            def transpose2(n):
                pe.wait_ge(prob_ready, len(ATT) + n + 1)
                dst = take(("at2", n))
                for i in range(4):
                    last = nc.tensor.transpose(dst[:, i * 128:(i + 1) * 128], esc[:, n % 2, 0, i * 128:(i + 1) * 128], ident)
                done(("at2", n), last)

            def values2(n):
                qt, h = ATT[n]
                emptied(pe, ("at2", n))
                dst = take(("o2", n))
                done(("o2", n), group(dst[:, 0:128], [(v2[:, i, h * 128:(h + 1) * 128], aT[:, n % 2, i * 128:(i + 1) * 128]) for i in range(4)]))

            dft_d, dft_n = cst2("dft_d"), cst2("dft_n")

            def dft_features(g):
                emptied(pe, ("f2", g // 2))
                dst = take(("z", g))
                for nt in range(2):
                    last = nc.tensor.matmul(dst[:, nt * 256:(nt + 1) * 256], f2[:, g, nt * 128:(nt + 1) * 128], dft_d, start=True, stop=True)
                done(("z", g), last)

            def dft_tokens(g):
                emptied(pe, ("z", g))
                dst = take(("four", g))
                done(("four", g), group(dst[:, 0:SEQ], [(zdft[:, g, nt, p * 128:(p + 1) * 128], dft_n[:, (2 * nt + p) * SEQ:(2 * nt + p + 1) * SEQ])
                                                        for nt in range(2) for p in range(2)]))

            pe.wait_ge(roped2_ready, 8)
            for n in range(len(ATT) + 2):
                if n < len(ATT):
                    scores2(n)
                if 2 <= n < 6:
                    dft_features(n - 2)
                if 4 <= n < 8:
                    dft_tokens(n - 4)
                if 1 <= n <= len(ATT):
                    transpose2(n - 1)
                if n >= 2:
                    values2(n - 2)
            pe.wait_ge(sq_ready, 20)
            for j in range(4):
                dst = take(("hss", j))
                done(("hss", j), nc.tensor.matmul(dst[:, :], ones, sq1[:, 2 * j:2 * j + 2, :], start=True, stop=True))
            def four_out(u):
                s = four_slot[0]
                w = by_k(s[0], 512)
                dst = take(("fo", u))
                for j in range(2):
                    a = (u % 2) * 256 + j * 128
                    last = group(dst[:, j * SEQ:(j + 1) * SEQ], [(w[:, k, a:a + 128], four[:, k, :]) for k in range(4)])
                if u % 2:
                    last.then_inc(unit_used[s[0]], 1)
                    banks.full_when[("fo", u)] = (unit_used[s[0]], s[1])
                else:
                    done(("fo", u), last)

            four_slot = [None]
            for u in range(4):
                tiles_of_unit("gate2a", u, lat, SEQ, [("gate2a", u)])
                if u == 0:
                    pe.wait_ge(heads_ready, 1)
                    emptied(pe, ("four", 3))
                tiles_of_unit("ao", u, heads, SEQ, [("ao2", u)])
                tiles_of_unit("gate2f", u, lat, SEQ, [("gate2f", u)])
                if u % 2 == 0:
                    four_slot[0] = unit("fo", u // 2)
                four_out(u)
            pe.wait_ge(merged2_ready, 4)
            for u in range(4):
                tiles_of_unit("wo2", u, merged2, SEQ, [("wo2", u)])
            pe.wait_ge(sq_ready, 21)
            feature_sum("ss_x1", sq2, SEQ)
            pe.wait_ge(h2_ready, 1)
            pe.wait_ge(wr_loaded, 16)
            dst = take("router")
            for qt in range(2):
                last = group(dst[:, qt * 20:(qt + 1) * 20], [(h2[:, k, qt * 128:(qt + 1) * 128], wr[:, k, :]) for k in range(KT)])
            done("router", last)
            pe.wait_ge(gates_ready, 1)
            dst = take("gT")
            for qt in range(2):
                last = nc.tensor.transpose(dst[0:16, qt * 128:(qt + 1) * 128], rt[:, 18 + qt, 0:16], ident)
            done("gT", last)
            emptied(pe, "gT")
            pe.wait_ge(sel_ready, 1)
            for e2 in range(N_EXP // 2):
                dst = take(("ge", e2))
                for j in range(2):
                    last = nc.tensor.matmul(dst[:, j * SEQ:(j + 1) * SEQ], sel[:, 2 * e2 + j, :], gT[:, :], start=True, stop=True)
                done(("ge", e2), last)

            for b in range(8):
                pe.wait_ge(banks.free[b], banks.freed[b])
            pe.wait_ge(sel_ready, 2)
            acc = psum[4:8]
            for b in range(4):
                nc.tensor.matmul(acc[b][:, :], hid[:, 1, 0, 0:128], hid[:, 1, 0:2, :], start=True, stop=False, skip_group_check=True)

            def expert_up(slots, loaded, e):
                for q in range(4):
                    s, half = slots[q], q % 2
                    pe.wait_ge(unit_loaded[s], loaded[q])
                    for j in range(2):
                        b = (q // 2) * 2 + j
                        if half == 0 and not (isinstance(e, int) and e == 0):
                            pe.wait_ge(hid_ready[b], e)
                        last = group(psum[b][:, half * SEQ:(half + 1) * SEQ],
                                     [(by_k(s)[:, k, j * 128:(j + 1) * 128], h2[:, k, :]) for k in range(KT)])
                        if half == 1 and j == 0:
                            last.then_inc(up_full[b // 2], 1)
                    last.then_inc(unit_used[s], 1)

            def expert_down(slots, loaded, e, parity, last_one=False):
                pe.wait_ge(hid_ready[3], e + 1)
                for q in range(2):
                    s = slots[q]
                    pe.wait_ge(unit_loaded[s], loaded)
                    for j in range(4):
                        ft = q * 4 + j
                        for k in range(4):
                            last = nc.tensor.matmul(acc[ft // 2][:, (ft % 2) * SEQ:(ft % 2 + 1) * SEQ],
                                                    by_k(s, 512)[:, k, j * 128:(j + 1) * 128], hid[:, parity, k, :],
                                                    start=False, stop=(last_one and k == 3), skip_group_check=True)
                    last.then_inc(unit_used[s], 1)

            assert at[0] == FIRST_EXPERT
            expert_up((0, 1, 2, 3), [16 * (BASE + 1)] * 4, 0)

            def pair(e, parity):
                n = 16 * (e + BASE)
                expert_up((4, 5, 0, 1), [n, n, n + 16, n + 16], e)
                expert_down((2, 3), n + 16, e - 1, parity)

            with pe.Fori(1, N_EXP - 1, 2) as e:
                pair(e, 0)
                pair(e + 1, 1)
            pair(N_EXP - 1, 0)
            expert_down((4, 5), 16 * (N_EXP + BASE), N_EXP - 1, 1, True)
            pe.wait_ge(sq_ready, 22)
            pe.wait_ge(hid_ready[0], N_EXP)
            dst = take("ss_out", bank=0)
            done("ss_out", group(dst[:, 0:SEQ], [(ones, sq2[:, k, :]) for k in range(KT)]))

        @block.sync
        def _(sp):
            sp.dma_start(qc[:, :, :], h_in).then_inc(h_loaded, 16)
            sp.dma_start(sm[:, :], sm_in).then_inc(sm_loaded, 16)
            sp.dma_start(c1[:, :], c1_in).then_inc(c1_loaded, 16)
            for s in range(SLOTS):
                sp.dma_start(ring[:, s, :], stream[s]).then_inc(unit_loaded[s], 16)
            with sp.Fori(1, len(ORDER) // SLOTS) as i:
                for s in range(SLOTS):
                    sp.wait_ge(unit_used[s], i)
                    sp.dma_start(ring[:, s, :], stream[i * SLOTS + s]).then_inc(unit_loaded[s], 16)
            sp.wait_ge(out_ready, 1)
            sp.dma_start(out, mix2[:, :, :]).then_inc(out_stored, 16)
            sp.wait_ge(out_stored, 16)

        @block.gpsimd
        def _(pool):
            pool.dma_start(ws[:, :], ws_in).then_inc(ws_loaded, 16)
            pool.dma_start(hT[:, :, :], h_in[:, :, META:T]).then_inc(res_loaded, 16)
            pool.dma_start(wr[:, :, :], wr_in).then_inc(wr_loaded, 16)
            pool.dma_start(lam[0:64, 0:4], lam_in).then_inc(lam_loaded, 16)
            pool.wait_ge(merged_ready, 4)
            pool.dma_start(ctxT[:, :, :], ctx_in).then_inc(ctx_loaded, 16)
            pool.dma_start(c2[:, :], c2_in).then_inc(c2_loaded, 16)

        @block.scalar
        def _(act):
            step = Steps(act, act_step)
            A = nc.scalar.activation

            def evac(name, dst, width, scale=1.0):
                src = full(act, name)[0:dst.shape[0], 0:width]
                if len(dst.shape) == 3:
                    src = src.rearrange("p (a b) -> p a b", b=dst.shape[2])
                A(dst, src, ACT.Copy, scale=scale).then_inc(free(name), 1)

            def evac_mod(u):
                evac(("mod", u), modT[:, 2 * u:2 * u + 2, :], 4)

            def rms_root(name, n, dst, width=D):
                A(dst, full(act, name)[:, 0:n], ACT.Sqrt, bias=eps, scale=1.0 / width).then_inc(free(name), 1)

            act.wait_ge(sm_loaded, 16)
            A(a1[:, :, :], small("c").rearrange("p (k n) -> p k n", n=2), ACT.Sigmoid).then_inc(sig_ready, 1)
            act.wait_ge(h_loaded, 16)
            A(vc[:, :, :], qc[:, :, :], ACT.Square).then_inc(sq_ready, 1)
            act.wait_ge(c1_loaded, 16)
            rms_root("ss_in", T, root[:, :])
            for u in range(4):
                evac_mod(u)
            bank = full(act, "gba")
            A(tok[:, 0, :].rearrange("p (g n) -> p g n", n=8), bank[:, 0:48].rearrange("p (g n) -> p g n", n=16)[:, :, 0:8],
              ACT.Sigmoid).then_inc(free("gba"), 1)
            for t in range(24):
                kind, j = CONV_TILES[t]
                emptied(act, (kind, j))
                if t >= 2:
                    act.wait_ge(silu_ready, t)
                A(scr[:, t % 2, 0:T], conv_dst(t), ACT.Sigmoid).then_inc(sig_ready, 1)
            act.wait_ge(silu_ready, 25)
            for i in range(13):
                if i < 12:
                    n = T if i < 8 else 512
                    src = kc[:, i, :] if i < 8 else qc[:, 2 * (i - 8):2 * (i - 8) + 2, META:T]
                    dst = scr[:, i % 2, 0:n]
                    if i >= 2:
                        act.wait_ge(*banks.full_when[("l2", i - 2)])
                    A(dst if i < 8 else dst.rearrange("p (a b) -> p a b", b=SEQ), src, ACT.Square).then_inc(sq_ready, 1)
                if i >= 1:
                    j = i - 1
                    n = T if j < 8 else 512
                    if j >= 2:
                        act.wait_ge(normed_ready, j - 1)
                    A(scr[:, j % 2, 512:512 + n], full(act, ("l2", j))[:, 0:n], ACT.Sqrt, bias=eps).then_inc(free(("l2", j)), 1)
                    if j % 4 == 3:
                        evac_mod(4 + j // 4)
            act.wait_ge(absx_ready, 1)
            step(A(tok[:, 2, :], tok[:, 2, :], ACT.Exp, scale=-1.0))
            step(A(tok[:, 7, 0:8], small("a_log"), ACT.Exp))
            step.settle()
            A(tok[:, 2, :], tok[:, 2, :], ACT.Ln, bias=1.0).then_inc(softplus_ready, 1)
            A(tok[:, 5, 0:16], full(act, "gct")[:, 0:16], ACT.Exp).then_inc(free("gct"), 1)
            act.wait_ge(meta_arg_ready, 1)
            A(metas[:, 4, :], metas[:, 4, :], ACT.Exp).then_inc(meta_exp_ready, 1)
            for h in range(H + 1):
                if h < H:
                    act.wait_ge(decay_arg_ready, h + 1)
                    A(scr[:, h % 2, 256:512], full(act, ("GB", h))[:, 0:256], ACT.Exp).then_inc(free(("GB", h)), 1)
                    A(scr[:, h % 2, 0:256], scr[:, h % 2, 0:256], ACT.Exp).then_inc(decay_exp_ready, 1)
                if h >= 1:
                    g = h - 1
                    emptied(act, ("KQ", g))
                    bank = full(act, ("TR", g))
                    for ci in range(NCH):
                        sy = g * NCH + ci
                        step(A(k_tail[:, sy, :], bank[:, ci * 128:(ci + 1) * 128], ACT.Copy, scale=scr[:, g % 2, ci * 128 + 127:ci * 128 + 128]))
                        ins = A(v_beta[:, sy, :], bank[:, 256 + ci * 128:384 + ci * 128], ACT.Copy, scale=tok[:, 0, 8 + 8 * ci + g:9 + 8 * ci + g])
                        if ci == NCH - 1:
                            ins.then_inc(free(("TR", g)), 1)
            for n, (l, g) in enumerate(LEVEL_ITEMS):
                w = 512 if g < 4 else 128
                if n >= 2:
                    act.wait_ge(*banks.full_when[("QT", n - 2)])
                evac(("P", n), prod[:, n % 2, 0:w], w)
                if n % 4 == 3:
                    evac_mod(7 + n // 4)
            evac_mod(15)
            evac("meta_v", metas[:, 3, :], 128)
            for hg in range(2):
                evac(("S0", hg), state[:, 0, hg * 512:(hg + 1) * 512], 512)
            for ci in range(NCH):
                for hg in range(2):
                    evac(("vn", ci, hg), scr[:, hg, 512:1024], 512)
                for hg in range(2):
                    evac(("o", ci, hg), y_gdn[:, hg * 4:hg * 4 + 4, ci * 128:(ci + 1) * 128], 512)
            for u in range(4):
                A(inv[:, 4 * u:4 * u + 4, :], full(act, ("gz", u))[:, :].rearrange("p (a b) -> p a b", b=128), ACT.Sigmoid).then_inc(sig_ready, 1)
                act.wait_ge(sig_ready, 26 + u)
                A(k_tail[:, 4 * u:4 * u + 4, :], full(act, ("gz", u))[:, :].rearrange("p (a b) -> p a b", b=128), ACT.Copy).then_inc(free(("gz", u)), 1)
            emptied(act, ("o", NCH - 1, 1))
            A(low[:, :, :], y_gdn[:, :, :].rearrange("p h (c s) -> p (h c) s", s=128), ACT.Square).then_inc(sq_ready, 1)
            for j in range(4):
                rms_root(("yss", j), 512, attn[:, 4 * j:4 * j + 4, :].rearrange("p a b -> p (a b)"), 128)
            act.wait_ge(y_ready, 1)
            for u in range(4):
                evac(("aq", u), aq[:, 2 * u:2 * u + 2, :], 512)
            for j in range(2):
                evac(("ak", j), ak[:, j, :], T)
            for g, m in enumerate((128, 128, META)):
                evac(("av", g), av[0:m, g, :], 256)
            for u in range(2):
                evac(("iq", u), iq[:, 2 * u:2 * u + 2, :], 512)
            evac("ik", ik[:, :], T)
            evac("iw", iw[:, :, :], 16, float(H * 64) ** -0.5)
            for n, (qt, h) in enumerate(ATT):
                if n >= 2:
                    act.wait_ge(score_ready, n - 1)
                A(relu[:, n % 2, 0:nkeys(qt)], full(act, ("ix", qt, h))[:, 0:nkeys(qt)], ACT.Relu).then_inc(free(("ix", qt, h)), 1)
            for u in range(4):
                if u >= 2:
                    emptied(act, ("bg", u - 2))
                A(gate[:, u % 2, :], full(act, ("gate_a", u))[:, :], ACT.Sigmoid).then_inc(free(("gate_a", u)), 1)
            for n in range(len(ATT) + 2):
                if n < len(ATT):
                    qt, h = ATT[n]
                    act.wait_ge(nmax_ready, n + 1)
                    if n >= 2:
                        act.wait_ge(*banks.full_when[("pt", n - 2)])
                    A(prob[:, n % 2, 0:nkeys(qt)], lmask[:, n % 2, 0:nkeys(qt)], ACT.Exp, bias=stat[:, n % 2, 0:1],
                      accum_out=stat[:, n % 2, 1:2]).then_inc(pexp_ready, 1)
                if 1 <= n <= len(ATT):
                    k = n - 1
                    qt, h = ATT[k]
                    bank = full(act, ("pt", k))
                    if k >= 2:
                        act.wait_ge(*banks.full_when[("ao", k - 2)])
                    nt = len(key_tiles(qt)) - 1
                    step(A(probT[:, k % 2, 0:nt * 128], bank[:, 0:nt * 128], ACT.Copy))
                    A(probT[0:META, k % 2, nt * 128:(nt + 1) * 128], bank[0:META, nt * 128:(nt + 1) * 128], ACT.Copy).then_inc(free(("pt", k)), 1)
                if n >= 2:
                    qt, h = ATT[n - 2]
                    evac(("ao", n - 2), y_dsa[:, h, qt * 128:(qt + 1) * 128], 128)
            for u in range(4):
                if u >= 2:
                    emptied(act, ("bd", u - 2))
                A(gate[:, u % 2, :], full(act, ("gate_b", u))[:, :], ACT.Sigmoid).then_inc(free(("gate_b", u)), 1)
            for u in range(4):
                bank = full(act, ("wo", u))[:, :].rearrange("p (a b) -> p a b", b=SEQ)
                ins = A(sq[:, 2 * u:2 * u + 2, :], bank, ACT.Square)
                if u == 3:
                    ins.then_inc(sq_ready, 1)
                evac(("wo", u), mix[:, 2 * u:2 * u + 2, :], 512)
            for u in range(16, 20):
                evac_mod(u)
            rms_root("ss_mix", SEQ, root[:, 0:SEQ])
            act.wait_ge(h1_ready, 1)
            A(sq[:, :, :], hT[:, :, :], ACT.Square).then_inc(sq_ready, 1)
            rms_root("ss_h1", SEQ, root[:, 0:SEQ])
            for u in range(16):
                A(up[:, 2 * u:2 * u + 2, :], full(act, ("up", u))[:, :].rearrange("p (a b) -> p a b", b=SEQ), ACT.Relu).then_inc(free(("up", u)), 1)
            act.wait_ge(ctx_loaded, 16)
            act.wait_ge(nM_ready, 1)
            A(sq[:, :, :], ctxT[:, :, :], ACT.Square).then_inc(sq_ready, 1)
            rms_root("ss_ctx", CTX, root[:, 0:CTX])
            for cp in range(4):
                bank = full(act, ("down", cp))[:, :].rearrange("p (a b) -> p a b", b=SEQ)
                ins = A(sq[:, 2 * cp:2 * cp + 2, :], bank, ACT.Square)
                if cp == 3:
                    ins.then_inc(sq_ready, 1)
                evac(("down", cp), mix[:, 2 * cp:2 * cp + 2, :], 512)
            for u in range(20, 24):
                evac_mod(u)
            A(lam[:, 6:8], full(act, "lam")[:, 0:2], ACT.Exp).then_inc(free("lam"), 1)
            act.wait_ge(h1_ready, 2)
            rms_root("ss_mlp", SEQ, root[:, 0:SEQ])

            act.wait_ge(h1_ready, 3)
            A(sq1[:, :, :], hT[:, :, :], ACT.Square).then_inc(sq_ready, 1)
            rms_root("ss_x", SEQ, root[:, 0:SEQ])
            for u in range(4):
                evac(("q2", u), q2[:, 2 * u:2 * u + 2, :], 512)
            for u in range(4):
                evac(("k2", 2 * u), k2[:, 2 * u, :], 512)
                evac(("k2", 2 * u + 1), k2[:, 2 * u + 1, :], 512)
            for u in range(4):
                for tp in range(2):
                    evac(("v2", u, tp), v2[:, 2 * tp:2 * tp + 2, u * 256:(u + 1) * 256], 512)
            for u in range(2):
                evac(("f2", u), f2[:, 2 * u:2 * u + 2, :], 512)
            for n in range(len(ATT) + 2):
                if n < len(ATT):
                    act.wait_ge(nmax_ready, len(ATT) + n + 1)
                    if n >= 2:
                        act.wait_ge(*banks.full_when[("at2", n - 2)])
                    for i in range(2):
                        A(esc[:, n % 2, i, :], full(act, ("s2", n, i))[:, :], ACT.Exp, bias=stat2[:, n % 2, 2 + i:3 + i], scale=0.125,
                          accum_out=stat2[:, n % 2, 4 + i:5 + i]).then_inc(free(("s2", n, i)), 1)
                if 2 <= n < 6:
                    evac(("z", n - 2), zdft[:, n - 2, :, :], 512)
                if 4 <= n < 8:
                    evac(("four", n - 4), four[:, n - 4, :], SEQ)
                if 1 <= n <= len(ATT):
                    k = n - 1
                    if k >= 2:
                        act.wait_ge(*banks.full_when[("o2", k - 2)])
                    evac(("at2", k), aT[:, k % 2, :], 512)
                if n >= 2:
                    qt, h = ATT[n - 2]
                    evac(("o2", n - 2), heads[:, h, qt * 128:(qt + 1) * 128], 128)
            emptied(act, ("o2", len(ATT) - 1))
            A(sq1[:, :, :], heads[:, :, :], ACT.Square).then_inc(sq_ready, 1)
            for j in range(4):
                rms_root(("hss", j), 512, q2[:, 2 * j:2 * j + 2, :].rearrange("p a b -> p (a b)"), 128)
            for u in range(4):
                if u >= 1:
                    act.wait_ge(merged2_ready, u)
                A(gate2[:, 0, :], full(act, ("gate2a", u))[:, :], ACT.Sigmoid).then_inc(free(("gate2a", u)), 1)
                A(gate2[:, 1, :], full(act, ("gate2f", u))[:, :], ACT.Sigmoid).then_inc(free(("gate2f", u)), 1)
            emptied(act, ("wo2", 3))
            A(sq2[:, :, :], hT[:, :, :], ACT.Square).then_inc(sq_ready, 1)
            rms_root("ss_x1", SEQ, root[:, 0:SEQ])
            act.wait_ge(rexp_arg_ready, 1)
            A(rflat(80, 8), rflat(80, 8), ACT.Exp).then_inc(rexp_ready, 1)
            act.wait_ge(rexp_arg_ready, 2)
            A(rflat(180, 2), rflat(180, 2), ACT.Exp).then_inc(rexp_ready, 1)
            evac("gT", gT[:, :], SEQ)
            for e2 in range(N_EXP // 2):
                evac(("ge", e2), geB[:, 2 * e2:2 * e2 + 2, :], 512)

            def expert(e, first=False):
                for b in range(4):
                    if b % 2 == 0:
                        act.wait_ge(up_full[b // 2], e + 1)
                    elif first:
                        act.wait_ge(unit_used[b], BASE + 1)
                    else:
                        act.wait_ge(unit_used[5 if b == 1 else 1], e + BASE + (b == 3))
                    if not first:
                        act.wait_ge(hid_ready[b], e)
                    A(sg[:, b, :], psum[b][:, 0:SEQ], ACT.Sigmoid).then_inc(w1_sig_ready, 1)

            expert(0, True)
            with act.Fori(1, N_EXP) as e:
                expert(e)
            act.wait_ge(h1_ready, 4)
            A(sq2[:, :, :], hT[:, :, :], ACT.Square).then_inc(sq_ready, 1)
            rms_root("ss_out", SEQ, root[:, 0:SEQ])

        @block.vector
        def _(dve):
            step = Steps(dve, dve_step)
            TT, TS, STT, CP = nc.vector.tensor_tensor, nc.vector.tensor_scalar, nc.vector.scalar_tensor_tensor, nc.vector.tensor_copy

            def split(ap, b):
                return ap.rearrange("p (a b) -> p a b", b=b)

            def over(ap, n):
                return ap.unsqueeze(1).to_broadcast([ap.shape[0], n, ap.shape[1]])

            def each(ap, n):
                return ap.unsqueeze(2).to_broadcast([ap.shape[0], ap.shape[1], n])

            def inv_rms(name, n):
                emptied(dve, name)
                step(nc.vector.reciprocal(rB[:, 0:n], root[:, 0:n]))
                step.settle()

            def scaled(dst, src, gains, n, last_sem=None):
                for k in range(KT):
                    ins = STT(dst[:, k, :], src[:, k, :], gains[:, k:k + 1], rB[:, 0:n], mul, mul)
                    if k == KT - 1 and last_sem is not None:
                        ins.then_inc(last_sem, 1)
                    else:
                        step(ins)

            dve.wait_ge(sm_loaded, 16)
            dve.wait_ge(sig_ready, 1)
            TT(silu_c[:, :, :], small("c").rearrange("p (k n) -> p k n", n=2), a1[:, :, :], mul).then_inc(silu_ready, 1)
            inv_rms("ss_in", T)
            scaled(nT, qc, small("g_pre_mix"), T, nT_ready)
            emptied(dve, "gba", 1)
            bank = psum[banks.at["gba"]]
            TT(tok[:, 1, :].rearrange("p (g n) -> p g n", n=8), bank[:, 0:48].rearrange("p (g n) -> p g n", n=16)[:, :, 8:16],
               over(small("dt_bias"), 3), add).then_inc(free("gba"), 1)
            emptied(dve, "gba")
            step(TS(tok[:, 3, :], tok[:, 1, :], -1.0, None, mul))
            step.settle()
            TT(tok[:, 2, :], tok[:, 1, :], tok[:, 3, :], ALU.max).then_inc(absx_ready, 1)

            def silu(t):
                dve.wait_ge(sig_ready, t + 2)
                TT(conv_dst(t), conv_dst(t), scr[:, t % 2, 0:T], mul).then_inc(silu_ready, 1)

            for t in range(24):
                kind, j = CONV_TILES[t]
                bank = full(dve, (kind, j))
                dst = conv_dst(t)
                a = SM["conv"][0] + 4 * ({"gq": 0, "gk": 8, "gv": 16}[kind] + j)
                step(TS(dst, bank[:, 0:T], sm[:, a + 3:a + 4], None, mul))
                for back in (1, 2, 3):
                    step.settle()
                    ins = STT(dst[:, back:T], bank[:, 0:T - back], sm[:, a + 3 - back:a + 4 - back], dst[:, back:T], mul, add)
                    if back < 3:
                        step(ins)
                    else:
                        ins.then_inc(free((kind, j)), 1)
                if t >= 1:
                    silu(t - 1)
            silu(23)
            for i in range(12):
                n = T if i < 8 else 512
                emptied(dve, ("l2", i))
                r = scr[:, i % 2, 512:512 + n]
                step(nc.vector.reciprocal(r, r))
                step.settle()
                if i < 8:
                    TT(kc[:, i, :], kc[:, i, :], r, mul).then_inc(normed_ready, 1)
                else:
                    q = qc[:, 2 * (i - 8):2 * (i - 8) + 2, META:T]
                    STT(q, q, 128.0 ** -0.5, split(r, SEQ), mul, mul).then_inc(normed_ready, 1)
            dve.wait_ge(softplus_ready, 1)
            step(STT(tok[:, 4, :], tok[:, 1, :], 0.0, tok[:, 2, :], ALU.max, add))
            step.settle()
            step(STT(split(tok[:, 3, :], 8), split(tok[:, 4, :], 8), -1.0, over(tok[:, 7, 0:8], 3), mul, mul))
            step.settle()
            dve.wait_ge(normed_ready, 12)
            for ci in range(NCH):
                a = 8 * (1 + ci)
                step(CP(inv[:, :, :].rearrange("p (h c) m -> p c h m", c=NCH)[:, ci], each(tok[:, 3, a:a + 8], 128)))
                step(CP(invT[:, :, :].rearrange("p (h c) m -> p c h m", c=NCH)[:, ci], each(tok[:, 0, a:a + 8], 128)))
            step(TT(split(metas[0:META, 0, :], META), each(tok[0:META, 3, 0:8], META), over(upper[0:META, 0:META], 8), mul))
            step(TT(split(metas[0:META, 1, :], META), each(tok[0:META, 0, 0:8], META), over(ident[0:META, 0:META], 8), mul))
            step(CP(split(metas[:, 2, :], META), kc[:, :, 0:META]))
            CP(split(metas[:, 3, :], META), vc[:, :, 0:META]).then_inc(tri_ready, 1)
            emptied(dve, "gct", 1)
            TS(tok[:, 6, 0:16], psum[banks.at["gct"]][:, 0:16], -1.0, None, mul).then_inc(free("gct"), 1)
            emptied(dve, "gct")
            step(STT(tok[:, 7, 8:24], tok[:, 5, 0:16], -1.0, tok[:, 0, 8:24], mul, mul))
            bank = full(dve, "metaGB")
            step(STT(metas[:, 5, :], bank[:, 0:128], 1.0, ident, mul, mul, accum_out=mcol[:, 0:1]))
            step(STT(metas[:, 6, :], bank[:, 128:256], 1.0, ident, mul, mul, accum_out=mcol[:, 1:2]))
            step.settle()
            TS(metas[:, 4, :], bank[:, 0:128], mcol[:, 0:1], 0.0, sub, ALU.min).then_inc(meta_arg_ready, 1)
            dve.wait_ge(meta_exp_ready, 1)
            step(TT(metas[:, 4, :], metas[:, 4, :], cst("meta_upper"), mul))
            step.settle()
            kbank = full(dve, "metaK")
            step(STT(metas[:, 6, :], metas[:, 4, :], 1.0, cst("meta_last"), mul, mul, accum_out=mcol[:, 2:3]))
            step(TT(metas[:, 5, :], kbank[:, 0:128], metas[:, 4, :], mul))
            step.settle()
            TT(metas[:, 5, :], metas[:, 5, :], bank[:, 128:256], mul).then_inc(free("metaGB"), 1)
            step(TS(metas[:, 6, :], kbank[:, 128:256], mcol[:, 2:3], None, mul))
            TS(metas[:, 7, :], kbank[:, 256:384], mcol[:, 1:2], None, mul).then_inc(free("metaK"), 1)

            def decay_args(h):
                if h >= 2:
                    emptied(dve, ("TR", h - 2))
                bank = full(dve, ("GB", h))
                for ci in range(NCH):
                    ins = TS(scr[:, h % 2, ci * 128:(ci + 1) * 128], bank[:, ci * 128:(ci + 1) * 128],
                             tok[:, 6, 8 * ci + h:8 * ci + h + 1], 0.0, add, ALU.min)
                    if ci == NCH - 1:
                        ins.then_inc(decay_arg_ready, 1)
                    else:
                        step(ins)

            def decay_use(h):
                dve.wait_ge(decay_exp_ready, h + 1)
                dt = scr[:, h % 2, 0:256]
                step(TT(split(dt, 128), split(dt, 128), over(upper, 2), mul))
                step(CP(egl[:, 2 * h:2 * h + 2], split(scr[:, h % 2, 256:512], 128)[:, :, 127]))
                step.settle()
                bank = full(dve, ("KQ", h))
                step(TT(attn[:, 2 * h:2 * h + 2, :], split(bank[:, 256:512], 128), split(dt, 128), mul))
                TT(low[:, 2 * h:2 * h + 2, :], split(bank[:, 0:256], 128), split(dt, 128), mul).then_inc(free(("KQ", h)), 1)
                step(TT(qc[:, h, META:T], qc[:, h, META:T], scr[:, h % 2, 256:512], mul))
                emptied(dve, ("KQ", h))
                TT(low[:, 2 * h:2 * h + 2, :], low[:, 2 * h:2 * h + 2, :], split(full(dve, ("GB", h))[:, 256:512], 128), mul).then_inc(free(("GB", h)), 1)

            for h in range(H + 1):
                if h < H:
                    decay_args(h)
                if h >= 1:
                    decay_use(h - 1)
            emptied(dve, ("TR", H - 1))
            TT(split(scr[:, 0, :], 128), over(metas[:, 6, :], H), each(cst("head_rows"), 128), mul).then_inc(scan_ready, 1)

            def mask_level(n):
                l, g = LEVEL_ITEMS[n]
                if n >= 2:
                    dve.wait_ge(*banks.full_when[("P", n - 2)])
                a, _w = C1["levels"]
                m = c1[:, a + 128 * l:a + 128 * (l + 1)]
                if g == 4:
                    TT(masked[:, n % 2, 0:128], metas[:, 5, :], m, mul).then_inc(masked_ready, 1)
                else:
                    TT(split(masked[:, n % 2, :], 128), low[:, 4 * g:4 * g + 4, :], over(m, 4), mul).then_inc(masked_ready, 1)

            def update_inverse(n):
                l, g = LEVEL_ITEMS[n]
                x = metas[:, 8:9, :] if g == 4 else inv[:, 4 * g:4 * g + 4, :]
                xt = metas[:, 9:10, :] if g == 4 else invT[:, 4 * g:4 * g + 4, :]
                w = 1 if g == 4 else 4
                if l == 0:
                    emptied(dve, ("P", n))
                    step(TT(x, over(ident, w), split(prod[:, n % 2, 0:w * 128], 128), sub))
                    TT(xt, over(ident, w), split(full(dve, ("QT", n))[:, 0:w * 128], 128), sub).then_inc(free(("QT", n)), 1)
                    return
                if ("Q", n) in banks.at:
                    TT(x, x, split(full(dve, ("Q", n))[:, 0:w * 128], 128), sub).then_inc(free(("Q", n)), 1)
                TT(xt, xt, split(full(dve, ("QT", n))[:, 0:w * 128], 128), sub).then_inc(free(("QT", n)), 1)

            emptied(dve, ("GB", H - 1))
            mask_level(0)
            for n in range(len(LEVEL_ITEMS)):
                if n + 1 < len(LEVEL_ITEMS):
                    mask_level(n + 1)
                update_inverse(n)
            for ci in range(NCH):
                for hg in range(2):
                    bank = full(dve, ("kS", ci, hg))
                    for j in range(4):
                        h = hg * 4 + j
                        ins = STT(scr[:, hg, j * 128:(j + 1) * 128], bank[:, j * 128:(j + 1) * 128], tok[:, 7, 8 + 8 * ci + h:9 + 8 * ci + h],
                                  v_beta[:, h * NCH + ci, :], mul, add)
                        if j == 3:
                            ins.then_inc(free(("kS", ci, hg)), 1)
                if ci + 1 < NCH:
                    for hg in range(2):
                        bank = full(dve, ("dS", ci, hg))
                        for j in range(4):
                            h = hg * 4 + j
                            sy = h * NCH + ci
                            ins = STT(state[:, ci + 1, h * 128:(h + 1) * 128], state[:, ci, h * 128:(h + 1) * 128], egl[:, sy:sy + 1],
                                      bank[:, j * 128:(j + 1) * 128], mul, add)
                            if j == 3:
                                ins.then_inc(free(("dS", ci, hg)), 1)
            for u in range(4):
                emptied(dve, ("gz", u))
                step(TT(inv[:, 4 * u:4 * u + 4, :], inv[:, 4 * u:4 * u + 4, :], k_tail[:, 4 * u:4 * u + 4, :], mul))
            for j in range(4):
                emptied(dve, ("yss", j))
                r = attn[:, 4 * j:4 * j + 4, :].rearrange("p a b -> p (a b)")
                yj = y_gdn[:, 2 * j:2 * j + 2, :].rearrange("p a b -> p (a b)")
                step(nc.vector.reciprocal(r, r))
                step.settle()
                step(STT(yj, yj, small("gdn_norm"), r, mul, mul))
                step.settle()
                ins = TT(yj, yj, inv[:, 4 * j:4 * j + 4, :].rearrange("p a b -> p (a b)"), mul)
                if j == 3:
                    ins.then_inc(y_ready, 1)
                else:
                    step(ins)
            for i, (kind, j) in enumerate(ROPES):
                bank = full(dve, ("rot", i))
                raw, _n = raw_of(kind, j)
                w, n = (2, SEQ) if kind in ("aq", "iq") else (1, T)
                tab = "att" if kind in ("aq", "ak") else "idx"
                if i:
                    dve.wait_ge(roped_ready, i)
                cos, sin = cst("cos_" + tab)[:, T - n:T], cst("sin_" + tab)[:, T - n:T]
                TT(split(rot1[:, 0:w * n], n), split(bank[:, 0:w * n], n), over(sin, w), mul).then_inc(free(("rot", i)), 1)
                step(TT(split(rot2[:, 0:w * n], n), raw, over(cos, w), mul))
                step.settle()
                emptied(dve, ("rot", i))
                TT(raw, split(rot1[:, 0:w * n], n), split(rot2[:, 0:w * n], n), add).then_inc(roped_ready, 1)
            emptied(dve, "iw")
            for n, (qt, h) in enumerate(ATT):
                emptied(dve, ("ix", qt, h))
                sc = score[:, qt, 0:nkeys(qt)]
                if h == 0:
                    TS(sc, relu[:, n % 2, 0:nkeys(qt)], iw[:, qt, h:h + 1], None, mul).then_inc(score_ready, 1)
                else:
                    dve.wait_ge(score_ready, n)
                    STT(sc, relu[:, n % 2, 0:nkeys(qt)], iw[:, qt, h:h + 1], sc, mul, add).then_inc(score_ready, 1)
            dve.wait_ge(score_ready, len(ATT))

            def choose(qt):
                n = nkeys(qt)
                causal = cst("causal")[:, qt * T:qt * T + n]
                step(TT(work[:, 0, 0:n], score[:, qt, 0:n], causal, add))
                for i in range(TOPK // 8):
                    step.settle()
                    step(nc.vector.max(best[:, :], work[:, i % 2, 0:n]))
                    step.settle()
                    step(nc.vector.match_replace(work[:, (i + 1) % 2, 0:n], best[:, :], work[:, i % 2, 0:n], TAKEN))
                step(TS(lmask[:, 0, 0:n], causal, 0.0, None, ALU.is_equal))
                step.settle()
                step(STT(lmask[:, 1, 0:n], work[:, (TOPK // 8) % 2, 0:n], (NEG + TAKEN) / 2, lmask[:, 0, 0:n], ALU.is_le, mul))
                step.settle()
                step(TS(bias[:, qt, 0:n], lmask[:, 1, 0:n], 1.0, 1.0e30, sub, mul))

            def merge_a(u):
                emptied(dve, ("gate_a", u))
                TT(merged[:, 2 * u:2 * u + 2, :], split(gate[:, u % 2, :], SEQ), split(full(dve, ("bg", u))[:, :], SEQ), mul).then_inc(free(("bg", u)), 1)

            choose(0)
            merge_a(0)
            merge_a(1)
            choose(1)
            merge_a(2)
            merge_a(3)
            step.settle()
            for n in range(len(ATT) + 1):
                if n < len(ATT):
                    qt, h = ATT[n]
                    w = nkeys(qt)
                    if n >= 2:
                        dve.wait_ge(pexp_ready, n - 1)
                    STT(lmask[:, n % 2, 0:w], full(dve, ("lg", n))[:, 0:w], 128.0 ** -0.5, bias[:, qt, 0:w], mul, add).then_inc(free(("lg", n)), 1)
                    emptied(dve, ("lg", n))
                    nc.vector.tensor_reduce(stat[:, n % 2, 0:1], lmask[:, n % 2, 0:w], AX, ALU.max, negate=True).then_inc(nmax_ready, 1)
                if n >= 1:
                    k = n - 1
                    w = nkeys(ATT[k][0])
                    dve.wait_ge(pexp_ready, k + 1)
                    step(nc.vector.reciprocal(stat[:, k % 2, 2:3], stat[:, k % 2, 1:2]))
                    step.settle()
                    TS(prob[:, k % 2, 0:w], prob[:, k % 2, 0:w], stat[:, k % 2, 2:3], None, mul).then_inc(prob_ready, 1)
            for u in range(4):
                emptied(dve, ("gate_b", u))
                gated = (rot1, rot2)[u % 2]
                TT(gated[:, :], gate[:, u % 2, :], full(dve, ("bd", u))[:, :], mul).then_inc(free(("bd", u)), 1)
                emptied(dve, ("bd", u))
                TT(merged[:, 2 * u:2 * u + 2, :], merged[:, 2 * u:2 * u + 2, :], split(gated[:, :], SEQ), add).then_inc(merged_ready, 1)
            dve.wait_ge(res_loaded, 16)
            inv_rms("ss_mix", SEQ)
            scaled(mix, mix, small("g_post_mix"), SEQ)
            step.settle()
            TT(hT[:, :, :], hT[:, :, :], mix[:, :, :], add).then_inc(h1_ready, 1)
            inv_rms("ss_h1", SEQ)
            dve.wait_ge(h1_ready, 1)
            scaled(nM, hT, small("g_pre_mlp"), SEQ, nM_ready)
            dve.wait_ge(lam_loaded, 16)
            step(TT(lam[0:64, 4:5], lam[0:64, 0:1], lam[0:64, 1:2], mul))
            TT(lam[0:64, 5:6], lam[0:64, 2:3], lam[0:64, 3:4], mul).then_inc(lamp_ready, 1)
            for u in range(16):
                emptied(dve, ("up", u))
                v = up[:, 2 * u:2 * u + 2, :]
                TT(v, v, v, mul).then_inc(up_ready, 1)
            inv_rms("ss_ctx", CTX)
            dve.wait_ge(ctx_loaded, 16)
            TT(ctxT[:, :, :], ctxT[:, :, :], over(rB[:, 0:CTX], KT), mul).then_inc(h1_ready, 1)
            inv_rms("ss_mlp", SEQ)
            emptied(dve, ("down", 3))
            scaled(mix, mix, small("g_post_mlp"), SEQ)
            step.settle()
            TT(hT[:, :, :], hT[:, :, :], mix[:, :, :], add).then_inc(h1_ready, 1)

            emptied(dve, ("mod", MOD_UNITS - 1))
            step(TT(modT[:, :, :], modT[:, :, :], each(small("b_mod"), 2), add))
            emptied(dve, "lam")
            step(TT(lam[:, 4:5], lam[:, 7:8], lam[:, 6:7], sub))
            step(TS(small("subln"), small("subln"), 1.0 - LAM_INIT, None, mul))
            step.settle()
            step(TS(lam[:, 5:6], lam[:, 4:5], -LAM_INIT, None, add))
            step(STT(a1[:, :, :], modT[:, 8:16, :], 1.0, each(small("g_n1"), 2), add, mul))
            step(STT(a2[:, :], modT[:, 32:40, 0], 1.0, small("g_n2"), add, mul))
            step.settle()
            for k in range(KT):
                step(TS(hcl[:, k, 0:CTX], ctxT[:, k, :], a1[:, k, 1:2], modT[:, k, 1:2], mul, add))
            inv_rms("ss_x", SEQ)
            for k in range(KT):
                step(STT(hcl[:, k, CTX:CTX + SEQ], hT[:, k, :], a1[:, k, 0:1], rB[:, 0:SEQ], mul, mul))
            step.settle()
            for k in range(KT):
                ins = TS(hcl[:, k, CTX:CTX + SEQ], hcl[:, k, CTX:CTX + SEQ], modT[:, k, 0:1], None, add)
                if k == KT - 1:
                    ins.then_inc(hcl_ready, 1)
                else:
                    step(ins)
            dve.wait_ge(c2_loaded, 16)
            for i in range(8):
                bank = full(dve, ("rot2", i))
                raw = q2[:, 2 * i:2 * i + 2, :] if i < 4 else k2[:, 2 * (i - 4):2 * (i - 4) + 2, CTX:CTX + SEQ]
                if i:
                    dve.wait_ge(roped2_ready, i)
                TT(split(rot3[:, 0, :], SEQ), split(bank[:, :], SEQ), over(cst2("sin_ax"), 2), mul).then_inc(free(("rot2", i)), 1)
                step(TT(split(rot3[:, 1, :], SEQ), raw, over(cst2("cos_ax"), 2), mul))
                step.settle()
                emptied(dve, ("rot2", i))
                TT(raw, split(rot3[:, 0, :], SEQ), split(rot3[:, 1, :], SEQ), add).then_inc(roped2_ready, 1)
            for n in range(len(ATT) + 1):
                if n < len(ATT):
                    st = stat2[:, n % 2, :]
                    for i in range(2):
                        nc.vector.tensor_reduce(st[:, i:i + 1], full(dve, ("s2", n, i))[:, :], AX, ALU.max, negate=True).then_inc(free(("s2", n, i)), 1)
                    dve.wait_ge(banks.free[banks.at[("s2", n, 1)]], banks.free_when[("s2", n, 1)] - 1)
                    TS(st[:, 2:4], st[:, 0:2], 0.125, None, mul).then_inc(nmax_ready, 1)
                if n >= 1:
                    k = n - 1
                    st = stat2[:, k % 2, :]
                    emptied(dve, ("s2", k, 0))
                    emptied(dve, ("s2", k, 1))
                    step(nc.vector.reciprocal(st[:, 6:8], st[:, 4:6]))
                    step.settle()
                    step(TT(st[:, 7:8], st[:, 7:8], lam[:, 5:6], mul))
                    step(TS(esc[:, k % 2, 0, :], esc[:, k % 2, 0, :], st[:, 6:7], None, mul))
                    step.settle()
                    STT(esc[:, k % 2, 0, :], esc[:, k % 2, 1, :], st[:, 7:8], esc[:, k % 2, 0, :], mul, add).then_inc(prob_ready, 1)
            for j in range(4):
                emptied(dve, ("hss", j))
                r = q2[:, 2 * j:2 * j + 2, :].rearrange("p a b -> p (a b)")
                hj = heads[:, 2 * j:2 * j + 2, :].rearrange("p a b -> p (a b)")
                step(nc.vector.reciprocal(r, r))
                step.settle()
                ins = STT(hj, hj, small("subln"), r, mul, mul)
                if j == 3:
                    ins.then_inc(heads_ready, 1)
                else:
                    step(ins)
            for u in range(4):
                emptied(dve, ("gate2a", u))
                m = merged2[:, 2 * u:2 * u + 2, :].rearrange("p a b -> p (a b)")
                TT(m, gate2[:, 0, :], full(dve, ("ao2", u))[:, :], mul).then_inc(free(("ao2", u)), 1)
                emptied(dve, ("gate2f", u))
                TT(rot3[:, u % 2, :], gate2[:, 1, :], full(dve, ("fo", u))[:, :], mul).then_inc(free(("fo", u)), 1)
                emptied(dve, ("ao2", u))
                emptied(dve, ("fo", u))
                TT(m, m, rot3[:, u % 2, :], add).then_inc(merged2_ready, 1)
            for u in range(4):
                bank = full(dve, ("wo2", u))
                for j in range(2):
                    k = 2 * u + j
                    ins = STT(hT[:, k, :], bank[:, j * SEQ:(j + 1) * SEQ], modT[:, 16 + k, 0:1], hT[:, k, :], mul, add)
                    if j == 1:
                        ins.then_inc(free(("wo2", u)), 1)
            emptied(dve, ("wo2", 3))
            inv_rms("ss_x1", SEQ)
            scaled(h2, hT, a2, SEQ)
            step.settle()
            for k in range(KT):
                ins = TS(h2[:, k, :], h2[:, k, :], modT[:, 24 + k, 0:1], None, add)
                if k == KT - 1:
                    ins.then_inc(h2_ready, 1)
                else:
                    step(ins)
            CP(sel[:, :, :], each(ident[0:N_EXP, 0:N_EXP], 128)).then_inc(sel_ready, 1)
            nc.vector.memset(hid[:, 1, :, :], 0.0).then_inc(sel_ready, 1)
            for j in range(4):
                step(nc.vector.memset(rflat(300 + j, 1), float(4 - j)))
            rank = over(rflat(300, 4), 2)

            def r2(a, n=4):
                return rflat(a, 2 * n).rearrange("p (q n) -> p q n", n=n)

            def one(a):
                return each(rflat(a, 2), 4)

            def now(ins):
                step(ins)
                step.settle()

            def first_of(dst, src, best_at, tmp, tmp2):
                now(nc.vector.tensor_reduce(rflat(best_at, 2), src, AX, ALU.max))
                now(TT(r2(tmp), src, one(best_at), ALU.is_equal))
                now(TT(r2(tmp), r2(tmp), rank, mul))
                now(nc.vector.tensor_reduce(rflat(tmp2, 2), r2(tmp), AX, ALU.max))
                now(TT(r2(dst), r2(tmp), one(tmp2), ALU.is_equal))

            bank = full(dve, "router")
            logits = rflat(0, 40).rearrange("p (q n) -> p q n", n=20)
            TT(logits, bank[:, 0:40].rearrange("p (q n) -> p q n", n=20), over(small("b_router"), 2), add).then_inc(free("router"), 1)
            emptied(dve, "router")
            lg = logits[:, :, 0:4]
            first_of(72, lg, 40, 48, 64)
            TT(r2(80), lg, one(40), sub).then_inc(rexp_arg_ready, 1)
            for g in range(4):
                pick = rflat(72, 8).rearrange("p (q n) -> p q n", n=4)[:, :, g:g + 1].to_broadcast([128, 2, 4])
                if g == 0:
                    now(TT(r2(96), logits[:, :, 4:8], pick, mul))
                else:
                    now(TT(r2(104), logits[:, :, 4 + 4 * g:8 + 4 * g], pick, mul))
                    now(TT(r2(96), r2(96), r2(104), add))
            first_of(112, r2(96), 120, 128, 136)
            now(STT(r2(144), r2(112), -1.0e30, r2(96), mul, add))
            first_of(152, r2(144), 160, 168, 176)
            TT(rflat(180, 2), rflat(160, 2), rflat(120, 2), sub).then_inc(rexp_arg_ready, 1)
            dve.wait_ge(rexp_ready, 2)
            now(nc.vector.tensor_reduce(rflat(190, 2), r2(80), AX, add))
            now(nc.vector.reciprocal(rflat(192, 2), rflat(190, 2)))
            now(TS(rflat(194, 2), rflat(180, 2), 1.0, None, add))
            now(nc.vector.reciprocal(rflat(196, 2), rflat(194, 2)))
            now(TT(rflat(198, 2), rflat(196, 2), rflat(192, 2), mul))
            now(TT(rflat(202, 2), rflat(198, 2), rflat(180, 2), mul))
            now(TT(r2(208), r2(112), one(198), mul))
            now(TT(r2(216), r2(152), one(202), mul))
            now(TT(r2(208), r2(208), r2(216), add))
            for qt in range(2):
                ins = TT(rt[:, 18 + qt, 0:16].rearrange("p (g j) -> p g j", j=4), each(rflat(72 + 4 * qt, 4), 4), over(rflat(208 + 4 * qt, 4), 4), mul)
                if qt == 1:
                    ins.then_inc(gates_ready, 1)
                else:
                    step(ins)
            emptied(dve, ("ge", N_EXP // 2 - 1))

            def expert(e, parity, first=False):
                for b in range(4):
                    dve.wait_ge(w1_sig_ready, 4 * e + (b + 1))
                    s = sg[:, b, :]
                    ge = geB[:, e, :]
                    now_e(TT(s, s, ge, mul), e, 2 * b)
                    now_e(TT(s, s, psum[b][:, 0:SEQ], mul), e, 2 * b + 1)
                    TT(hid[:, parity, b, :], s, psum[b][:, SEQ:2 * SEQ], mul).then_inc(hid_ready[b], 1)

            def now_e(ins, e, k):
                ins.then_inc(gated_step, 1)
                dve.wait_ge(gated_step, 8 * e + (k + 1))

            expert(0, 0)
            with dve.Fori(1, N_EXP - 1, 2) as e:
                expert(e, 1)
                expert(e + 1, 0)
            expert(N_EXP - 1, 1)
            dve.wait_ge(unit_used[5], len(ORDER) // SLOTS)
            for k in range(KT):
                ins = STT(hT[:, k, :], psum[4 + k // 2][:, (k % 2) * SEQ:(k % 2 + 1) * SEQ], modT[:, 40 + k, 0:1], hT[:, k, :], mul, add)
                if k == KT - 1:
                    ins.then_inc(h1_ready, 1)
                else:
                    step(ins)
            step.settle()
            inv_rms("ss_out", SEQ)
            scaled(mix2, hT, small("g_final"), SEQ, out_ready)


def _freqs(dim):
    return (10000.0 ** (-(np.arange(0, dim, 2) / dim))).astype(np.float32)


def _rotation(block):
    r = np.zeros((128, 128), np.float32)
    for p in range(128):
        q = p % block
        if q < block // 2:
            r[p, p + block // 2] = -1.0
        else:
            r[p, p - block // 2] = 1.0
    return r.T


def _constants_one():
    c = np.zeros((128, C1_W), np.float32)

    def put(name, a):
        at, w = C1[name]
        c[:, at:at + w] = np.asarray(a).reshape(128, w)

    p, f = np.arange(128)[:, None], np.arange(128)[None, :]
    put("ident", p == f)
    put("ones", np.ones((128, 128)))
    put("eps", np.full((128, 1), EPS))
    put("upper", p <= f)
    put("rot_att", _rotation(128))
    put("rot_idx", _rotation(64))
    for name, dim in (("att", 128), ("idx", 64)):
        inv = _freqs(dim)
        ang = (np.arange(T, dtype=np.float32)[None, :] * inv[np.arange(128) % (dim // 2)][:, None]).astype(np.float64)
        put("cos_" + name, np.cos(ang))
        put("sin_" + name, np.sin(ang))
    put("meta_upper", (p // META == f // META) & (p <= f))
    put("meta_last", f == p // META * META + META - 1)
    put("levels", np.concatenate([(p >> (l + 1) == f >> (l + 1)) & ((p >> l) % 2 == 0) & ((f >> l) % 2 == 1) for l in range(LEVELS)], 1))
    key = np.arange(T)[None, :]
    put("causal", np.concatenate([np.where(key <= META + qt * 128 + p, 0.0, NEG) for qt in range(2)], 1))
    put("head_rows", p // META == np.arange(H)[None, :])
    return c


def _constants_two():
    c = np.zeros((128, C2_W), np.float32)

    def put(name, a):
        at, w = C2[name]
        c[:, at:at + w] = np.asarray(a).reshape(128, w)

    put("rot_ax", _rotation(32))
    p, n = np.arange(128), np.arange(SEQ)
    inv = (1.0 / (10000.0 ** (np.arange(16) / 16))).astype(np.float32)
    pos = np.where((p % 64 // 32 == 0)[:, None], (n // 64)[None, :], (n % 64)[None, :]).astype(np.float32)
    ang = (pos * inv[p % 16][:, None]).astype(np.float64)
    put("cos_ax", np.cos(ang))
    put("sin_ax", np.sin(ang))
    d = 2 * np.pi * np.outer(p, p) / 128
    put("dft_d", np.concatenate([np.cos(d), np.sin(d)], 1) / np.sqrt(128))
    t = 2 * np.pi * np.outer(n, n) / SEQ
    put("dft_n", np.concatenate([m[nt * 128:(nt + 1) * 128] for nt in range(2) for m in (np.cos(t), -np.sin(t))], 1) / np.sqrt(SEQ))
    return c


def _unit(w, rows, cols):
    return w[rows, cols].reshape(-1, 128, cols.stop - cols.start).transpose(1, 0, 2).reshape(128, -1)


def _stream(x):
    w_in, w_in2 = x["w_in"][0], x["w_in_2"][0]
    every = slice(0, D)
    offsets = {"gq": 0, "gk": 1024, "gv": 2048, "gz": 3072, "aq": 4112, "ak": 5136, "av": 5392, "iq": 5648, "gate_a": 6232, "gate_b": 7256}
    offsets2 = {"q2": 0, "k2": 1024, "v2": 2048, "f2": 3072, "gate2a": 3584, "gate2f": 4608}
    whole = {"mod": x["w_mod_2"][0], "bg": x["w_branch_gdn"][0], "bd": x["w_branch_dsa"][0], "wo": x["w_out"][0], "up": x["w_up"][0],
             "ao": x["w_attn_out_2"][0], "wo2": x["w_out_2"][0]}
    s = np.empty((len(ORDER), 128, KT * UNIT_COLS), np.float32)
    for i, (kind, u) in enumerate(ORDER):
        c = slice(u * 256, (u + 1) * 256)
        if kind in offsets:
            s[i] = _unit(w_in, every, slice(offsets[kind] + c.start, offsets[kind] + c.stop))
        elif kind in offsets2:
            s[i] = _unit(w_in2, every, slice(offsets2[kind] + c.start, offsets2[kind] + c.stop))
        elif kind in whole:
            s[i] = _unit(whole[kind], every, c)
        elif kind == "down":
            cp, kg = divmod(u, 4)
            s[i] = _unit(x["w_down"][0], slice(kg * D, (kg + 1) * D), slice(cp * 256, (cp + 1) * 256))
        elif kind == "fo":
            s[i] = _unit(x["w_four_out_2"][0], slice(0, 512), slice(u * 512, (u + 1) * 512))
        elif kind == "e_up":
            e, q = divmod(u, 4)
            w = x["w_exp_gate_2" if q % 2 == 0 else "w_exp_up_2"][0, e]
            s[i] = _unit(w, every, slice(q // 2 * 256, (q // 2 + 1) * 256))
        else:
            e, q = divmod(u, 2)
            s[i] = _unit(x["w_exp_down_2"][0, e], slice(0, EH), slice(q * 512, (q + 1) * 512))
    return s


def _smalls(x):
    c = np.zeros((128, SM_W), np.float32)

    def put(name, a):
        at, w = SM[name]
        c[:, at:at + w] = a.reshape(128, w)

    def cols(v):
        return v.reshape(-1, 128).T

    for name, v in (("g_pre_mix", x["pre_mix_norm"]), ("g_post_mix", x["post_mix_norm"]), ("g_pre_mlp", x["pre_mlp_norm"]),
                    ("g_post_mlp", x["post_mlp_norm"]), ("g_n1", x["norm1_g_2"]), ("g_n2", x["norm2_g_2"]), ("g_final", x["final_g_2"]),
                    ("gdn_norm", x["gdn_norm"]), ("subln", x["subln_g_2"]), ("b_mod", x["b_mod_2"])):
        put(name, cols(v))
    put("conv", x["conv_w"][0].reshape(4, 24, 128).transpose(2, 1, 0))
    put("c", np.stack([cols(x["c_2"]), cols(x["c_ctx_2"])], 2))
    put("dt_bias", np.broadcast_to(x["dt_bias"], (128, H)))
    put("a_log", np.broadcast_to(x["a_log"], (128, H)))
    put("b_router", np.broadcast_to(np.concatenate([x["b_router_group_2"][0], x["b_router_expert_2"][0]]), (128, 20)))
    return c


def _small_weights(x):
    w = x["w_in"][0]

    def cols(a, b):
        return w[:, a:b].reshape(KT, 128, b - a).transpose(1, 0, 2)

    ik = cols(6160, 6224)
    return np.concatenate([cols(4096, 4112).reshape(128, -1), np.concatenate([ik, ik], 2).reshape(128, -1),
                           cols(6224, 6232).reshape(128, -1)], 1)


def _columns(a):
    return np.ascontiguousarray(a.T.reshape(KT, 128, -1).transpose(1, 0, 2))


def kernel(**inputs):
    import concourse.bacc as bacc
    from concourse.bass_utils import run_bass_kernel_spmd

    x = {name: np.asarray(a) for name, a in inputs.items()}
    router = np.concatenate([x["w_router_group_2"][0], x["w_router_expert_2"][0]], 1)
    arrays = {
        "stream": _stream(x),
        "h_in": _columns(np.concatenate([x["meta_tokens"], x["x"][0]])),
        "ctx_in": _columns(x["ctx_2"][0]),
        "constants_one": _constants_one(),
        "constants_two": _constants_two(),
        "smalls": _smalls(x),
        "small_weights": _small_weights(x),
        "router": np.ascontiguousarray(router.reshape(KT, 128, 20).transpose(1, 0, 2)),
        "lambdas": np.stack([x["lam_q1_2"][0], x["lam_k1_2"][0], x["lam_q2_2"][0], x["lam_k2_2"][0]], 1),
    }
    nc = bacc.Bacc("TRN2", target_bir_lowering=False, num_devices=1)
    args = [nc.dram_tensor(name, a.shape, mybir.dt.float32, kind="ExternalInput").ap() for name, a in arrays.items()]
    args.append(nc.dram_tensor("result", (128, KT, SEQ), mybir.dt.float32, kind="ExternalOutput").ap())
    build(nc, *args)
    r = run_bass_kernel_spmd(nc, [arrays], core_ids=[0])
    return np.ascontiguousarray(r.results[0]["result"].transpose(2, 1, 0)).reshape(1, SEQ, D)
```

```python
import math
from contextlib import ExitStack

import concourse.bass as bass
import numpy as np
from concourse import mybir

D = 1024
KT = D // 128
META = 16
SEQ = 256
T = META + SEQ
H = 8
CH = 128
NCH = SEQ // CH
NSYS = H * NCH
LEVELS = 7
META_LEVELS = 4
TOPK = SEQ // 4
KV_HEADS = 2
CTX = 256
DFF = 4096
FT = DFF // 128
EPS = 1e-6
N_EXP = 16
LAM_INIT = 0.8 - 0.6 * math.exp(-0.0)
EH = D // 2
NGRP = 4
PAIRS = N_EXP // 2
CAP = 64
UNIT_COLS = 256
SLOTS = 6
NEG = -3.0e38
TAKEN = -3.3e38
MOD_TILES = 6 * D // 128
MOD_UNITS = MOD_TILES // 2

def _layout(widths):
    at, out = 0, {}
    for name, w in widths:
        out[name] = (at, w)
        at += w
    return out, at

C1, C1_W = _layout([("ident", 128), ("ones", 128), ("eps", 1), ("upper", 128), ("rot_att", 128), ("rot_idx", 128),
                    ("cos_att", T), ("sin_att", T), ("cos_idx", T), ("sin_idx", T),
                    ("meta_upper", 128), ("meta_last", 128), ("levels", LEVELS * 128),
                    ("causal", NCH * T), ("head_rows", H)])
C2, C2_W = _layout([("rot_ax", 128), ("cos_ax", SEQ), ("sin_ax", SEQ), ("dft_d", 256), ("dft_n", 4 * SEQ),
                    ("earlier", 128), ("iota", CAP)])
SM, SM_W = _layout([("g_pre_mix", KT), ("g_post_mix", KT), ("g_pre_mlp", KT), ("g_post_mlp", KT),
                    ("g_n1", KT), ("g_n2", KT), ("g_final", KT), ("conv", 24 * 4), ("gdn_norm", 1),
                    ("subln", 1), ("b_mod", MOD_TILES), ("c", KT * 2), ("dt_bias", H), ("a_log", H),
                    ("b_router", 20)])
C2_AT = C1["upper"][0]
WS, WS_W = _layout([("gba", KT * 16), ("ik", KT * 128), ("iw", KT * 8)])

def weight_order():
    order = [("gk", u) for u in range(4)] + [("gv", u) for u in range(4)] + [("gq", u) for u in range(4)]
    order += [("mod", u) for u in range(6)]
    order += [("gz", u) for u in range(4)] + [("aq", u) for u in range(4)] + [("ak", 0), ("av", 0)]
    order += [("iq", u) for u in range(2)]
    for u in range(4):
        order += [("gate_a", u), ("bg", u)]
    for u in range(4):
        order += [("gate_b", u), ("bd", u)]
    order += [("wo", u) for u in range(4)]
    order += [("mod", u) for u in range(6, 11)]
    order += [("up", u) for u in range(16)]
    order += [("down", u) for u in range(16)]
    order += [("mod", u) for u in range(11, 16)]
    order += [("q2", u) for u in range(4)] + [("k2", u) for u in range(4)] + [("v2", u) for u in range(4)]
    order += [("f2", u) for u in range(2)]
    order += [("mod", 16), ("mod", 17)]
    for u in range(4):
        order += [("gate2a", u)] + ([("mod", 18), ("mod", 19)] if u == 0 else []) + [("ao", u), ("gate2f", u)] + ([("fo", u // 2)] if u % 2 == 0 else [])
    order += [("wo2", u) for u in range(4)]
    order += [("mod", u) for u in range(20, 24)]
    for e in range(N_EXP):
        order += [("e_up", 4 * e + u) for u in range(4)] + [("e_down", 2 * e + u) for u in range(2)]
    return order

ORDER = weight_order()
FIRST_EXPERT = ORDER.index(("e_up", 0))
BASE = FIRST_EXPERT // SLOTS
assert len(ORDER) % SLOTS == 0 and FIRST_EXPERT % SLOTS == 0


class Steps:

    def __init__(self, eng, sem):
        self.eng, self.sem, self.n = eng, sem, 0

    def __call__(self, ins):
        self.n += 1
        ins.then_inc(self.sem, 1)

    def settle(self):
        self.eng.wait_ge(self.sem, self.n)


class Banks:

    def __init__(self, full, free):
        self.full, self.free = full, free
        self.turn, self.filled, self.freed = 0, [0] * 8, [0] * 8
        self.at, self.full_when, self.free_when = {}, {}, {}

    def take(self, name, drains, bank=None):
        if bank is None:
            bank = self.turn % 8
            self.turn += 1
        before = self.freed[bank]
        self.freed[bank] += drains
        self.at[name] = bank
        self.free_when[name] = self.freed[bank]
        return bank, before

    def fill(self, name):
        bank = self.at[name]
        self.filled[bank] += 1
        self.full_when[name] = (self.full[bank], self.filled[bank])
        return self.full[bank]


def build(nc, stream, h_in, ctx_in, c1_in, c2_in, sm_in, ws_in, wr_in, lam_in, out):
    f32 = mybir.dt.float32
    ALU, ACT, AX = mybir.AluOpType, mybir.ActivationFunctionType, mybir.AxisListType.X
    mul, add, sub = ALU.mult, ALU.add, ALU.subtract
    top = ExitStack()
    with top:
        def sb(stack, name, *shape):
            return stack.enter_context(nc.sbuf_tensor(name, list(shape), f32))

        def sem(name):
            return top.enter_context(nc.semaphore(name))

        ring = sb(top, "ring", 128, SLOTS, KT * UNIT_COLS)
        c1 = sb(top, "c1", 128, C1_W)
        sm = sb(top, "sm", 128, SM_W)
        hT = sb(top, "hT", 128, KT, SEQ)
        modT = sb(top, "modT", 128, MOD_TILES, 2)
        silu_c = sb(top, "silu_c", 128, KT, 2)
        a1 = sb(top, "a1", 128, KT, 2)
        a2 = sb(top, "a2", 128, KT)
        rB = sb(top, "rB", 128, T)
        root = sb(top, "root", 128, T)
        lam = sb(top, "lam", 128, 8)
        wr = sb(top, "wr", 128, KT, 20)

        def cst(name, rows=128):
            a, w = C1[name]
            return c1[0:rows, a:a + w]

        def small(name):
            a, w = SM[name]
            return sm[:, a:a + w]

        ident, ones, upper, eps = cst("ident"), cst("ones"), cst("upper"), cst("eps")

        with ExitStack() as mixer:
            nT = sb(mixer, "nT", 128, KT, T)
            ws = sb(mixer, "ws", 128, WS_W)
            y_gdn = sb(mixer, "y_gdn", 128, H, SEQ)
            with ExitStack() as m:
                kc = sb(m, "kc", 128, H, T)
                vc = sb(m, "vc", 128, H, T)
                qc = sb(m, "qc", 128, H, T)
                v_beta = sb(m, "v_beta", 128, NSYS, 128)
                attn = sb(m, "attn", 128, NSYS, 128)
                k_tail = sb(m, "k_tail", 128, NSYS, 128)
                inv = sb(m, "inv", 128, NSYS, 128)
                invT = sb(m, "invT", 128, NSYS, 128)
                low = sb(m, "low", 128, NSYS, 128)
                masked = sb(m, "masked", 128, 2, 512)
                prod = sb(m, "prod", 128, 2, 512)
                state = sb(m, "state", 128, 2, H * 128)
                scr = sb(m, "scr", 128, 2, 1024)
                metas = sb(m, "metas", 128, 10, 128)
                mcol = sb(m, "mcol", 128, 4)
                egl = sb(m, "egl", 128, NSYS)
                tok = sb(m, "tok", 128, 8, 24)
            with ExitStack() as m:
                merged = sb(m, "merged", 128, KT, SEQ)
                gate = sb(m, "gate", 128, 2, 512)
                aq = sb(m, "aq", 128, H, SEQ)
                ak = sb(m, "ak", 128, KV_HEADS, T)
                av = sb(m, "av", 128, 3, KV_HEADS * 128)
                iq = sb(m, "iq", 128, 4, SEQ)
                ik = sb(m, "ik", 128, T)
                iw = sb(m, "iw", 128, NCH, H)
                rot1 = sb(m, "rot1", 128, 512)
                rot2 = sb(m, "rot2", 128, 512)
                relu = sb(m, "relu", 128, 2, T)
                score = sb(m, "score", 128, NCH, T)
                work = sb(m, "work", 128, 2, T)
                best = sb(m, "best", 128, 8)
                bias = sb(m, "bias", 128, NCH, T)
                lmask = sb(m, "lmask", 128, 2, T)
                prob = sb(m, "prob", 128, 2, T)
                probT = sb(m, "probT", 128, 2, 3 * 128)
                stat = sb(m, "stat", 128, 2, 4)
                y_dsa = sb(m, "y_dsa", 128, H, SEQ)
        with ExitStack() as rest:
            ctxT = sb(rest, "ctxT", 128, KT, CTX)
            with ExitStack() as m:
                _under = sb(m, "under_merged", 128, KT * T + WS_W + H * SEQ - KT * CTX)
                _merged = sb(m, "merged_still", 128, KT, SEQ)
                mix = sb(m, "mix", 128, KT, SEQ)
                sq = sb(m, "sq", 128, KT, SEQ)
                nM = sb(m, "nM", 128, KT, SEQ)
                up = sb(m, "up", 128, FT, SEQ)
            with ExitStack() as m:
                hcl = sb(m, "hcl", 128, KT, CTX + SEQ)
                q2 = sb(m, "q2", 128, H, SEQ)
                k2 = sb(m, "k2", 128, H, CTX + SEQ)
                v2 = sb(m, "v2", 128, 4, D)
                f2 = sb(m, "f2", 128, 4, SEQ)
                zdft = sb(m, "zdft", 128, 4, 2, 256)
                four = sb(m, "four", 128, 4, SEQ)
                sq1 = sb(m, "sq1", 128, KT, SEQ)
                heads = sb(m, "heads", 128, H, SEQ)
                esc = sb(m, "esc", 128, 2, 2, 512)
                aT = sb(m, "aT", 128, 2, 512)
                stat2 = sb(m, "stat2", 128, 2, 8)
                rot3 = sb(m, "rot3", 128, 2, 512)
                merged2 = sb(m, "merged2", 128, KT, SEQ)
                gate2 = sb(m, "gate2", 128, 2, 512)
            with ExitStack() as m:
                mix2 = sb(m, "mix2", 128, KT, SEQ)
                sq2 = sb(m, "sq2", 128, KT, SEQ)
                h2 = sb(m, "h2", 128, KT, SEQ)
                h2tok = sb(m, "h2tok", 128, 2, D)
                rt = sb(m, "rt", 128, 24, 32)
                slot_of = sb(m, "slot_of", 128, 2, 2)
                gate_of = sb(m, "gate_of", 128, 2, 2)
                pick = sb(m, "pick", 128, 2, 2 * CAP)
                pick_gated = sb(m, "pick_gated", 128, 2, 2 * CAP)
                spread = sb(m, "spread", 128, SEQ)
                xg = sb(m, "xg", 128, KT, 2 * CAP)
                sg = sb(m, "sg", 128, 2, 4 * CAP)
                hid = sb(m, "hid", 128, 2, 4, CAP)
                ys = sb(m, "ys", 128, KT, 2 * CAP)
                ysT = sb(m, "ysT", 128, KT * 128)
                passes = m.enter_context(nc.sbuf_tensor("passes", [128, PAIRS], mybir.dt.int32))
                ring2 = sb(m, "ring2", 128, SLOTS, KT * UNIT_COLS)
        c2 = c1[:, C2_AT:C2_AT + C2_W]

        def cst2(name):
            a, w = C2[name]
            return c2[:, a:a + w]

        psum = [top.enter_context(nc.psum_tensor(f"bank{b}", [128, 512], f32)) for b in range(8)]
        banks = Banks([sem(f"bank_full{b}") for b in range(8)], [sem(f"bank_free{b}") for b in range(8)])

        unit_loaded = [sem(f"unit_loaded{s}") for s in range(SLOTS)]
        unit_used = [sem(f"unit_used{s}") for s in range(SLOTS)]
        h_loaded, c1_loaded, sm_loaded, ws_loaded = sem("h_loaded"), sem("c1_loaded"), sem("sm_loaded"), sem("ws_loaded")
        res_loaded, ctx_loaded, c2_loaded, lam_loaded, wr_loaded = (sem("res_loaded"), sem("ctx_loaded"), sem("c2_loaded"),
                                                        sem("lam_loaded"), sem("wr_loaded"))
        unit_loaded2 = [sem(f"unit_loaded2_{s}") for s in range(SLOTS)]
        unit_used2 = [sem(f"unit_used2_{s}") for s in range(SLOTS)]
        act_step, dve_step, out_stored = sem("act_step"), sem("dve_step"), sem("out_stored")

        block = top.enter_context(nc.Block())

        def full(eng, name):
            eng.wait_ge(*banks.full_when[name])
            return psum[banks.at[name]]

        def free(name):
            return banks.free[banks.at[name]]

        def emptied(eng, name, but=0):
            eng.wait_ge(banks.free[banks.at[name]], banks.free_when[name] - but)

        sq_ready = sem("sq_ready")
        silu_ready = sem("silu_ready")
        sig_ready = sem("sig_ready")
        nT_ready = sem("nT_ready")
        normed_ready = sem("normed_ready")
        absx_ready = sem("absx_ready")
        softplus_ready = sem("softplus_ready")
        tri_ready = sem("tri_ready")
        meta_arg_ready = sem("meta_arg_ready")
        meta_exp_ready = sem("meta_exp_ready")
        decay_arg_ready = sem("decay_arg_ready")
        decay_exp_ready = sem("decay_exp_ready")
        gated_step = sem("gated_step")
        masked_ready = sem("masked_ready")
        scan_ready = sem("scan_ready")
        y_ready = sem("y_ready")
        roped_ready = sem("roped_ready")
        score_ready = sem("score_ready")
        nmax_ready = sem("nmax_ready")
        pexp_ready = sem("pexp_ready")
        prob_ready = sem("prob_ready")
        merged_ready = sem("merged_ready")
        h1_ready = sem("h1_ready")
        nM_ready = sem("nM_ready")
        up_ready = sem("up_ready")
        lamp_ready = sem("lamp_ready")
        hcl_ready = sem("hcl_ready")
        roped2_ready = sem("roped2_ready")
        heads_ready = sem("heads_ready")
        merged2_ready = sem("merged2_ready")
        h2_ready = sem("h2_ready")
        zeros_ready = sem("zeros_ready")
        rexp_arg_ready = sem("rexp_arg_ready")
        rexp_ready = sem("rexp_ready")
        routed_ready = sem("routed_ready")
        passes_ready = sem("passes_ready")
        slots_loaded = sem("slots_loaded")
        pick_ready = sem("pick_ready")
        spread_full = sem("spread_full")
        spread_ready = sem("spread_ready")
        xg_full = [sem(f"xg_full{j}") for j in range(2)]
        xg_ready = [sem(f"xg_ready{j}") for j in range(2)]
        sig_w1_ready = [sem(f"sig_w1_ready{j}") for j in range(2)]
        hid_ready = [sem(f"hid_ready{j}") for j in range(2)]
        ys_ready = sem("ys_ready")
        ysT_full = sem("ysT_full")
        ysT_ready = sem("ysT_ready")
        scattered = sem("scattered")
        moe_step = sem("moe_step")
        out_ready = sem("out_ready")

        LEVEL_ITEMS = [(l, g) for l in range(LEVELS) for g in (4, 0, 1, 2, 3) if g < 4 or l < META_LEVELS]

        CONV_TILES = [(kind, j) for kind in ("gk", "gv", "gq") for j in range(H)]

        def conv_dst(t):
            kind, j = CONV_TILES[t]
            return {"gk": kc, "gv": vc, "gq": qc}[kind][:, j, :]

        def raw_of(kind, j):
            if kind == "ik":
                return ik[:, :].unsqueeze(1), T
            if kind == "ak":
                return ak[:, j:j + 1, :], T
            return (aq if kind == "aq" else iq)[:, 2 * j:2 * j + 2, :], 512

        def rflat(a, n):
            return rt[:, :, :].rearrange("p a b -> p (a b)")[:, a:a + n]

        def systems(g):
            return [4 * g + s for s in range(4)] if g < 4 else [None]

        def sysview(t, meta_slot, s):
            return t[:, s, :] if s is not None else metas[:, meta_slot, :]

        def chunk(t, h, ci):
            a = META + ci * CH
            return t[:, h, a:a + CH]

        def nkeys(qt):
            return META + (qt + 1) * 128

        def key_tiles(qt):
            n = nkeys(qt)
            return [(a, min(128, n - a)) for a in range(0, n, 128)]

        ATT = [(qt, h) for qt in range(2) for h in range(H)]
        ROPES = [("aq", j) for j in range(4)] + [("ak", j) for j in range(2)] + [("iq", j) for j in range(2)] + [("ik", 0)]

        def each_pass(eng, body, start_pair=lambda pair: None):
            eng.wait_ge(passes_ready, 1)
            so_far = eng.alloc_register()
            eng.reg_mov(so_far, 0)
            with eng.Fori(0, PAIRS) as pair:
                start_pair(pair)
                count = eng.value_load(passes[0:1, bass.ds(pair, 1)], min_val=1, max_val=SEQ // CAP)
                with eng.Fori(0, count):
                    body(pair, eng.snap(so_far, min_val=0, max_val=PAIRS * SEQ // CAP))
                    eng.reg_add(so_far, so_far, 1)
            return eng.snap(so_far, min_val=PAIRS, max_val=PAIRS * SEQ // CAP)

        @block.tensor
        def _(pe):
            at = [0]

            def unit(kind, u):
                assert ORDER[at[0]] == (kind, u), (ORDER[at[0]], kind, u)
                s, n = at[0] % SLOTS, at[0] // SLOTS + 1
                at[0] += 1
                pe.wait_ge(unit_loaded[s], 16 * n)
                return s, n

            def by_k(s, cols=UNIT_COLS):
                return ring[:, s, :].rearrange("p (k n) -> p k n", n=cols)

            def take(name, drains=1, bank=None):
                b, before = banks.take(name, drains, bank)
                if before:
                    pe.wait_ge(banks.free[b], before)
                return psum[b]

            def done(name, ins):
                ins.then_inc(banks.fill(name), 1)

            def group(dst, pairs):
                for i, (lhs, rhs) in enumerate(pairs):
                    last = nc.tensor.matmul(dst, lhs, rhs, start=(i == 0), stop=(i == len(pairs) - 1))
                return last

            def tiles_of_unit(kind, u, rhs, n, names, kt=KT, drains=1):
                s, cnt = unit(kind, u)
                w = by_k(s)
                if len(names) == 2:
                    for j in range(2):
                        dst = take(names[j], drains)
                        last = group(dst[:, 0:n], [(w[:, k, j * 128:(j + 1) * 128], rhs[:, k, :]) for k in range(kt)])
                        if j == 0:
                            done(names[0], last)
                else:
                    dst = take(names[0], drains)
                    for j in range(2):
                        last = group(dst[:, j * n:(j + 1) * n], [(w[:, k, j * 128:(j + 1) * 128], rhs[:, k, :]) for k in range(kt)])
                last.then_inc(unit_used[s], 1)
                banks.full_when[names[-1]] = (unit_used[s], cnt)

            def mod_unit(u):
                tiles_of_unit("mod", u, silu_c, 2, [("mod", u)])

            def feature_sum(name, src, n, drains=1):
                dst = take(name, drains)
                done(name, group(dst[:, 0:n], [(ones, src[:, k, :]) for k in range(KT)]))

            pe.wait_ge(c1_loaded, 16)
            pe.wait_ge(sq_ready, 1)
            feature_sum("ss_in", vc[:, :, :], T)

            pe.wait_ge(nT_ready, 1)
            pe.wait_ge(ws_loaded, 16)
            gba = ws[:, 0:KT * 16].rearrange("p (k n) -> p k n", n=16)
            dst = take("gba", 2)
            for g, a in enumerate((0, META, META + CH)):
                last = group(dst[:, g * 16:(g + 1) * 16], [(nT[:, k, a:a + 128], gba[:, k, :]) for k in range(KT)])
            done("gba", last)

            for kind in ("gk", "gv", "gq"):
                for u in range(4):
                    tiles_of_unit(kind, u, nT, T, [(kind, 2 * u), (kind, 2 * u + 1)])

            for i in range(12):
                n = T if i < 8 else 512
                pe.wait_ge(sq_ready, 2 + i)
                dst = take(("l2", i), 1)
                done(("l2", i), nc.tensor.matmul(dst[:, 0:n], ones, scr[:, i % 2, 0:n], start=True, stop=True))
            pe.wait_ge(silu_ready, 1)
            for u in range(4):
                mod_unit(u)

            pe.wait_ge(tri_ready, 1)
            dst = take("gct", 2)
            for ci in range(NCH):
                last = nc.tensor.matmul(dst[:, ci * 8:(ci + 1) * 8], upper, tok[:, 3, (1 + ci) * 8:(2 + ci) * 8], start=True, stop=True)
            done("gct", last)
            dst = take("metaGB", 1)
            nc.tensor.matmul(dst[:, 0:128], ones[0:META, :], metas[0:META, 0, :], start=True, stop=True)
            done("metaGB", nc.tensor.matmul(dst[:, 128:256], ones[0:META, :], metas[0:META, 1, :], start=True, stop=True))
            dst = take("metaK", 1)
            nc.tensor.matmul(dst[:, 0:128], metas[:, 2, :], metas[:, 2, :], start=True, stop=True)
            nc.tensor.transpose(dst[:, 128:256], metas[:, 2, :], ident)
            done("metaK", nc.tensor.transpose(dst[:, 256:384], metas[:, 3, :], ident))

            for h in range(H):
                dst = take(("GB", h), 2)
                for ci in range(NCH):
                    sy = h * NCH + ci
                    nc.tensor.matmul(dst[:, ci * 128:(ci + 1) * 128], inv[:, sy, :], upper, start=True, stop=True)
                    last = nc.tensor.matmul(dst[:, 256 + ci * 128:384 + ci * 128], invT[:, sy, :], ident, start=True, stop=True)
                done(("GB", h), last)
                dst = take(("KQ", h), 1)
                for ci in range(NCH):
                    k_c, q_c = chunk(kc, h, ci), chunk(qc, h, ci)
                    nc.tensor.matmul(dst[:, ci * 128:(ci + 1) * 128], k_c, k_c, start=True, stop=True)
                    last = nc.tensor.matmul(dst[:, 256 + ci * 128:384 + ci * 128], k_c, q_c, start=True, stop=True)
                done(("KQ", h), last)
                dst = take(("TR", h), 1)
                for ci in range(NCH):
                    nc.tensor.transpose(dst[:, ci * 128:(ci + 1) * 128], chunk(kc, h, ci), ident)
                    last = nc.tensor.transpose(dst[:, 256 + ci * 128:384 + ci * 128], chunk(vc, h, ci), ident)
                done(("TR", h), last)

            def level_p(n):
                l, g = LEVEL_ITEMS[n]
                pe.wait_ge(masked_ready, n + 1)
                if l > 0:
                    emptied(pe, ("QT", LEVEL_ITEMS.index((l - 1, g))))
                dst = take(("P", n))
                for j, s in enumerate(systems(g)):
                    rhs = ident if l == 0 else sysview(inv, 8, s)
                    last = nc.tensor.matmul(dst[:, j * 128:(j + 1) * 128], masked[:, n % 2, j * 128:(j + 1) * 128], rhs, start=True, stop=True)
                done(("P", n), last)

            def level_q(n):
                l, g = LEVEL_ITEMS[n]
                emptied(pe, ("P", n))
                end = META_LEVELS - 1 if g == 4 else LEVELS - 1
                if 0 < l < end:
                    dst = take(("Q", n), 1)
                    for j, s in enumerate(systems(g)):
                        last = nc.tensor.matmul(dst[:, j * 128:(j + 1) * 128], sysview(invT, 9, s), prod[:, n % 2, j * 128:(j + 1) * 128], start=True, stop=True)
                    done(("Q", n), last)
                dst = take(("QT", n), 1)
                for j, s in enumerate(systems(g)):
                    rhs = ident if l == 0 else sysview(invT, 9, s)
                    last = nc.tensor.matmul(dst[:, j * 128:(j + 1) * 128], prod[:, n % 2, j * 128:(j + 1) * 128], rhs, start=True, stop=True)
                done(("QT", n), last)

            for n in range(len(LEVEL_ITEMS)):
                level_p(n)
                if n >= 1:
                    level_q(n - 1)
            mod_unit(4)
            level_q(len(LEVEL_ITEMS) - 1)
            mod_unit(5)
            assert ORDER[at[0]] == ("gz", 0), ORDER[at[0]]

            pe.wait_ge(scan_ready, 1)
            dst = take("meta_v", 1)
            emptied(pe, ("QT", LEVEL_ITEMS.index((META_LEVELS - 1, 4))))
            done("meta_v", nc.tensor.matmul(dst[:, 0:128], metas[:, 9, :], metas[:, 7, :], start=True, stop=True))
            emptied(pe, "meta_v")
            for hg in range(2):
                dst = take(("S0", hg), 1)
                for j in range(4):
                    h = hg * 4 + j
                    last = nc.tensor.matmul(dst[:, j * 128:(j + 1) * 128], scr[:, 0, h * 128:(h + 1) * 128], metas[:, 3, :], start=True, stop=True)
                done(("S0", hg), last)
            emptied(pe, ("QT", len(LEVEL_ITEMS) - 1))
            for ci in range(NCH):
                for hg in range(2):
                    emptied(pe, ("S0", hg) if ci == 0 else ("dS", ci - 1, hg))
                    dst = take(("kS", ci, hg), 1)
                    for j in range(4):
                        h = hg * 4 + j
                        last = nc.tensor.matmul(dst[:, j * 128:(j + 1) * 128], chunk(kc, h, ci), state[:, ci, h * 128:(h + 1) * 128], start=True, stop=True)
                    done(("kS", ci, hg), last)
                for hg in range(2):
                    emptied(pe, ("kS", ci, hg))
                    dst = take(("vn", ci, hg), 1)
                    for j in range(4):
                        sy = (hg * 4 + j) * NCH + ci
                        last = nc.tensor.matmul(dst[:, j * 128:(j + 1) * 128], invT[:, sy, :], scr[:, hg, j * 128:(j + 1) * 128], start=True, stop=True)
                    done(("vn", ci, hg), last)
                for hg in range(2):
                    emptied(pe, ("vn", ci, hg))
                    if ci + 1 < NCH:
                        dst = take(("dS", ci, hg), 1)
                        for j in range(4):
                            sy = (hg * 4 + j) * NCH + ci
                            last = nc.tensor.matmul(dst[:, j * 128:(j + 1) * 128], k_tail[:, sy, :], scr[:, hg, 512 + j * 128:640 + j * 128], start=True, stop=True)
                        done(("dS", ci, hg), last)
                    dst = take(("o", ci, hg), 1)
                    for j in range(4):
                        h = hg * 4 + j
                        last = group(dst[:, j * 128:(j + 1) * 128],
                                     [(state[:, ci, h * 128:(h + 1) * 128], chunk(qc, h, ci)),
                                      (scr[:, hg, 512 + j * 128:640 + j * 128], attn[:, h * NCH + ci, :])])
                    done(("o", ci, hg), last)
            for u in range(4):
                tiles_of_unit("gz", u, nT[:, :, META:T], SEQ, [("gz", u)])
            pe.wait_ge(sq_ready, 14)
            for j in range(4):
                dst = take(("yss", j), 1)
                done(("yss", j), nc.tensor.matmul(dst[:, :], ones, low[:, 4 * j:4 * j + 4, :], start=True, stop=True))

            def rope(i):
                kind, j = ROPES[i]
                emptied(pe, "ik" if kind == "ik" else ROPES[i])
                dst = take(("rot", i), 1)
                src, n = raw_of(kind, j)
                r = "rot_att" if kind in ("aq", "ak") else "rot_idx"
                done(("rot", i), nc.tensor.matmul(dst[:, 0:n], cst(r), src, start=True, stop=True))

            real = nT[:, :, META:T]
            for u in range(4):
                tiles_of_unit("aq", u, real, SEQ, [("aq", u)])
                if u:
                    rope(u - 1)
            tiles_of_unit("ak", 0, nT, T, [("ak", 0), ("ak", 1)])
            rope(3)
            s, cnt = unit("av", 0)
            for g, (a, m) in enumerate(((0, 128), (128, 128), (256, META))):
                dst = take(("av", g), 1)
                last = group(dst[0:m, 0:256], [(nT[:, k, a:a + m], by_k(s)[:, k, :]) for k in range(KT)])
                if g < 2:
                    done(("av", g), last)
            last.then_inc(unit_used[s], 1)
            banks.full_when[("av", 2)] = (unit_used[s], cnt)
            rope(4)
            rope(5)
            tiles_of_unit("iq", 0, real, SEQ, [("iq", 0)])
            tiles_of_unit("iq", 1, real, SEQ, [("iq", 1)])
            rope(6)
            wik = ws[:, WS["ik"][0]:WS["ik"][0] + KT * 128].rearrange("p (k n) -> p k n", n=128)
            wiw = ws[:, WS["iw"][0]:WS["iw"][0] + KT * 8].rearrange("p (k n) -> p k n", n=8)
            dst = take("ik")
            done("ik", group(dst[:, 0:T], [(wik[:, k, :], nT[:, k, :]) for k in range(KT)]))
            dst = take("iw")
            for qt in range(2):
                a = META + qt * 128
                last = group(dst[:, qt * 8:(qt + 1) * 8], [(nT[:, k, a:a + 128], wiw[:, k, :]) for k in range(KT)])
            done("iw", last)
            rope(7)
            rope(8)

            pe.wait_ge(roped_ready, 9)
            for qt, h in ATT:
                a = 64 * (h % 2)
                dst = take(("ix", qt, h))
                done(("ix", qt, h), nc.tensor.matmul(dst[:, 0:nkeys(qt)], iq[a:a + 64, h // 2, qt * 128:(qt + 1) * 128],
                                                     ik[a:a + 64, 0:nkeys(qt)], start=True, stop=True))
            pe.wait_ge(y_ready, 1)
            for u in range(4):
                tiles_of_unit("gate_a", u, real, SEQ, [("gate_a", u)])
                tiles_of_unit("bg", u, y_gdn, SEQ, [("bg", u)])

            def att_logits(n):
                qt, h = ATT[n]
                dst = take(("lg", n))
                done(("lg", n), nc.tensor.matmul(dst[:, 0:nkeys(qt)], aq[:, h, qt * 128:(qt + 1) * 128],
                                                 ak[:, h // 4, 0:nkeys(qt)], start=True, stop=True))

            def att_transpose(n):
                qt, h = ATT[n]
                pe.wait_ge(prob_ready, n + 1)
                dst = take(("pt", n), 1)
                for i, (a, m) in enumerate(key_tiles(qt)):
                    last = nc.tensor.transpose(dst[0:m, i * 128:(i + 1) * 128], prob[:, n % 2, a:a + m], ident)
                done(("pt", n), last)

            def att_values(n):
                qt, h = ATT[n]
                emptied(pe, ("pt", n))
                dst = take(("ao", n), 1)
                g = h // 4
                done(("ao", n), group(dst[:, 0:128], [(av[0:m, i, g * 128:(g + 1) * 128], probT[0:m, n % 2, i * 128:(i + 1) * 128])
                                                      for i, (a, m) in enumerate(key_tiles(qt))]))

            att_logits(0)
            for n in range(len(ATT) + 3):
                if n + 1 < len(ATT):
                    att_logits(n + 1)
                if 1 <= n <= len(ATT):
                    att_transpose(n - 1)
                if n >= 3:
                    att_values(n - 3)
            for u in range(4):
                tiles_of_unit("gate_b", u, real, SEQ, [("gate_b", u)])
                if u == 0:
                    emptied(pe, ("ao", len(ATT) - 1))
                tiles_of_unit("bd", u, y_dsa, SEQ, [("bd", u)])
            pe.wait_ge(merged_ready, 4)
            for u in range(4):
                tiles_of_unit("wo", u, merged, SEQ, [("wo", u)])
            pe.wait_ge(sq_ready, 15)
            feature_sum("ss_mix", sq, SEQ)
            for u in range(6, 9):
                mod_unit(u)
            pe.wait_ge(sq_ready, 16)
            feature_sum("ss_h1", sq, SEQ)
            for u in range(9, 11):
                mod_unit(u)
            pe.wait_ge(nM_ready, 1)
            for u in range(16):
                tiles_of_unit("up", u, nM, SEQ, [("up", u)])
            pe.wait_ge(sq_ready, 17)
            feature_sum("ss_ctx", sq, CTX)
            pe.wait_ge(up_ready, 16)
            for cp in range(4):
                dst = take(("down", cp))
                for kg in range(4):
                    s, cnt = unit("down", cp * 4 + kg)
                    for j in range(2):
                        for k in range(KT):
                            last = nc.tensor.matmul(dst[:, j * SEQ:(j + 1) * SEQ], by_k(s)[:, k, j * 128:(j + 1) * 128],
                                                    up[:, kg * KT + k, :], start=(kg == 0 and j == 0 and k == 0),
                                                    stop=(kg == 3 and k == KT - 1), skip_group_check=True)
                    last.then_inc(unit_used[s], 1)
                banks.full_when[("down", cp)] = (unit_used[s], cnt)
            pe.wait_ge(lamp_ready, 1)
            dst = take("lam")
            done("lam", nc.tensor.matmul(dst[:, 0:2], ones[0:64, :], lam[0:64, 4:6], start=True, stop=True))
            pe.wait_ge(sq_ready, 18)
            feature_sum("ss_mlp", sq, SEQ)
            for u in range(11, 14):
                mod_unit(u)

            pe.wait_ge(sq_ready, 19)
            feature_sum("ss_x", sq1, SEQ)
            for u in range(14, 16):
                mod_unit(u)
            pe.wait_ge(hcl_ready, 1)
            lat = hcl[:, :, CTX:CTX + SEQ]
            for u in range(4):
                tiles_of_unit("q2", u, lat, SEQ, [("q2", u)])

            def rope2(i):
                emptied(pe, ("q2", i) if i < 4 else ("k2", 2 * (i - 4) + 1))
                src = q2[:, 2 * i:2 * i + 2, :] if i < 4 else k2[:, 2 * (i - 4):2 * (i - 4) + 2, CTX:CTX + SEQ]
                dst = take(("rot2", i))
                done(("rot2", i), nc.tensor.matmul(dst[:, :], cst2("rot_ax"), src, start=True, stop=True))

            pe.wait_ge(c2_loaded, 16)
            for u in range(4):
                tiles_of_unit("k2", u, hcl, 512, [("k2", 2 * u), ("k2", 2 * u + 1)])
                rope2(u)
            for u in range(4):
                s, cnt = unit("v2", u)
                for tp in range(2):
                    dst = take(("v2", u, tp))
                    for j in range(2):
                        a = (2 * tp + j) * 128
                        last = group(dst[:, j * 256:(j + 1) * 256], [(hcl[:, k, a:a + 128], by_k(s)[:, k, :]) for k in range(KT)])
                    if tp == 0:
                        done(("v2", u, 0), last)
                last.then_inc(unit_used[s], 1)
                banks.full_when[("v2", u, 1)] = (unit_used[s], cnt)
                rope2(4 + u)
            for u in range(2):
                tiles_of_unit("f2", u, lat, SEQ, [("f2", u)])

            def scores2(n):
                qt, h = ATT[n]
                for i in range(2):
                    dst = take(("s2", n, i), 2)
                    done(("s2", n, i), nc.tensor.matmul(dst[:, :], q2[64 * i:64 * i + 64, h, qt * 128:(qt + 1) * 128],
                                                        k2[64 * i:64 * i + 64, h, :], start=True, stop=True))

            def transpose2(n):
                pe.wait_ge(prob_ready, len(ATT) + n + 1)
                dst = take(("at2", n))
                for i in range(4):
                    last = nc.tensor.transpose(dst[:, i * 128:(i + 1) * 128], esc[:, n % 2, 0, i * 128:(i + 1) * 128], ident)
                done(("at2", n), last)

            def values2(n):
                qt, h = ATT[n]
                emptied(pe, ("at2", n))
                dst = take(("o2", n))
                done(("o2", n), group(dst[:, 0:128], [(v2[:, i, h * 128:(h + 1) * 128], aT[:, n % 2, i * 128:(i + 1) * 128]) for i in range(4)]))

            dft_d, dft_n = cst2("dft_d"), cst2("dft_n")

            def dft_features(g):
                emptied(pe, ("f2", g // 2))
                dst = take(("z", g))
                for nt in range(2):
                    last = nc.tensor.matmul(dst[:, nt * 256:(nt + 1) * 256], f2[:, g, nt * 128:(nt + 1) * 128], dft_d, start=True, stop=True)
                done(("z", g), last)

            def dft_tokens(g):
                emptied(pe, ("z", g))
                dst = take(("four", g))
                done(("four", g), group(dst[:, 0:SEQ], [(zdft[:, g, nt, p * 128:(p + 1) * 128], dft_n[:, (2 * nt + p) * SEQ:(2 * nt + p + 1) * SEQ])
                                                        for nt in range(2) for p in range(2)]))

            pe.wait_ge(roped2_ready, 8)
            scores2(0)
            for n in range(len(ATT) + 3):
                if n + 1 < len(ATT):
                    scores2(n + 1)
                if n < 2:
                    mod_unit(16 + n)
                if 2 <= n < 6:
                    dft_features(n - 2)
                if 4 <= n < 8:
                    dft_tokens(n - 4)
                if 1 <= n <= len(ATT):
                    transpose2(n - 1)
                if n >= 3:
                    values2(n - 3)
            pe.wait_ge(sq_ready, 20)
            for j in range(4):
                dst = take(("hss", j))
                done(("hss", j), nc.tensor.matmul(dst[:, :], ones, sq1[:, 2 * j:2 * j + 2, :], start=True, stop=True))
            def four_out(u):
                s = four_slot[0]
                w = by_k(s[0], 512)
                dst = take(("fo", u))
                for j in range(2):
                    a = (u % 2) * 256 + j * 128
                    last = group(dst[:, j * SEQ:(j + 1) * SEQ], [(w[:, k, a:a + 128], four[:, k, :]) for k in range(4)])
                if u % 2:
                    last.then_inc(unit_used[s[0]], 1)
                    banks.full_when[("fo", u)] = (unit_used[s[0]], s[1])
                else:
                    done(("fo", u), last)

            four_slot = [None]
            for u in range(4):
                tiles_of_unit("gate2a", u, lat, SEQ, [("gate2a", u)])
                if u == 0:
                    mod_unit(18)
                    mod_unit(19)
                    pe.wait_ge(heads_ready, 1)
                    emptied(pe, ("four", 3))
                tiles_of_unit("ao", u, heads, SEQ, [("ao2", u)])
                tiles_of_unit("gate2f", u, lat, SEQ, [("gate2f", u)])
                if u % 2 == 0:
                    four_slot[0] = unit("fo", u // 2)
                four_out(u)
            pe.wait_ge(merged2_ready, 4)
            for u in range(4):
                tiles_of_unit("wo2", u, merged2, SEQ, [("wo2", u)])
            pe.wait_ge(sq_ready, 21)
            feature_sum("ss_x1", sq2, SEQ)
            for u in range(20, 24):
                mod_unit(u)
            pe.wait_ge(h2_ready, 1)
            pe.wait_ge(wr_loaded, 16)
            dst = take("router")
            for qt in range(2):
                last = group(dst[:, qt * 20:(qt + 1) * 20], [(h2[:, k, qt * 128:(qt + 1) * 128], wr[:, k, :]) for k in range(KT)])
            done("router", last)
            for qt in range(2):
                for i in range(2):
                    dst = take(("ht", qt, i))
                    for j in range(4):
                        last = nc.tensor.transpose(dst[:, j * 128:(j + 1) * 128], h2[:, 4 * i + j, qt * 128:(qt + 1) * 128], ident)
                    done(("ht", qt, i), last)
            pe.wait_ge(routed_ready, 1)
            dst = take("rank")
            m0, m1, earlier = rt[:, 20, 0:N_EXP], rt[:, 21, 0:N_EXP], cst2("earlier")
            group(dst[:, 0:16], [(earlier, m0)])
            group(dst[:, 16:32], [(ones, m0), (earlier, m1)])
            done("rank", group(dst[:, 32:48], [(ones, m0), (ones, m1)]))

            for b in range(8):
                pe.wait_ge(banks.free[b], banks.freed[b])
            pe.wait_ge(zeros_ready, 1)
            acc = psum[4:8]
            for b in range(4):
                nc.tensor.matmul(acc[b][:, :], xg[:, 0, :], xg[:, 4:8, :], start=True, stop=False, skip_group_check=True)

            def expert_pass(pair, n):
                loaded = [16 * (pair + (BASE + 1)), 16 * (pair + 1)]
                pe.wait_ge(pick_ready, n + 1)
                for qt in range(2):
                    last = nc.tensor.transpose(psum[2][:, qt * 128:(qt + 1) * 128], pick_gated[:, qt, :], ident)
                last.then_inc(spread_full, 1)
                for ft in range(KT):
                    last = group(psum[ft // 4][:, (ft % 4) * 2 * CAP:(ft % 4 + 1) * 2 * CAP],
                                 [(h2tok[:, qt, ft * 128:(ft + 1) * 128], pick[:, qt, :]) for qt in range(2)])
                    if ft % 4 == 3:
                        last.then_inc(xg_full[ft // 4], 1)
                pe.wait_ge(spread_ready, n + 1)
                for j in range(2):
                    pe.wait_ge(xg_ready[1 - j], n + 1)
                    x = xg[:, :, j * CAP:(j + 1) * CAP]
                    for q in range(4):
                        pe.wait_ge((unit_loaded, unit_loaded2)[j][q], loaded[j])
                        w = (ring, ring2)[j][:, q, :].rearrange("p (k n) -> p k n", n=UNIT_COLS)
                        for t in range(2):
                            a = (2 * q + t) * CAP
                            last = group(psum[2 + j][:, a:a + CAP], [(w[:, k, t * 128:(t + 1) * 128], x[:, k, :]) for k in range(KT)])
                        last.then_inc((unit_used, unit_used2)[j][q], 1)
                for j in range(2):
                    pe.wait_ge(hid_ready[j], n + 1)
                    for q in range(4, 6):
                        pe.wait_ge((unit_loaded, unit_loaded2)[j][q], loaded[j])
                        w = (ring, ring2)[j][:, q, :].rearrange("p (k n) -> p k n", n=512)
                        for t in range(4):
                            a = ((q - 4) * 4 + t) * CAP
                            last = group(psum[j][:, a:a + CAP], [(w[:, k, t * 128:(t + 1) * 128], hid[:, j, k, :]) for k in range(4)])
                        last.then_inc((unit_used, unit_used2)[j][q], 1)
                pe.wait_ge(ys_ready, 2 * n + 2)
                for ft in range(KT):
                    last = nc.tensor.transpose(psum[2 + ft // 4][:, (ft % 4) * 128:(ft % 4 + 1) * 128], ys[:, ft, :], ident)
                    if ft % 4 == 3:
                        last.then_inc(ysT_full, 1)
                for ft in range(KT):
                    if ft % 4 == 0:
                        pe.wait_ge(ysT_ready, 2 * n + (1 + ft // 4))
                    last = nc.tensor.matmul(acc[ft // 2][:, (ft % 2) * SEQ:(ft % 2 + 1) * SEQ], ysT[:, ft * 128:(ft + 1) * 128], spread[:, :],
                                            start=False, stop=False, skip_group_check=True)
                last.then_inc(scattered, 1)

            assert at[0] == FIRST_EXPERT
            each_pass(pe, expert_pass)
            pe.wait_ge(sq_ready, 22)
            dst = take("ss_out", bank=0)
            done("ss_out", group(dst[:, 0:SEQ], [(ones, sq2[:, k, :]) for k in range(KT)]))

        @block.sync
        def _(sp):
            sp.dma_start(qc[:, :, :], h_in).then_inc(h_loaded, 16)
            sp.dma_start(sm[:, :], sm_in).then_inc(sm_loaded, 16)
            sp.dma_start(c1[:, :], c1_in).then_inc(c1_loaded, 16)
            for s in range(SLOTS):
                sp.dma_start(ring[:, s, :], stream[s]).then_inc(unit_loaded[s], 16)
            with sp.Fori(1, BASE + 1) as i:
                for s in range(SLOTS):
                    sp.wait_ge(unit_used[s], i)
                    sp.dma_start(ring[:, s, :], stream[i * SLOTS + s]).then_inc(unit_loaded[s], 16)
            sp.wait_ge(merged2_ready, 4)
            for s in range(SLOTS):
                sp.dma_start(ring2[:, s, :], stream[(BASE + 1) * SLOTS + s]).then_inc(unit_loaded2[s], 16)
            sp.wait_ge(passes_ready, 1)
            so_far = sp.alloc_register()
            sp.reg_mov(so_far, 0)
            with sp.Fori(1, PAIRS) as pair:
                count = sp.value_load(passes[0:1, bass.ds(pair - 1, 1)], min_val=1, max_val=SEQ // CAP)
                sp.reg_add(so_far, so_far, count)
                n = sp.snap(so_far, min_val=1, max_val=PAIRS * SEQ // CAP)
                for s in range(SLOTS):
                    sp.wait_ge(unit_used[s], n + BASE)
                    sp.dma_start(ring[:, s, :], stream[pair * (2 * SLOTS) + (BASE * SLOTS + s)]).then_inc(unit_loaded[s], 16)
                for s in range(SLOTS):
                    sp.wait_ge(unit_used2[s], n)
                    sp.dma_start(ring2[:, s, :], stream[pair * (2 * SLOTS) + ((BASE + 1) * SLOTS + s)]).then_inc(unit_loaded2[s], 16)
            sp.wait_ge(out_ready, 1)
            sp.dma_start(out, mix2[:, :, :]).then_inc(out_stored, 16)
            sp.wait_ge(out_stored, 16)

        @block.gpsimd
        def _(pool):
            pool.dma_start(ws[:, :], ws_in).then_inc(ws_loaded, 16)
            pool.dma_start(hT[:, :, :], h_in[:, :, META:T]).then_inc(res_loaded, 16)
            pool.dma_start(wr[:, :, :], wr_in).then_inc(wr_loaded, 16)
            pool.dma_start(lam[0:64, 0:4], lam_in).then_inc(lam_loaded, 16)
            emptied(pool, ("GB", H - 1))
            for n, (l, g) in enumerate(LEVEL_ITEMS):
                if n >= 2:
                    pool.wait_ge(*banks.full_when[("P", n - 2)])
                a, _w = C1["levels"]
                m = c1[:, a + 128 * l:a + 128 * (l + 1)]
                if g == 4:
                    nc.gpsimd.tensor_tensor(masked[:, n % 2, 0:128], metas[:, 5, :], m, mul).then_inc(masked_ready, 1)
                else:
                    nc.gpsimd.tensor_tensor(masked[:, n % 2, :].rearrange("p (a b) -> p a b", b=128), low[:, 4 * g:4 * g + 4, :],
                                            m.unsqueeze(1).to_broadcast([128, 4, 128]), mul).then_inc(masked_ready, 1)
            pool.wait_ge(merged_ready, 4)
            pool.dma_start(ctxT[:, :, :], ctx_in).then_inc(ctx_loaded, 16)
            pool.dma_start(c2[:, :], c2_in).then_inc(c2_loaded, 16)

        @block.scalar
        def _(act):
            step = Steps(act, act_step)
            A = nc.scalar.activation

            def evac(name, dst, width, scale=1.0):
                src = full(act, name)[0:dst.shape[0], 0:width]
                if len(dst.shape) == 3:
                    src = src.rearrange("p (a b) -> p a b", b=dst.shape[2])
                A(dst, src, ACT.Copy, scale=scale).then_inc(free(name), 1)

            def evac_mod(u):
                evac(("mod", u), modT[:, 2 * u:2 * u + 2, :], 4)

            def rms_root(name, n, dst, width=D):
                A(dst, full(act, name)[:, 0:n], ACT.Sqrt, bias=eps, scale=1.0 / width).then_inc(free(name), 1)

            act.wait_ge(sm_loaded, 16)
            A(a1[:, :, :], small("c").rearrange("p (k n) -> p k n", n=2), ACT.Sigmoid).then_inc(sig_ready, 1)
            act.wait_ge(h_loaded, 16)
            A(vc[:, :, :], qc[:, :, :], ACT.Square).then_inc(sq_ready, 1)
            act.wait_ge(c1_loaded, 16)
            rms_root("ss_in", T, root[:, :])
            bank = full(act, "gba")
            A(tok[:, 0, :].rearrange("p (g n) -> p g n", n=8), bank[:, 0:48].rearrange("p (g n) -> p g n", n=16)[:, :, 0:8],
              ACT.Sigmoid).then_inc(free("gba"), 1)
            for t in range(24):
                kind, j = CONV_TILES[t]
                emptied(act, (kind, j))
                if t >= 2:
                    act.wait_ge(silu_ready, t)
                A(scr[:, t % 2, 0:T], conv_dst(t), ACT.Sigmoid).then_inc(sig_ready, 1)
            act.wait_ge(silu_ready, 25)
            for i in range(13):
                if i < 12:
                    n = T if i < 8 else 512
                    src = kc[:, i, :] if i < 8 else qc[:, 2 * (i - 8):2 * (i - 8) + 2, META:T]
                    dst = scr[:, i % 2, 0:n]
                    if i >= 2:
                        act.wait_ge(*banks.full_when[("l2", i - 2)])
                    A(dst if i < 8 else dst.rearrange("p (a b) -> p a b", b=SEQ), src, ACT.Square).then_inc(sq_ready, 1)
                if i >= 1:
                    j = i - 1
                    n = T if j < 8 else 512
                    if j >= 2:
                        act.wait_ge(normed_ready, j - 1)
                    A(scr[:, j % 2, 512:512 + n], full(act, ("l2", j))[:, 0:n], ACT.Sqrt, bias=eps).then_inc(free(("l2", j)), 1)
            for u in range(4):
                evac_mod(u)
            act.wait_ge(absx_ready, 1)
            step(A(tok[:, 2, :], tok[:, 2, :], ACT.Exp, scale=-1.0))
            step(A(tok[:, 7, 0:8], small("a_log"), ACT.Exp))
            step.settle()
            A(tok[:, 2, :], tok[:, 2, :], ACT.Ln, bias=1.0).then_inc(softplus_ready, 1)
            A(tok[:, 5, 0:16], full(act, "gct")[:, 0:16], ACT.Exp).then_inc(free("gct"), 1)
            act.wait_ge(meta_arg_ready, 1)
            A(metas[:, 4, :], metas[:, 4, :], ACT.Exp).then_inc(meta_exp_ready, 1)
            for h in range(H + 1):
                if h < H:
                    act.wait_ge(decay_arg_ready, h + 1)
                    A(scr[:, h % 2, 256:512], full(act, ("GB", h))[:, 0:256], ACT.Exp).then_inc(free(("GB", h)), 1)
                    A(scr[:, h % 2, 0:256], scr[:, h % 2, 0:256], ACT.Exp).then_inc(decay_exp_ready, 1)
                if h >= 1:
                    g = h - 1
                    emptied(act, ("KQ", g))
                    bank = full(act, ("TR", g))
                    for ci in range(NCH):
                        sy = g * NCH + ci
                        step(A(k_tail[:, sy, :], bank[:, ci * 128:(ci + 1) * 128], ACT.Copy, scale=scr[:, g % 2, ci * 128 + 127:ci * 128 + 128]))
                        ins = A(v_beta[:, sy, :], bank[:, 256 + ci * 128:384 + ci * 128], ACT.Copy, scale=tok[:, 0, 8 + 8 * ci + g:9 + 8 * ci + g])
                        if ci == NCH - 1:
                            ins.then_inc(free(("TR", g)), 1)
            for n, (l, g) in enumerate(LEVEL_ITEMS):
                w = 512 if g < 4 else 128
                if n >= 2:
                    act.wait_ge(*banks.full_when[("QT", n - 2)])
                    if LEVEL_ITEMS[n - 2][0] == 0:
                        emptied(act, ("QT", n - 2))
                evac(("P", n), prod[:, n % 2, 0:w], w)
                if n == len(LEVEL_ITEMS) - 1:
                    evac_mod(4)
            evac_mod(5)
            evac("meta_v", metas[:, 3, :], 128)
            for hg in range(2):
                evac(("S0", hg), state[:, 0, hg * 512:(hg + 1) * 512], 512)
            for ci in range(NCH):
                for hg in range(2):
                    evac(("vn", ci, hg), scr[:, hg, 512:1024], 512)
                for hg in range(2):
                    evac(("o", ci, hg), y_gdn[:, hg * 4:hg * 4 + 4, ci * 128:(ci + 1) * 128], 512)
            for u in range(4):
                A(inv[:, 4 * u:4 * u + 4, :], full(act, ("gz", u))[:, :].rearrange("p (a b) -> p a b", b=128), ACT.Sigmoid).then_inc(sig_ready, 1)
                act.wait_ge(sig_ready, 26 + u)
                A(k_tail[:, 4 * u:4 * u + 4, :], full(act, ("gz", u))[:, :].rearrange("p (a b) -> p a b", b=128), ACT.Copy).then_inc(free(("gz", u)), 1)
            emptied(act, ("o", NCH - 1, 1))
            A(low[:, :, :], y_gdn[:, :, :].rearrange("p h (c s) -> p (h c) s", s=128), ACT.Square).then_inc(sq_ready, 1)
            for j in range(4):
                rms_root(("yss", j), 512, attn[:, 4 * j:4 * j + 4, :].rearrange("p a b -> p (a b)"), 128)
            act.wait_ge(y_ready, 1)
            for u in range(4):
                evac(("aq", u), aq[:, 2 * u:2 * u + 2, :], 512)
            for j in range(2):
                evac(("ak", j), ak[:, j, :], T)
            for g, m in enumerate((128, 128, META)):
                evac(("av", g), av[0:m, g, :], 256)
            for u in range(2):
                evac(("iq", u), iq[:, 2 * u:2 * u + 2, :], 512)
            evac("ik", ik[:, :], T)
            evac("iw", iw[:, :, :], 16, float(H * 64) ** -0.5)
            for n, (qt, h) in enumerate(ATT):
                if n >= 2:
                    act.wait_ge(score_ready, n - 1)
                A(relu[:, n % 2, 0:nkeys(qt)], full(act, ("ix", qt, h))[:, 0:nkeys(qt)], ACT.Relu).then_inc(free(("ix", qt, h)), 1)
            for u in range(4):
                if u >= 2:
                    emptied(act, ("bg", u - 2))
                A(gate[:, u % 2, :], full(act, ("gate_a", u))[:, :], ACT.Sigmoid).then_inc(free(("gate_a", u)), 1)
            for n in range(len(ATT) + 4):
                if n < len(ATT):
                    qt, h = ATT[n]
                    act.wait_ge(nmax_ready, n + 1)
                    if n >= 2:
                        act.wait_ge(*banks.full_when[("pt", n - 2)])
                    A(prob[:, n % 2, 0:nkeys(qt)], lmask[:, n % 2, 0:nkeys(qt)], ACT.Exp, bias=stat[:, n % 2, 0:1],
                      accum_out=stat[:, n % 2, 1:2]).then_inc(pexp_ready, 1)
                if 2 <= n < len(ATT) + 2:
                    k = n - 2
                    qt, h = ATT[k]
                    bank = full(act, ("pt", k))
                    if k >= 2:
                        act.wait_ge(*banks.full_when[("ao", k - 2)])
                    nt = len(key_tiles(qt)) - 1
                    step(A(probT[:, k % 2, 0:nt * 128], bank[:, 0:nt * 128], ACT.Copy))
                    A(probT[0:META, k % 2, nt * 128:(nt + 1) * 128], bank[0:META, nt * 128:(nt + 1) * 128], ACT.Copy).then_inc(free(("pt", k)), 1)
                if n >= 4:
                    qt, h = ATT[n - 4]
                    evac(("ao", n - 4), y_dsa[:, h, qt * 128:(qt + 1) * 128], 128)
            for u in range(4):
                if u >= 2:
                    emptied(act, ("bd", u - 2))
                A(gate[:, u % 2, :], full(act, ("gate_b", u))[:, :], ACT.Sigmoid).then_inc(free(("gate_b", u)), 1)
            for u in range(4):
                bank = full(act, ("wo", u))[:, :].rearrange("p (a b) -> p a b", b=SEQ)
                ins = A(sq[:, 2 * u:2 * u + 2, :], bank, ACT.Square)
                if u == 3:
                    ins.then_inc(sq_ready, 1)
                evac(("wo", u), mix[:, 2 * u:2 * u + 2, :], 512)
            rms_root("ss_mix", SEQ, root[:, 0:SEQ])
            for u in range(6, 9):
                evac_mod(u)
            act.wait_ge(h1_ready, 1)
            A(sq[:, :, :], hT[:, :, :], ACT.Square).then_inc(sq_ready, 1)
            rms_root("ss_h1", SEQ, root[:, 0:SEQ])
            for u in range(9, 11):
                evac_mod(u)
            for u in range(16):
                A(up[:, 2 * u:2 * u + 2, :], full(act, ("up", u))[:, :].rearrange("p (a b) -> p a b", b=SEQ), ACT.Relu).then_inc(free(("up", u)), 1)
            act.wait_ge(ctx_loaded, 16)
            act.wait_ge(nM_ready, 1)
            A(sq[:, :, :], ctxT[:, :, :], ACT.Square).then_inc(sq_ready, 1)
            rms_root("ss_ctx", CTX, root[:, 0:CTX])
            for cp in range(4):
                bank = full(act, ("down", cp))[:, :].rearrange("p (a b) -> p a b", b=SEQ)
                ins = A(sq[:, 2 * cp:2 * cp + 2, :], bank, ACT.Square)
                if cp == 3:
                    ins.then_inc(sq_ready, 1)
                evac(("down", cp), mix[:, 2 * cp:2 * cp + 2, :], 512)
            A(lam[:, 6:8], full(act, "lam")[:, 0:2], ACT.Exp).then_inc(free("lam"), 1)
            act.wait_ge(h1_ready, 2)
            rms_root("ss_mlp", SEQ, root[:, 0:SEQ])
            for u in range(11, 14):
                evac_mod(u)

            act.wait_ge(h1_ready, 3)
            A(sq1[:, :, :], hT[:, :, :], ACT.Square).then_inc(sq_ready, 1)
            rms_root("ss_x", SEQ, root[:, 0:SEQ])
            for u in range(14, 16):
                evac_mod(u)
            for u in range(4):
                evac(("q2", u), q2[:, 2 * u:2 * u + 2, :], 512)
            for u in range(4):
                evac(("k2", 2 * u), k2[:, 2 * u, :], 512)
                evac(("k2", 2 * u + 1), k2[:, 2 * u + 1, :], 512)
            for u in range(4):
                for tp in range(2):
                    evac(("v2", u, tp), v2[:, 2 * tp:2 * tp + 2, u * 256:(u + 1) * 256], 512)
            for u in range(2):
                evac(("f2", u), f2[:, 2 * u:2 * u + 2, :], 512)
            for n in range(len(ATT) + 4):
                if n < len(ATT):
                    act.wait_ge(nmax_ready, len(ATT) + n + 1)
                    if n >= 2:
                        act.wait_ge(*banks.full_when[("at2", n - 2)])
                    for i in range(2):
                        A(esc[:, n % 2, i, :], full(act, ("s2", n, i))[:, :], ACT.Exp, bias=stat2[:, n % 2, 2 + i:3 + i], scale=0.125,
                          accum_out=stat2[:, n % 2, 4 + i:5 + i]).then_inc(free(("s2", n, i)), 1)
                if n < 2:
                    evac_mod(16 + n)
                if 2 <= n < 6:
                    evac(("z", n - 2), zdft[:, n - 2, :, :], 512)
                if 4 <= n < 8:
                    evac(("four", n - 4), four[:, n - 4, :], SEQ)
                if 2 <= n < len(ATT) + 2:
                    k = n - 2
                    if k >= 2:
                        act.wait_ge(*banks.full_when[("o2", k - 2)])
                    evac(("at2", k), aT[:, k % 2, :], 512)
                if n >= 4:
                    qt, h = ATT[n - 4]
                    evac(("o2", n - 4), heads[:, h, qt * 128:(qt + 1) * 128], 128)
            emptied(act, ("o2", len(ATT) - 1))
            A(sq1[:, :, :], heads[:, :, :], ACT.Square).then_inc(sq_ready, 1)
            for j in range(4):
                rms_root(("hss", j), 512, q2[:, 2 * j:2 * j + 2, :].rearrange("p a b -> p (a b)"), 128)
            for u in range(4):
                if u >= 1:
                    act.wait_ge(merged2_ready, u)
                A(gate2[:, 0, :], full(act, ("gate2a", u))[:, :], ACT.Sigmoid).then_inc(free(("gate2a", u)), 1)
                if u == 0:
                    evac_mod(18)
                    evac_mod(19)
                A(gate2[:, 1, :], full(act, ("gate2f", u))[:, :], ACT.Sigmoid).then_inc(free(("gate2f", u)), 1)
            emptied(act, ("wo2", 3))
            A(sq2[:, :, :], hT[:, :, :], ACT.Square).then_inc(sq_ready, 1)
            rms_root("ss_x1", SEQ, root[:, 0:SEQ])
            for u in range(20, 24):
                evac_mod(u)
            act.wait_ge(rexp_arg_ready, 1)
            A(rflat(80, 8), rflat(80, 8), ACT.Exp).then_inc(rexp_ready, 1)
            act.wait_ge(rexp_arg_ready, 2)
            A(rflat(180, 2), rflat(180, 2), ACT.Exp).then_inc(rexp_ready, 1)
            for qt in range(2):
                for i in range(2):
                    evac(("ht", qt, i), h2tok[:, qt, i * 512:(i + 1) * 512], 512)

            def expert_pass(pair, n):
                act.wait_ge(spread_full, n + 1)
                A(spread[:, :], psum[2][:, 0:SEQ], ACT.Copy).then_inc(spread_ready, 1)
                for j in range(2):
                    act.wait_ge(xg_full[j], n + 1)
                    A(xg[:, 4 * j:4 * j + 4, :], psum[j][:, :].rearrange("p (a b) -> p a b", b=2 * CAP), ACT.Copy).then_inc(xg_ready[j], 1)
                for j in range(2):
                    act.wait_ge((unit_used, unit_used2)[j][3], n + ((BASE + 1) if j == 0 else 1))
                    A(sg[:, j, :], psum[2 + j][:, 0:4 * CAP], ACT.Sigmoid).then_inc(sig_w1_ready[j], 1)
                for j in range(2):
                    act.wait_ge((unit_used, unit_used2)[j][5], n + ((BASE + 1) if j == 0 else 1))
                    A(ys[:, :, j * CAP:(j + 1) * CAP], psum[j][:, :].rearrange("p (a b) -> p a b", b=CAP), ACT.Copy).then_inc(ys_ready, 1)
                for i in range(2):
                    act.wait_ge(ysT_full, 2 * n + (1 + i))
                    A(ysT[:, i * 512:(i + 1) * 512], psum[2 + i][:, :], ACT.Copy).then_inc(ysT_ready, 1)

            each_pass(act, expert_pass)
            act.wait_ge(h1_ready, 4)
            A(sq2[:, :, :], hT[:, :, :], ACT.Square).then_inc(sq_ready, 1)
            rms_root("ss_out", SEQ, root[:, 0:SEQ])

        @block.vector
        def _(dve):
            step = Steps(dve, dve_step)
            TT, TS, STT, CP = nc.vector.tensor_tensor, nc.vector.tensor_scalar, nc.vector.scalar_tensor_tensor, nc.vector.tensor_copy

            def split(ap, b):
                return ap.rearrange("p (a b) -> p a b", b=b)

            def over(ap, n):
                return ap.unsqueeze(1).to_broadcast([ap.shape[0], n, ap.shape[1]])

            def each(ap, n):
                return ap.unsqueeze(2).to_broadcast([ap.shape[0], ap.shape[1], n])

            def inv_rms(name, n):
                emptied(dve, name)
                step(nc.vector.reciprocal(rB[:, 0:n], root[:, 0:n]))
                step.settle()

            def scaled(dst, src, gains, n, last_sem=None):
                for k in range(KT):
                    ins = STT(dst[:, k, :], src[:, k, :], gains[:, k:k + 1], rB[:, 0:n], mul, mul)
                    if k == KT - 1 and last_sem is not None:
                        ins.then_inc(last_sem, 1)
                    else:
                        step(ins)

            dve.wait_ge(sm_loaded, 16)
            dve.wait_ge(sig_ready, 1)
            TT(silu_c[:, :, :], small("c").rearrange("p (k n) -> p k n", n=2), a1[:, :, :], mul).then_inc(silu_ready, 1)
            inv_rms("ss_in", T)
            scaled(nT, qc, small("g_pre_mix"), T, nT_ready)
            emptied(dve, "gba", 1)
            bank = psum[banks.at["gba"]]
            TT(tok[:, 1, :].rearrange("p (g n) -> p g n", n=8), bank[:, 0:48].rearrange("p (g n) -> p g n", n=16)[:, :, 8:16],
               over(small("dt_bias"), 3), add).then_inc(free("gba"), 1)
            emptied(dve, "gba")
            step(TS(tok[:, 3, :], tok[:, 1, :], -1.0, None, mul))
            step.settle()
            TT(tok[:, 2, :], tok[:, 1, :], tok[:, 3, :], ALU.max).then_inc(absx_ready, 1)

            def silu(t):
                dve.wait_ge(sig_ready, t + 2)
                TT(conv_dst(t), conv_dst(t), scr[:, t % 2, 0:T], mul).then_inc(silu_ready, 1)

            for t in range(24):
                kind, j = CONV_TILES[t]
                bank = full(dve, (kind, j))
                dst = conv_dst(t)
                a = SM["conv"][0] + 4 * ({"gq": 0, "gk": 8, "gv": 16}[kind] + j)
                step(TS(dst, bank[:, 0:T], sm[:, a + 3:a + 4], None, mul))
                for back in (1, 2, 3):
                    step.settle()
                    ins = STT(dst[:, back:T], bank[:, 0:T - back], sm[:, a + 3 - back:a + 4 - back], dst[:, back:T], mul, add)
                    if back < 3:
                        step(ins)
                    else:
                        ins.then_inc(free((kind, j)), 1)
                if t >= 1:
                    silu(t - 1)
            silu(23)
            for i in range(12):
                n = T if i < 8 else 512
                emptied(dve, ("l2", i))
                r = scr[:, i % 2, 512:512 + n]
                step(nc.vector.reciprocal(r, r))
                step.settle()
                if i < 8:
                    TT(kc[:, i, :], kc[:, i, :], r, mul).then_inc(normed_ready, 1)
                else:
                    q = qc[:, 2 * (i - 8):2 * (i - 8) + 2, META:T]
                    STT(q, q, 128.0 ** -0.5, split(r, SEQ), mul, mul).then_inc(normed_ready, 1)
            dve.wait_ge(softplus_ready, 1)
            step(STT(tok[:, 4, :], tok[:, 1, :], 0.0, tok[:, 2, :], ALU.max, add))
            step.settle()
            step(STT(split(tok[:, 3, :], 8), split(tok[:, 4, :], 8), -1.0, over(tok[:, 7, 0:8], 3), mul, mul))
            step.settle()
            dve.wait_ge(normed_ready, 12)
            for ci in range(NCH):
                a = 8 * (1 + ci)
                step(CP(inv[:, :, :].rearrange("p (h c) m -> p c h m", c=NCH)[:, ci], each(tok[:, 3, a:a + 8], 128)))
                step(CP(invT[:, :, :].rearrange("p (h c) m -> p c h m", c=NCH)[:, ci], each(tok[:, 0, a:a + 8], 128)))
            step(TT(split(metas[0:META, 0, :], META), each(tok[0:META, 3, 0:8], META), over(upper[0:META, 0:META], 8), mul))
            step(TT(split(metas[0:META, 1, :], META), each(tok[0:META, 0, 0:8], META), over(ident[0:META, 0:META], 8), mul))
            step(CP(split(metas[:, 2, :], META), kc[:, :, 0:META]))
            CP(split(metas[:, 3, :], META), vc[:, :, 0:META]).then_inc(tri_ready, 1)
            emptied(dve, "gct", 1)
            TS(tok[:, 6, 0:16], psum[banks.at["gct"]][:, 0:16], -1.0, None, mul).then_inc(free("gct"), 1)
            emptied(dve, "gct")
            step(STT(tok[:, 7, 8:24], tok[:, 5, 0:16], -1.0, tok[:, 0, 8:24], mul, mul))
            bank = full(dve, "metaGB")
            step(STT(metas[:, 5, :], bank[:, 0:128], 1.0, ident, mul, mul, accum_out=mcol[:, 0:1]))
            step(STT(metas[:, 6, :], bank[:, 128:256], 1.0, ident, mul, mul, accum_out=mcol[:, 1:2]))
            step.settle()
            TS(metas[:, 4, :], bank[:, 0:128], mcol[:, 0:1], 0.0, sub, ALU.min).then_inc(meta_arg_ready, 1)
            dve.wait_ge(meta_exp_ready, 1)
            step(TT(metas[:, 4, :], metas[:, 4, :], cst("meta_upper"), mul))
            step.settle()
            kbank = full(dve, "metaK")
            step(STT(metas[:, 6, :], metas[:, 4, :], 1.0, cst("meta_last"), mul, mul, accum_out=mcol[:, 2:3]))
            step(TT(metas[:, 5, :], kbank[:, 0:128], metas[:, 4, :], mul))
            step.settle()
            TT(metas[:, 5, :], metas[:, 5, :], bank[:, 128:256], mul).then_inc(free("metaGB"), 1)
            step(TS(metas[:, 6, :], kbank[:, 128:256], mcol[:, 2:3], None, mul))
            TS(metas[:, 7, :], kbank[:, 256:384], mcol[:, 1:2], None, mul).then_inc(free("metaK"), 1)

            def decay_args(h):
                if h >= 2:
                    emptied(dve, ("TR", h - 2))
                bank = full(dve, ("GB", h))
                for ci in range(NCH):
                    ins = TS(scr[:, h % 2, ci * 128:(ci + 1) * 128], bank[:, ci * 128:(ci + 1) * 128],
                             tok[:, 6, 8 * ci + h:8 * ci + h + 1], 0.0, add, ALU.min)
                    if ci == NCH - 1:
                        ins.then_inc(decay_arg_ready, 1)
                    else:
                        step(ins)

            def decay_use(h):
                dve.wait_ge(decay_exp_ready, h + 1)
                dt = scr[:, h % 2, 0:256]
                step(TT(split(dt, 128), split(dt, 128), over(upper, 2), mul))
                step(CP(egl[:, 2 * h:2 * h + 2], split(scr[:, h % 2, 256:512], 128)[:, :, 127]))
                step.settle()
                bank = full(dve, ("KQ", h))
                step(TT(attn[:, 2 * h:2 * h + 2, :], split(bank[:, 256:512], 128), split(dt, 128), mul))
                TT(low[:, 2 * h:2 * h + 2, :], split(bank[:, 0:256], 128), split(dt, 128), mul).then_inc(free(("KQ", h)), 1)
                step(TT(qc[:, h, META:T], qc[:, h, META:T], scr[:, h % 2, 256:512], mul))
                emptied(dve, ("KQ", h))
                TT(low[:, 2 * h:2 * h + 2, :], low[:, 2 * h:2 * h + 2, :], split(full(dve, ("GB", h))[:, 256:512], 128), mul).then_inc(free(("GB", h)), 1)

            for h in range(H + 1):
                if h < H:
                    decay_args(h)
                if h >= 1:
                    decay_use(h - 1)
            emptied(dve, ("TR", H - 1))
            TT(split(scr[:, 0, :], 128), over(metas[:, 6, :], H), each(cst("head_rows"), 128), mul).then_inc(scan_ready, 1)

            def update_inverse(n):
                l, g = LEVEL_ITEMS[n]
                x = metas[:, 8:9, :] if g == 4 else inv[:, 4 * g:4 * g + 4, :]
                xt = metas[:, 9:10, :] if g == 4 else invT[:, 4 * g:4 * g + 4, :]
                w = 1 if g == 4 else 4
                if l == 0:
                    emptied(dve, ("P", n))
                    step(TT(x, over(ident, w), split(prod[:, n % 2, 0:w * 128], 128), sub))
                    TT(xt, over(ident, w), split(full(dve, ("QT", n))[:, 0:w * 128], 128), sub).then_inc(free(("QT", n)), 1)
                    return
                if ("Q", n) in banks.at:
                    TT(x, x, split(full(dve, ("Q", n))[:, 0:w * 128], 128), sub).then_inc(free(("Q", n)), 1)
                TT(xt, xt, split(full(dve, ("QT", n))[:, 0:w * 128], 128), sub).then_inc(free(("QT", n)), 1)

            for n in range(len(LEVEL_ITEMS)):
                update_inverse(n)
            for ci in range(NCH):
                for hg in range(2):
                    bank = full(dve, ("kS", ci, hg))
                    for j in range(4):
                        h = hg * 4 + j
                        ins = STT(scr[:, hg, j * 128:(j + 1) * 128], bank[:, j * 128:(j + 1) * 128], tok[:, 7, 8 + 8 * ci + h:9 + 8 * ci + h],
                                  v_beta[:, h * NCH + ci, :], mul, add)
                        if j == 3:
                            ins.then_inc(free(("kS", ci, hg)), 1)
                if ci + 1 < NCH:
                    for hg in range(2):
                        bank = full(dve, ("dS", ci, hg))
                        for j in range(4):
                            h = hg * 4 + j
                            sy = h * NCH + ci
                            ins = STT(state[:, ci + 1, h * 128:(h + 1) * 128], state[:, ci, h * 128:(h + 1) * 128], egl[:, sy:sy + 1],
                                      bank[:, j * 128:(j + 1) * 128], mul, add)
                            if j == 3:
                                ins.then_inc(free(("dS", ci, hg)), 1)
            for u in range(4):
                emptied(dve, ("gz", u))
                step(TT(inv[:, 4 * u:4 * u + 4, :], inv[:, 4 * u:4 * u + 4, :], k_tail[:, 4 * u:4 * u + 4, :], mul))
            for j in range(4):
                emptied(dve, ("yss", j))
                r = attn[:, 4 * j:4 * j + 4, :].rearrange("p a b -> p (a b)")
                yj = y_gdn[:, 2 * j:2 * j + 2, :].rearrange("p a b -> p (a b)")
                step(nc.vector.reciprocal(r, r))
                step.settle()
                step(STT(yj, yj, small("gdn_norm"), r, mul, mul))
                step.settle()
                ins = TT(yj, yj, inv[:, 4 * j:4 * j + 4, :].rearrange("p a b -> p (a b)"), mul)
                if j == 3:
                    ins.then_inc(y_ready, 1)
                else:
                    step(ins)
            for i, (kind, j) in enumerate(ROPES):
                bank = full(dve, ("rot", i))
                raw, _n = raw_of(kind, j)
                w, n = (2, SEQ) if kind in ("aq", "iq") else (1, T)
                tab = "att" if kind in ("aq", "ak") else "idx"
                if i:
                    dve.wait_ge(roped_ready, i)
                cos, sin = cst("cos_" + tab)[:, T - n:T], cst("sin_" + tab)[:, T - n:T]
                TT(split(rot1[:, 0:w * n], n), split(bank[:, 0:w * n], n), over(sin, w), mul).then_inc(free(("rot", i)), 1)
                step(TT(split(rot2[:, 0:w * n], n), raw, over(cos, w), mul))
                step.settle()
                emptied(dve, ("rot", i))
                TT(raw, split(rot1[:, 0:w * n], n), split(rot2[:, 0:w * n], n), add).then_inc(roped_ready, 1)
            emptied(dve, "iw")
            for n, (qt, h) in enumerate(ATT):
                emptied(dve, ("ix", qt, h))
                sc = score[:, qt, 0:nkeys(qt)]
                if h == 0:
                    TS(sc, relu[:, n % 2, 0:nkeys(qt)], iw[:, qt, h:h + 1], None, mul).then_inc(score_ready, 1)
                else:
                    dve.wait_ge(score_ready, n)
                    STT(sc, relu[:, n % 2, 0:nkeys(qt)], iw[:, qt, h:h + 1], sc, mul, add).then_inc(score_ready, 1)
            dve.wait_ge(score_ready, len(ATT))

            def choose(qt):
                n = nkeys(qt)
                causal = cst("causal")[:, qt * T:qt * T + n]
                step(TT(work[:, 0, 0:n], score[:, qt, 0:n], causal, add))
                for i in range(TOPK // 8):
                    step.settle()
                    step(nc.vector.max(best[:, :], work[:, i % 2, 0:n]))
                    step.settle()
                    step(nc.vector.match_replace(work[:, (i + 1) % 2, 0:n], best[:, :], work[:, i % 2, 0:n], TAKEN))
                step(TS(lmask[:, 0, 0:n], causal, 0.0, None, ALU.is_equal))
                step.settle()
                step(STT(lmask[:, 1, 0:n], work[:, (TOPK // 8) % 2, 0:n], (NEG + TAKEN) / 2, lmask[:, 0, 0:n], ALU.is_le, mul))
                step.settle()
                step(TS(bias[:, qt, 0:n], lmask[:, 1, 0:n], 1.0, 1.0e30, sub, mul))

            def merge_a(u):
                emptied(dve, ("gate_a", u))
                TT(merged[:, 2 * u:2 * u + 2, :], split(gate[:, u % 2, :], SEQ), split(full(dve, ("bg", u))[:, :], SEQ), mul).then_inc(free(("bg", u)), 1)

            choose(0)
            merge_a(0)
            merge_a(1)
            choose(1)
            merge_a(2)
            merge_a(3)
            step.settle()
            for n in range(len(ATT) + 1):
                if n < len(ATT):
                    qt, h = ATT[n]
                    w = nkeys(qt)
                    if n >= 2:
                        dve.wait_ge(pexp_ready, n - 1)
                    STT(lmask[:, n % 2, 0:w], full(dve, ("lg", n))[:, 0:w], 128.0 ** -0.5, bias[:, qt, 0:w], mul, add).then_inc(free(("lg", n)), 1)
                    emptied(dve, ("lg", n))
                    nc.vector.tensor_reduce(stat[:, n % 2, 0:1], lmask[:, n % 2, 0:w], AX, ALU.max, negate=True).then_inc(nmax_ready, 1)
                if n >= 1:
                    k = n - 1
                    w = nkeys(ATT[k][0])
                    dve.wait_ge(pexp_ready, k + 1)
                    step(nc.vector.reciprocal(stat[:, k % 2, 2:3], stat[:, k % 2, 1:2]))
                    step.settle()
                    TS(prob[:, k % 2, 0:w], prob[:, k % 2, 0:w], stat[:, k % 2, 2:3], None, mul).then_inc(prob_ready, 1)
            for u in range(4):
                emptied(dve, ("gate_b", u))
                gated = (rot1, rot2)[u % 2]
                TT(gated[:, :], gate[:, u % 2, :], full(dve, ("bd", u))[:, :], mul).then_inc(free(("bd", u)), 1)
                emptied(dve, ("bd", u))
                TT(merged[:, 2 * u:2 * u + 2, :], merged[:, 2 * u:2 * u + 2, :], split(gated[:, :], SEQ), add).then_inc(merged_ready, 1)
            dve.wait_ge(res_loaded, 16)
            inv_rms("ss_mix", SEQ)
            scaled(mix, mix, small("g_post_mix"), SEQ)
            step.settle()
            TT(hT[:, :, :], hT[:, :, :], mix[:, :, :], add).then_inc(h1_ready, 1)
            inv_rms("ss_h1", SEQ)
            dve.wait_ge(h1_ready, 1)
            scaled(nM, hT, small("g_pre_mlp"), SEQ, nM_ready)
            dve.wait_ge(lam_loaded, 16)
            step(TT(lam[0:64, 4:5], lam[0:64, 0:1], lam[0:64, 1:2], mul))
            TT(lam[0:64, 5:6], lam[0:64, 2:3], lam[0:64, 3:4], mul).then_inc(lamp_ready, 1)
            for u in range(16):
                emptied(dve, ("up", u))
                v = up[:, 2 * u:2 * u + 2, :]
                TT(v, v, v, mul).then_inc(up_ready, 1)
            inv_rms("ss_ctx", CTX)
            dve.wait_ge(ctx_loaded, 16)
            TT(ctxT[:, :, :], ctxT[:, :, :], over(rB[:, 0:CTX], KT), mul).then_inc(h1_ready, 1)
            inv_rms("ss_mlp", SEQ)
            emptied(dve, ("down", 3))
            scaled(mix, mix, small("g_post_mlp"), SEQ)
            step.settle()
            TT(hT[:, :, :], hT[:, :, :], mix[:, :, :], add).then_inc(h1_ready, 1)

            def mod_bias(a, b):
                emptied(dve, ("mod", b // 2 - 1))
                step(TT(modT[:, a:b, :], modT[:, a:b, :], each(small("b_mod")[:, a:b], 2), add))

            mod_bias(0, 16)
            emptied(dve, "lam")
            step(TT(lam[:, 4:5], lam[:, 7:8], lam[:, 6:7], sub))
            step(TS(small("subln"), small("subln"), 1.0 - LAM_INIT, None, mul))
            step.settle()
            step(TS(lam[:, 5:6], lam[:, 4:5], -LAM_INIT, None, add))
            step(STT(a1[:, :, :], modT[:, 8:16, :], 1.0, each(small("g_n1"), 2), add, mul))
            step.settle()
            for k in range(KT):
                step(TS(hcl[:, k, 0:CTX], ctxT[:, k, :], a1[:, k, 1:2], modT[:, k, 1:2], mul, add))
            inv_rms("ss_x", SEQ)
            for k in range(KT):
                step(STT(hcl[:, k, CTX:CTX + SEQ], hT[:, k, :], a1[:, k, 0:1], rB[:, 0:SEQ], mul, mul))
            step.settle()
            for k in range(KT):
                ins = TS(hcl[:, k, CTX:CTX + SEQ], hcl[:, k, CTX:CTX + SEQ], modT[:, k, 0:1], None, add)
                if k == KT - 1:
                    ins.then_inc(hcl_ready, 1)
                else:
                    step(ins)
            dve.wait_ge(c2_loaded, 16)
            for i in range(8):
                bank = full(dve, ("rot2", i))
                raw = q2[:, 2 * i:2 * i + 2, :] if i < 4 else k2[:, 2 * (i - 4):2 * (i - 4) + 2, CTX:CTX + SEQ]
                if i:
                    dve.wait_ge(roped2_ready, i)
                TT(split(rot3[:, 0, :], SEQ), split(bank[:, :], SEQ), over(cst2("sin_ax"), 2), mul).then_inc(free(("rot2", i)), 1)
                step(TT(split(rot3[:, 1, :], SEQ), raw, over(cst2("cos_ax"), 2), mul))
                step.settle()
                emptied(dve, ("rot2", i))
                TT(raw, split(rot3[:, 0, :], SEQ), split(rot3[:, 1, :], SEQ), add).then_inc(roped2_ready, 1)
            for n in range(len(ATT) + 1):
                if n < len(ATT):
                    st = stat2[:, n % 2, :]
                    for i in range(2):
                        nc.vector.tensor_reduce(st[:, i:i + 1], full(dve, ("s2", n, i))[:, :], AX, ALU.max, negate=True).then_inc(free(("s2", n, i)), 1)
                    dve.wait_ge(banks.free[banks.at[("s2", n, 1)]], banks.free_when[("s2", n, 1)] - 1)
                    TS(st[:, 2:4], st[:, 0:2], 0.125, None, mul).then_inc(nmax_ready, 1)
                if n >= 1:
                    k = n - 1
                    st = stat2[:, k % 2, :]
                    emptied(dve, ("s2", k, 0))
                    emptied(dve, ("s2", k, 1))
                    step(nc.vector.reciprocal(st[:, 6:8], st[:, 4:6]))
                    step.settle()
                    step(TT(st[:, 7:8], st[:, 7:8], lam[:, 5:6], mul))
                    step(TS(esc[:, k % 2, 0, :], esc[:, k % 2, 0, :], st[:, 6:7], None, mul))
                    step.settle()
                    STT(esc[:, k % 2, 0, :], esc[:, k % 2, 1, :], st[:, 7:8], esc[:, k % 2, 0, :], mul, add).then_inc(prob_ready, 1)
            for j in range(4):
                emptied(dve, ("hss", j))
                r = q2[:, 2 * j:2 * j + 2, :].rearrange("p a b -> p (a b)")
                hj = heads[:, 2 * j:2 * j + 2, :].rearrange("p a b -> p (a b)")
                step(nc.vector.reciprocal(r, r))
                step.settle()
                ins = STT(hj, hj, small("subln"), r, mul, mul)
                if j == 3:
                    ins.then_inc(heads_ready, 1)
                else:
                    step(ins)
            for u in range(4):
                emptied(dve, ("gate2a", u))
                m = merged2[:, 2 * u:2 * u + 2, :].rearrange("p a b -> p (a b)")
                TT(m, gate2[:, 0, :], full(dve, ("ao2", u))[:, :], mul).then_inc(free(("ao2", u)), 1)
                emptied(dve, ("gate2f", u))
                TT(rot3[:, u % 2, :], gate2[:, 1, :], full(dve, ("fo", u))[:, :], mul).then_inc(free(("fo", u)), 1)
                emptied(dve, ("ao2", u))
                emptied(dve, ("fo", u))
                TT(m, m, rot3[:, u % 2, :], add).then_inc(merged2_ready, 1)
            mod_bias(16, 40)
            step.settle()
            step(STT(a2[:, :], modT[:, 32:40, 0], 1.0, small("g_n2"), add, mul))
            for u in range(4):
                bank = full(dve, ("wo2", u))
                for j in range(2):
                    k = 2 * u + j
                    ins = STT(hT[:, k, :], bank[:, j * SEQ:(j + 1) * SEQ], modT[:, 16 + k, 0:1], hT[:, k, :], mul, add)
                    if j == 1:
                        ins.then_inc(free(("wo2", u)), 1)
            emptied(dve, ("wo2", 3))
            inv_rms("ss_x1", SEQ)
            scaled(h2, hT, a2, SEQ)
            step.settle()
            for k in range(KT):
                ins = TS(h2[:, k, :], h2[:, k, :], modT[:, 24 + k, 0:1], None, add)
                if k == KT - 1:
                    ins.then_inc(h2_ready, 1)
                else:
                    step(ins)
            mod_bias(40, 48)
            nc.vector.memset(xg[:, :, :], 0.0).then_inc(zeros_ready, 1)
            for j in range(4):
                step(nc.vector.memset(rflat(300 + j, 1), float(4 - j)))
            rank = over(rflat(300, 4), 2)

            def r2(a, n=4):
                return rflat(a, 2 * n).rearrange("p (q n) -> p q n", n=n)

            def one(a):
                return each(rflat(a, 2), 4)

            def now(ins):
                step(ins)
                step.settle()

            def first_of(dst, src, best_at, tmp, tmp2):
                now(nc.vector.tensor_reduce(rflat(best_at, 2), src, AX, ALU.max))
                now(TT(r2(tmp), src, one(best_at), ALU.is_equal))
                now(TT(r2(tmp), r2(tmp), rank, mul))
                now(nc.vector.tensor_reduce(rflat(tmp2, 2), r2(tmp), AX, ALU.max))
                now(TT(r2(dst), r2(tmp), one(tmp2), ALU.is_equal))

            bank = full(dve, "router")
            logits = rflat(0, 40).rearrange("p (q n) -> p q n", n=20)
            TT(logits, bank[:, 0:40].rearrange("p (q n) -> p q n", n=20), over(small("b_router"), 2), add).then_inc(free("router"), 1)
            emptied(dve, "router")
            lg = logits[:, :, 0:4]
            first_of(72, lg, 40, 48, 64)
            TT(r2(80), lg, one(40), sub).then_inc(rexp_arg_ready, 1)
            for g in range(4):
                chosen = rflat(72, 8).rearrange("p (q n) -> p q n", n=4)[:, :, g:g + 1].to_broadcast([128, 2, 4])
                if g == 0:
                    now(TT(r2(96), logits[:, :, 4:8], chosen, mul))
                else:
                    now(TT(r2(104), logits[:, :, 4 + 4 * g:8 + 4 * g], chosen, mul))
                    now(TT(r2(96), r2(96), r2(104), add))
            first_of(112, r2(96), 120, 128, 136)
            now(STT(r2(144), r2(112), -1.0e30, r2(96), mul, add))
            first_of(152, r2(144), 160, 168, 176)
            TT(rflat(180, 2), rflat(160, 2), rflat(120, 2), sub).then_inc(rexp_arg_ready, 1)
            dve.wait_ge(rexp_ready, 2)
            now(nc.vector.tensor_reduce(rflat(190, 2), r2(80), AX, add))
            now(nc.vector.reciprocal(rflat(192, 2), rflat(190, 2)))
            now(TS(rflat(194, 2), rflat(180, 2), 1.0, None, add))
            now(nc.vector.reciprocal(rflat(196, 2), rflat(194, 2)))
            now(TT(rflat(198, 2), rflat(196, 2), rflat(192, 2), mul))
            now(TT(rflat(202, 2), rflat(198, 2), rflat(180, 2), mul))
            now(TT(r2(208), r2(112), one(198), mul))
            now(TT(r2(216), r2(152), one(202), mul))
            now(TT(r2(208), r2(208), r2(216), add))
            for qt in range(2):
                ins = TT(rt[:, 18 + qt, 0:16].rearrange("p (g j) -> p g j", j=4), each(rflat(72 + 4 * qt, 4), 4), over(rflat(208 + 4 * qt, 4), 4), mul)
                step(ins)
            now(TT(r2(224), r2(112), r2(152), add))
            for qt in range(2):
                ins = TT(rt[:, 20 + qt, 0:16].rearrange("p (g j) -> p g j", j=4), each(rflat(72 + 4 * qt, 4), 4), over(rflat(224 + 4 * qt, 4), 4), mul)
                if qt == 1:
                    ins.then_inc(routed_ready, 1)
                else:
                    step(ins)
            step.settle()
            dve.wait_ge(routed_ready, 1)
            bank = full(dve, "rank")
            for qt in range(2):
                m = rt[:, 20 + qt, 0:16]
                place = rt[:, 16 + qt, 0:16]
                now(TS(place, bank[:, qt * 16:(qt + 1) * 16], float(1 + CAP), None, add))
                now(TT(place, place, m, mul))
                now(TS(place, place, 1.0, None, sub))
            CP(rt[:, 22, 0:16], bank[:, 32:48]).then_inc(free("rank"), 1)
            emptied(dve, "rank")
            now(nc.vector.tensor_reduce(rt[:, 23, 0:8], rt[:, 22, 0:16].rearrange("p (a b) -> p a b", b=2), AX, ALU.max))
            now(TS(rt[:, 23, 8:16], rt[:, 23, 0:8], float(CAP), 1.0, ALU.is_gt, add))
            for i in range(2, SEQ // CAP):
                now(STT(rt[:, 23, 8:16], rt[:, 23, 0:8], float(CAP * i), rt[:, 23, 8:16], ALU.is_gt, add))
            CP(passes[:, :], rt[:, 23, 8:16]).then_inc(passes_ready, 1)

            STEPS = 10

            def start_pair(pair):
                for qt in range(2):
                    CP(slot_of[:, qt, :], rt[:, 16 + qt, bass.ds(pair * 2, 2)]).then_inc(slots_loaded, 1)
                    CP(gate_of[:, qt, :], rt[:, 18 + qt, bass.ds(pair * 2, 2)]).then_inc(slots_loaded, 1)
                dve.wait_ge(slots_loaded, 4 * pair + 4)

            def expert_pass(pair, n):
                taken = [0]

                def stp(ins, wait=True):
                    taken[0] += 1
                    ins.then_inc(moe_step, 1)
                    if wait:
                        dve.wait_ge(moe_step, n * STEPS + taken[0])

                stp(TS(slot_of[:, :, :], slot_of[:, :, :], float(CAP), None, sub))
                for j in range(2):
                    for qt in range(2):
                        a = slice(j * CAP, (j + 1) * CAP)
                        stp(TS(pick[:, qt, a], cst2("iota"), slot_of[:, qt, j:j + 1], None, ALU.is_equal), False)
                        ins = TS(pick_gated[:, qt, a], cst2("iota"), slot_of[:, qt, j:j + 1], gate_of[:, qt, j:j + 1], ALU.is_equal, mul)
                        if j == 1 and qt == 1:
                            ins.then_inc(pick_ready, 1)
                        else:
                            stp(ins, False)
                for j in range(2):
                    dve.wait_ge(sig_w1_ready[j], n + 1)
                    stp(TT(sg[:, j, :], sg[:, j, :], psum[2 + j][:, 0:4 * CAP], mul))
                    TT(hid[:, j, :, :], split(sg[:, j, :], CAP), split(psum[2 + j][:, 4 * CAP:8 * CAP], CAP), mul).then_inc(hid_ready[j], 1)
                assert taken[0] == STEPS

            total = each_pass(dve, expert_pass, start_pair)
            dve.wait_ge(scattered, total)
            for k in range(KT):
                ins = STT(hT[:, k, :], psum[4 + k // 2][:, (k % 2) * SEQ:(k % 2 + 1) * SEQ], modT[:, 40 + k, 0:1], hT[:, k, :], mul, add)
                if k == KT - 1:
                    ins.then_inc(h1_ready, 1)
                else:
                    step(ins)
            step.settle()
            inv_rms("ss_out", SEQ)
            scaled(mix2, hT, small("g_final"), SEQ, out_ready)


def _freqs(dim):
    return (10000.0 ** (-(np.arange(0, dim, 2) / dim))).astype(np.float32)


def _rotation(block):
    r = np.zeros((128, 128), np.float32)
    for p in range(128):
        q = p % block
        if q < block // 2:
            r[p, p + block // 2] = -1.0
        else:
            r[p, p - block // 2] = 1.0
    return r.T


def _constants_one():
    c = np.zeros((128, C1_W), np.float32)

    def put(name, a):
        at, w = C1[name]
        c[:, at:at + w] = np.asarray(a).reshape(128, w)

    p, f = np.arange(128)[:, None], np.arange(128)[None, :]
    put("ident", p == f)
    put("ones", np.ones((128, 128)))
    put("eps", np.full((128, 1), EPS))
    put("upper", p <= f)
    put("rot_att", _rotation(128))
    put("rot_idx", _rotation(64))
    for name, dim in (("att", 128), ("idx", 64)):
        inv = _freqs(dim)
        ang = (np.arange(T, dtype=np.float32)[None, :] * inv[np.arange(128) % (dim // 2)][:, None]).astype(np.float64)
        put("cos_" + name, np.cos(ang))
        put("sin_" + name, np.sin(ang))
    put("meta_upper", (p // META == f // META) & (p <= f))
    put("meta_last", f == p // META * META + META - 1)
    put("levels", np.concatenate([(p >> (l + 1) == f >> (l + 1)) & ((p >> l) % 2 == 0) & ((f >> l) % 2 == 1) for l in range(LEVELS)], 1))
    key = np.arange(T)[None, :]
    put("causal", np.concatenate([np.where(key <= META + qt * 128 + p, 0.0, NEG) for qt in range(2)], 1))
    put("head_rows", p // META == np.arange(H)[None, :])
    return c


def _constants_two():
    c = np.zeros((128, C2_W), np.float32)

    def put(name, a):
        at, w = C2[name]
        c[:, at:at + w] = np.asarray(a).reshape(128, w)

    put("rot_ax", _rotation(32))
    p, n = np.arange(128), np.arange(SEQ)
    inv = (1.0 / (10000.0 ** (np.arange(16) / 16))).astype(np.float32)
    pos = np.where((p % 64 // 32 == 0)[:, None], (n // 64)[None, :], (n % 64)[None, :]).astype(np.float32)
    ang = (pos * inv[p % 16][:, None]).astype(np.float64)
    put("cos_ax", np.cos(ang))
    put("sin_ax", np.sin(ang))
    d = 2 * np.pi * np.outer(p, p) / 128
    put("dft_d", np.concatenate([np.cos(d), np.sin(d)], 1) / np.sqrt(128))
    t = 2 * np.pi * np.outer(n, n) / SEQ
    put("earlier", p[:, None] < p[None, :])
    put("iota", np.broadcast_to(np.arange(CAP), (128, CAP)))
    put("dft_n", np.concatenate([m[nt * 128:(nt + 1) * 128] for nt in range(2) for m in (np.cos(t), -np.sin(t))], 1) / np.sqrt(SEQ))
    return c


def _unit(w, rows, cols):
    return w[rows, cols].reshape(-1, 128, cols.stop - cols.start).transpose(1, 0, 2).reshape(128, -1)


def _stream(x):
    w_in, w_in2 = x["w_in"][0], x["w_in_2"][0]
    every = slice(0, D)
    offsets = {"gq": 0, "gk": 1024, "gv": 2048, "gz": 3072, "aq": 4112, "ak": 5136, "av": 5392, "iq": 5648, "gate_a": 6232, "gate_b": 7256}
    offsets2 = {"q2": 0, "k2": 1024, "v2": 2048, "f2": 3072, "gate2a": 3584, "gate2f": 4608}
    whole = {"mod": x["w_mod_2"][0], "bg": x["w_branch_gdn"][0], "bd": x["w_branch_dsa"][0], "wo": x["w_out"][0], "up": x["w_up"][0],
             "ao": x["w_attn_out_2"][0], "wo2": x["w_out_2"][0]}
    s = np.empty((len(ORDER), 128, KT * UNIT_COLS), np.float32)
    for i, (kind, u) in enumerate(ORDER):
        c = slice(u * 256, (u + 1) * 256)
        if kind in offsets:
            s[i] = _unit(w_in, every, slice(offsets[kind] + c.start, offsets[kind] + c.stop))
        elif kind in offsets2:
            s[i] = _unit(w_in2, every, slice(offsets2[kind] + c.start, offsets2[kind] + c.stop))
        elif kind in whole:
            s[i] = _unit(whole[kind], every, c)
        elif kind == "down":
            cp, kg = divmod(u, 4)
            s[i] = _unit(x["w_down"][0], slice(kg * D, (kg + 1) * D), slice(cp * 256, (cp + 1) * 256))
        elif kind == "fo":
            s[i] = _unit(x["w_four_out_2"][0], slice(0, 512), slice(u * 512, (u + 1) * 512))
        elif kind == "e_up":
            e, q = divmod(u, 4)
            w = x["w_exp_gate_2" if q < 2 else "w_exp_up_2"][0, e]
            s[i] = _unit(w, every, slice(q % 2 * 256, (q % 2 + 1) * 256))
        else:
            e, q = divmod(u, 2)
            s[i] = _unit(x["w_exp_down_2"][0, e], slice(0, EH), slice(q * 512, (q + 1) * 512))
    return s


def _smalls(x):
    c = np.zeros((128, SM_W), np.float32)

    def put(name, a):
        at, w = SM[name]
        c[:, at:at + w] = a.reshape(128, w)

    def cols(v):
        return v.reshape(-1, 128).T

    for name, v in (("g_pre_mix", x["pre_mix_norm"]), ("g_post_mix", x["post_mix_norm"]), ("g_pre_mlp", x["pre_mlp_norm"]),
                    ("g_post_mlp", x["post_mlp_norm"]), ("g_n1", x["norm1_g_2"]), ("g_n2", x["norm2_g_2"]), ("g_final", x["final_g_2"]),
                    ("gdn_norm", x["gdn_norm"]), ("subln", x["subln_g_2"]), ("b_mod", x["b_mod_2"])):
        put(name, cols(v))
    put("conv", x["conv_w"][0].reshape(4, 24, 128).transpose(2, 1, 0))
    put("c", np.stack([cols(x["c_2"]), cols(x["c_ctx_2"])], 2))
    put("dt_bias", np.broadcast_to(x["dt_bias"], (128, H)))
    put("a_log", np.broadcast_to(x["a_log"], (128, H)))
    put("b_router", np.broadcast_to(np.concatenate([x["b_router_group_2"][0], x["b_router_expert_2"][0]]), (128, 20)))
    return c


def _small_weights(x):
    w = x["w_in"][0]

    def cols(a, b):
        return w[:, a:b].reshape(KT, 128, b - a).transpose(1, 0, 2)

    ik = cols(6160, 6224)
    return np.concatenate([cols(4096, 4112).reshape(128, -1), np.concatenate([ik, ik], 2).reshape(128, -1),
                           cols(6224, 6232).reshape(128, -1)], 1)


def _columns(a):
    return np.ascontiguousarray(a.T.reshape(KT, 128, -1).transpose(1, 0, 2))


def kernel(**inputs):
    import concourse.bacc as bacc
    from concourse.bass_utils import run_bass_kernel_spmd

    x = {name: np.asarray(a) for name, a in inputs.items()}
    router = np.concatenate([x["w_router_group_2"][0], x["w_router_expert_2"][0]], 1)
    arrays = {
        "stream": _stream(x),
        "h_in": _columns(np.concatenate([x["meta_tokens"], x["x"][0]])),
        "ctx_in": _columns(x["ctx_2"][0]),
        "constants_one": _constants_one(),
        "constants_two": _constants_two(),
        "smalls": _smalls(x),
        "small_weights": _small_weights(x),
        "router": np.ascontiguousarray(router.reshape(KT, 128, 20).transpose(1, 0, 2)),
        "lambdas": np.stack([x["lam_q1_2"][0], x["lam_k1_2"][0], x["lam_q2_2"][0], x["lam_k2_2"][0]], 1),
    }
    nc = bacc.Bacc("TRN2", target_bir_lowering=False, num_devices=1)
    args = [nc.dram_tensor(name, a.shape, mybir.dt.float32, kind="ExternalInput").ap() for name, a in arrays.items()]
    args.append(nc.dram_tensor("result", (128, KT, SEQ), mybir.dt.float32, kind="ExternalOutput").ap())
    build(nc, *args)
    r = run_bass_kernel_spmd(nc, [arrays], core_ids=[0])
    return np.ascontiguousarray(r.results[0]["result"].transpose(2, 1, 0)).reshape(1, SEQ, D)
```

```python
import math
from contextlib import ExitStack

import concourse.bass as bass
import numpy as np
from concourse import mybir

D = 1024
KT = D // 128
META = 16
SEQ = 256
T = META + SEQ
H = 8
CH = 128
NCH = SEQ // CH
NSYS = H * NCH
LEVELS = 7
META_LEVELS = 4
TOPK = SEQ // 4
KV_HEADS = 2
CTX = 256
DFF = 4096
FT = DFF // 128
EPS = 1e-6
N_EXP = 16
LAM_INIT = 0.8 - 0.6 * math.exp(-0.0)
EH = D // 2
NGRP = 4
PAIRS = N_EXP // 2
CAP = 64
UNIT_COLS = 256
SLOTS = 6
SPLITS = 4
EXPERT_UNITS = 12
G_EVERY, G_FIRST = 3, 1
NEG = -3.0e38
TAKEN = -3.3e38
MOD_TILES = 6 * D // 128
MOD_UNITS = MOD_TILES // 2
MOD_SLOTS = 6

def _layout(widths):
    at, out = 0, {}
    for name, w in widths:
        out[name] = (at, w)
        at += w
    return out, at

C1, C1_W = _layout([("ident", 128), ("upper", 128), ("rot_att", 128), ("rot_idx", 128),
                    ("cos_att", T), ("sin_att", T), ("cos_idx", T), ("sin_idx", T),
                    ("meta_upper", 128), ("meta_last", 128), ("levels", LEVELS * 128),
                    ("causal", NCH * T), ("head_rows", H)])
C2, C2_W = _layout([("rot_ax", 128), ("cos_ax", SEQ), ("sin_ax", SEQ), ("dft_d", 256), ("dft_n", 4 * SEQ),
                    ("earlier", 128), ("iota", CAP)])
SM, SM_W = _layout([("g_pre_mix", KT), ("g_post_mix", KT), ("g_pre_mlp", KT), ("g_post_mlp", KT),
                    ("g_n1", KT), ("g_n2", KT), ("g_final", KT), ("conv", 24 * 4), ("gdn_norm", 1),
                    ("subln", 1), ("b_mod", MOD_TILES), ("c", KT * 2), ("dt_bias", H), ("a_log", H),
                    ("b_router", 20)])
C2_AT = C1["upper"][0]
WS, WS_W = _layout([("gba", KT * 16), ("ik", KT * 128), ("iw", KT * 8)])

def weight_order():
    order = [("gk", u) for u in range(4)] + [("gv", u) for u in range(4)] + [("gq", u) for u in range(4)]
    order += [("mod", u) for u in range(8)]
    order += [("gz", u) for u in range(4)] + [("aq", u) for u in range(4)] + [("ak", 0), ("av", 0)]
    order += [("iq", u) for u in range(2)]
    for u in range(4):
        order += [("gate_a", u), ("bg", u)]
    for u in range(4):
        order += [("gate_b", u), ("bd", u)]
    order += [("wo", u) for u in range(4)]
    order += [("mod", u) for u in range(8, 13)]
    order += [("up", u) for u in range(16)]
    order += [("down", u) for u in range(16)]
    order += [("mod", u) for u in range(13, 18)]
    order += [("q2", u) for u in range(4)] + [("k2", u) for u in range(4)] + [("v2", u) for u in range(4)]
    order += [("f2", u) for u in range(2)]
    for u in range(4):
        order += [("gate2a", u)] + ([("mod", 18), ("mod", 19)] if u == 0 else []) + [("ao", u), ("gate2f", u)] + ([("fo", u // 2)] if u % 2 == 0 else [])
    order += [("wo2", u) for u in range(4)]
    order += [("mod", u) for u in range(20, 24)]
    for pair in range(PAIRS):
        order += [("e_up", 8 * pair + u) for u in range(8)] + [("e_down", 4 * pair + u) for u in range(4)]
    return order

ORDER = weight_order()
FIRST_EXPERT = ORDER.index(("e_up", 0))
BASE = FIRST_EXPERT // SLOTS
MAX_PASSES = PAIRS * (SEQ // CAP)
assert EXPERT_UNITS == 2 * SLOTS and EXPERT_UNITS % SPLITS == 0
assert len(ORDER) % SLOTS == 0 and FIRST_EXPERT % SLOTS == 0


class Steps:

    def __init__(self, eng, sem):
        self.eng, self.sem, self.n = eng, sem, 0

    def __call__(self, ins):
        self.n += 1
        ins.then_inc(self.sem, 1)

    def settle(self):
        self.eng.wait_ge(self.sem, self.n)


class Banks:

    def __init__(self, full, free):
        self.full, self.free = full, free
        self.turn, self.filled, self.freed = 0, [0] * 8, [0] * 8
        self.at, self.full_when, self.free_when = {}, {}, {}

    def take(self, name, drains, bank=None):
        if bank is None:
            bank = self.turn % 8
            self.turn += 1
        before = self.freed[bank]
        self.freed[bank] += drains
        self.at[name] = bank
        self.free_when[name] = self.freed[bank]
        return bank, before

    def fill(self, name):
        bank = self.at[name]
        self.filled[bank] += 1
        self.full_when[name] = (self.full[bank], self.filled[bank])
        return self.full[bank]


def build(nc, stream, h_in, ctx_in, c1_in, c2_in, sm_in, ws_in, wr_in, lam_in, out):
    f32 = mybir.dt.float32
    ALU, ACT, AX = mybir.AluOpType, mybir.ActivationFunctionType, mybir.AxisListType.X
    mul, add, sub = ALU.mult, ALU.add, ALU.subtract
    top = ExitStack()
    with top:
        def sb(stack, name, *shape):
            return stack.enter_context(nc.sbuf_tensor(name, list(shape), f32))

        def sbr(stack, name, *shape):
            return stack.enter_context(nc.sbuf_tensor(name, list(shape), mybir.dt.float32r))

        def sem(name):
            return top.enter_context(nc.semaphore(name))

        ring = sb(top, "ring", 128, SLOTS, KT * UNIT_COLS)
        c1 = sb(top, "c1", 128, C1_W)
        sm = sb(top, "sm", 128, SM_W)
        hT = sb(top, "hT", 128, KT, SEQ)
        modT = sb(top, "modT", 128, MOD_TILES, 2)
        silu_c = sb(top, "silu_c", 128, KT, 2)
        mod_rows = sb(top, "mod_rows", 2, MOD_SLOTS, UNIT_COLS)
        a1 = sb(top, "a1", 128, KT, 2)
        a2 = sb(top, "a2", 128, KT)
        rB = sb(top, "rB", 128, T)
        root = sb(top, "root", 128, T)
        lam = sb(top, "lam", 128, 8)
        wr = sb(top, "wr", 128, KT, 20)

        def cst(name, rows=128):
            a, w = C1[name]
            return c1[0:rows, a:a + w]

        def small(name):
            a, w = SM[name]
            return sm[:, a:a + w]

        ident, upper = cst("ident"), cst("upper")
        ones, eps = sb(top, "ones", 128, 128)[:, :], sb(top, "eps", 128, 1)[:, :]

        with ExitStack() as mixer:
            nT = sb(mixer, "nT", 128, KT, T)
            ws = sb(mixer, "ws", 128, WS_W)
            y_gdn = sb(mixer, "y_gdn", 128, H, SEQ)
            with ExitStack() as m:
                kc = sb(m, "kc", 128, H, T)
                vc = sb(m, "vc", 128, H, T)
                qc = sb(m, "qc", 128, H, T)
                v_beta = sb(m, "v_beta", 128, NSYS, 128)
                attn = sb(m, "attn", 128, NSYS, 128)
                k_tail = sb(m, "k_tail", 128, NSYS, 128)
                inv = sb(m, "inv", 128, NSYS, 128)
                invT = sb(m, "invT", 128, NSYS, 128)
                low = sb(m, "low", 128, NSYS, 128)
                masked = sb(m, "masked", 128, 2, 512)
                prod = sb(m, "prod", 128, 2, 512)
                state = sb(m, "state", 128, 2, H * 128)
                scr = sb(m, "scr", 128, 2, 1024)
                metas = sb(m, "metas", 128, 10, 128)
                mcol = sb(m, "mcol", 128, 4)
                egl = sb(m, "egl", 128, NSYS)
                tok = sb(m, "tok", 128, 8, 24)
            with ExitStack() as m:
                merged = sb(m, "merged", 128, KT, SEQ)
                gate = sb(m, "gate", 128, 2, 512)
                aq = sb(m, "aq", 128, H, SEQ)
                ak = sb(m, "ak", 128, KV_HEADS, T)
                av = sb(m, "av", 128, 3, KV_HEADS * 128)
                iq = sb(m, "iq", 128, 4, SEQ)
                ik = sb(m, "ik", 128, T)
                iw = sb(m, "iw", 128, NCH, H)
                rot1 = sb(m, "rot1", 128, 512)
                rot2 = sb(m, "rot2", 128, 512)
                relu = sb(m, "relu", 128, 2, T)
                score = sb(m, "score", 128, NCH, T)
                work = sb(m, "work", 128, 2, T)
                best = sb(m, "best", 128, 8)
                bias = sb(m, "bias", 128, NCH, T)
                lmask = sb(m, "lmask", 128, 2, T)
                prob = sb(m, "prob", 128, 2, T)
                probT = sb(m, "probT", 128, 2, 3 * 128)
                stat = sb(m, "stat", 128, 2, 4)
                y_dsa = sb(m, "y_dsa", 128, H, SEQ)
        with ExitStack() as rest:
            ctxT = sb(rest, "ctxT", 128, KT, CTX)
            with ExitStack() as m:
                with ExitStack() as early:
                    _first = sb(early, "before_nM", 128, (FT - KT // 2) * 2 * SEQ)
                    nM = sb(early, "nM", 128, KT, SEQ)
                up = sbr(m, "up", 128, FT, 2, SEQ)
                with ExitStack() as outer:
                    mix = sb(outer, "mix", 128, KT, SEQ)
                    sq = sb(outer, "sq", 128, KT, SEQ)
                nMs = sbr(m, "nMs", 128, KT, 2, SEQ)
                mlp_parts = sbr(m, "mlp_parts", 128, 2, 2, KT * UNIT_COLS)
                hidden_now = sb(m, "hidden_now", 128, 2, 512)
            with ExitStack() as m:
                hcl = sb(m, "hcl", 128, KT, CTX + SEQ)
                q2 = sb(m, "q2", 128, H, SEQ)
                k2 = sb(m, "k2", 128, H, CTX + SEQ)
                v2 = sb(m, "v2", 128, 4, D)
                f2 = sb(m, "f2", 128, 4, SEQ)
                zdft = sb(m, "zdft", 128, 4, 2, 256)
                four = sb(m, "four", 128, 4, SEQ)
                sq1 = sb(m, "sq1", 128, KT, SEQ)
                heads = sb(m, "heads", 128, H, SEQ)
                esc = sb(m, "esc", 128, 2, 2, 512)
                aT = sb(m, "aT", 128, 2, 512)
                stat2 = sb(m, "stat2", 128, 2, 8)
                rot3 = sb(m, "rot3", 128, 2, 512)
                merged2 = sb(m, "merged2", 128, KT, SEQ)
                gate2 = sb(m, "gate2", 128, 2, 512)
            with ExitStack() as m:
                h2 = sb(m, "h2", 128, KT, SEQ)
                sq2 = h2
                h2tok = sb(m, "h2tok", 128, 2, D)
                mix2 = h2tok[:, :, :].rearrange("p a (b n) -> p (a b) n", n=SEQ)
                rt = sb(m, "rt", 128, 24, 32)
                slot_of = sb(m, "slot_of", 128, 2, 2)
                gate_of = sb(m, "gate_of", 128, 2, 2)
                pick = sb(m, "pick", 128, 2, 2 * CAP)
                pick_gated = sb(m, "pick_gated", 128, 2, 2, 2, CAP)
                spread = sb(m, "spread", 128, 2, SEQ)
                xs = sbr(m, "xs", 128, KT, 2, 2 * CAP)
                yb = sb(m, "yb", 128, 2, D)
                sg = sb(m, "sg", 128, 2, 4 * CAP)
                hid = sb(m, "hid", 128, 2, 4 * CAP)
                hids = sbr(m, "hids", 128, 2, 4, 2 * CAP)
                fold = sb(m, "fold", 128, CAP)
                passes = m.enter_context(nc.sbuf_tensor("passes", [128, PAIRS], mybir.dt.int32))
                plan = m.enter_context(nc.sbuf_tensor("plan", [128, MAX_PASSES + 1], mybir.dt.int32))
                parts = sbr(m, "parts", 128, SPLITS, 2, KT * UNIT_COLS)
        c2 = c1[:, C2_AT:C2_AT + C2_W]

        def cst2(name):
            a, w = C2[name]
            return c2[:, a:a + w]

        psum = [top.enter_context(nc.psum_tensor(f"bank{b}", [128, 512], f32)) for b in range(8)]
        banks = Banks([sem(f"bank_full{b}") for b in range(8)], [sem(f"bank_free{b}") for b in range(8)])

        unit_loaded = [sem(f"unit_loaded{s}") for s in range(SLOTS)]
        unit_used = [sem(f"unit_used{s}") for s in range(SLOTS)]
        h_loaded, c1_loaded, sm_loaded, ws_loaded = sem("h_loaded"), sem("c1_loaded"), sem("sm_loaded"), sem("ws_loaded")
        res_loaded, ctx_loaded, c2_loaded, lam_loaded, wr_loaded = (sem("res_loaded"), sem("ctx_loaded"), sem("c2_loaded"),
                                                        sem("lam_loaded"), sem("wr_loaded"))
        act_step, dve_step, out_stored = sem("act_step"), sem("dve_step"), sem("out_stored")

        block = top.enter_context(nc.Block())

        MLP_FIRST = ORDER.index(("up", 0))
        MLP_UNITS = 32
        G_COLS = 512

        def ring_unit(g):
            return g % SLOTS, g // SLOTS + 1

        def mlp_unit_used(eng, m):
            s, n = ring_unit(MLP_FIRST + m)
            eng.wait_ge(unit_used[s], n)

        def low_part_of(n, i):
            if i % G_EVERY == G_FIRST:
                return low_ready_g, n * 4 + (i // G_EVERY + 1)
            return low_ready, n * 8 + (i - (i + 1) // G_EVERY + 1)

        def full(eng, name):
            eng.wait_ge(*banks.full_when[name])
            return psum[banks.at[name]]

        def free(name):
            return banks.free[banks.at[name]]

        def emptied(eng, name, but=0):
            eng.wait_ge(banks.free[banks.at[name]], banks.free_when[name] - but)

        ones_ready = sem("ones_ready")
        sq_ready = sem("sq_ready")
        silu_ready = sem("silu_ready")
        sig_ready = sem("sig_ready")
        nT_ready = sem("nT_ready")
        normed_ready = sem("normed_ready")
        absx_ready = sem("absx_ready")
        softplus_ready = sem("softplus_ready")
        tri_ready = sem("tri_ready")
        meta_arg_ready = sem("meta_arg_ready")
        meta_exp_ready = sem("meta_exp_ready")
        decay_arg_ready = sem("decay_arg_ready")
        decay_exp_ready = sem("decay_exp_ready")
        masked_ready = sem("masked_ready")
        scan_ready = sem("scan_ready")
        y_ready = sem("y_ready")
        roped_ready = sem("roped_ready")
        score_ready = sem("score_ready")
        nmax_ready = sem("nmax_ready")
        pexp_ready = sem("pexp_ready")
        prob_ready = sem("prob_ready")
        merged_ready = sem("merged_ready")
        h1_ready = sem("h1_ready")
        nM_ready = sem("nM_ready")
        up_ready = sem("up_ready")
        lamp_ready = sem("lamp_ready")
        hcl_ready = sem("hcl_ready")
        roped2_ready = sem("roped2_ready")
        heads_ready = sem("heads_ready")
        merged2_ready = sem("merged2_ready")
        h2_ready = sem("h2_ready")
        rexp_arg_ready = sem("rexp_arg_ready")
        rexp_ready = sem("rexp_ready")
        routed_ready = sem("routed_ready")
        passes_ready = sem("passes_ready")
        plan_ready = sem("plan_ready")
        slots_loaded = sem("slots_loaded")
        pick_ready = sem("pick_ready")
        moe_step = sem("moe_step")
        mlp_high_ready = sem("mlp_high_ready")
        mlp_low_ready = sem("mlp_low_ready")
        mlp_low_ready_g = sem("mlp_low_ready_g")
        hid_high_ready = sem("hid_high_ready")
        high_ready = sem("high_ready")
        low_ready = sem("low_ready")
        low_ready_g = sem("low_ready_g")
        parts_used = sem("parts_used")
        gathered = sem("gathered")
        xs_ready = sem("xs_ready")
        spread_full = sem("spread_full")
        spread_ready = sem("spread_ready")
        yb_ready = sem("yb_ready")
        folded = [sem(f"folded{j}") for j in range(2)]
        sig_w1_ready = [sem(f"sig_w1_ready{j}") for j in range(2)]
        hid_ready = [sem(f"hid_ready{j}") for j in range(2)]
        ys_ready = sem("ys_ready")
        scattered = sem("scattered")
        out_ready = sem("out_ready")

        LEVEL_ITEMS = [(l, g) for l in range(LEVELS) for g in (4, 0, 1, 2, 3) if g < 4 or l < META_LEVELS]

        CONV_TILES = [(kind, j) for kind in ("gk", "gv", "gq") for j in range(H)]

        L2_AFTER = list(range(8, 16)) + [17, 19, 21, 23]

        def conv_dst(t):
            kind, j = CONV_TILES[t]
            return {"gk": kc, "gv": vc, "gq": qc}[kind][:, j, :]

        def raw_of(kind, j):
            if kind == "ik":
                return ik[:, :].unsqueeze(1), T
            if kind == "ak":
                return ak[:, j:j + 1, :], T
            return (aq if kind == "aq" else iq)[:, 2 * j:2 * j + 2, :], 512

        def rflat(a, n):
            return rt[:, :, :].rearrange("p a b -> p (a b)")[:, a:a + n]

        def systems(g):
            return [4 * g + s for s in range(4)] if g < 4 else [None]

        def sysview(t, meta_slot, s):
            return t[:, s, :] if s is not None else metas[:, meta_slot, :]

        def chunk(t, h, ci):
            a = META + ci * CH
            return t[:, h, a:a + CH]

        def nkeys(qt):
            return META + (qt + 1) * 128

        def key_tiles(qt):
            n = nkeys(qt)
            return [(a, min(128, n - a)) for a in range(0, n, 128)]

        ATT = [(qt, h) for qt in range(2) for h in range(H)]
        ROPES = [("aq", j) for j in range(4)] + [("ak", j) for j in range(2)] + [("iq", j) for j in range(2)] + [("ik", 0)]

        def each_pass(eng, body, start_pair=lambda pair: None):
            eng.wait_ge(passes_ready, 1)
            so_far = eng.alloc_register()
            eng.reg_mov(so_far, 0)
            with eng.Fori(0, PAIRS) as pair:
                start_pair(pair)
                count = eng.value_load(passes[0:1, bass.ds(pair, 1)], min_val=1, max_val=SEQ // CAP)
                with eng.Fori(0, count):
                    body(pair, eng.snap(so_far, min_val=0, max_val=MAX_PASSES))
                    eng.reg_add(so_far, so_far, 1)
            return eng.snap(so_far, min_val=PAIRS, max_val=MAX_PASSES)

        @block.tensor
        def _(pe):
            at = [0]

            def unit(kind, u):
                assert ORDER[at[0]] == (kind, u), (ORDER[at[0]], kind, u)
                s, n = at[0] % SLOTS, at[0] // SLOTS + 1
                at[0] += 1
                pe.wait_ge(unit_loaded[s], 16 * n)
                return s, n

            def by_k(s, cols=UNIT_COLS):
                return ring[:, s, :].rearrange("p (k n) -> p k n", n=cols)

            def take(name, drains=1, bank=None):
                b, before = banks.take(name, drains, bank)
                if before:
                    pe.wait_ge(banks.free[b], before)
                return psum[b]

            def done(name, ins):
                ins.then_inc(banks.fill(name), 1)

            def group(dst, pairs):
                for i, (lhs, rhs) in enumerate(pairs):
                    last = nc.tensor.matmul(dst, lhs, rhs, start=(i == 0), stop=(i == len(pairs) - 1))
                return last

            def tiles_of_unit(kind, u, rhs, n, names, kt=KT, drains=1):
                s, cnt = unit(kind, u)
                w = by_k(s)
                if len(names) == 2:
                    for j in range(2):
                        dst = take(names[j], drains)
                        last = group(dst[:, 0:n], [(w[:, k, j * 128:(j + 1) * 128], rhs[:, k, :]) for k in range(kt)])
                        if j == 0:
                            done(names[0], last)
                else:
                    dst = take(names[0], drains)
                    for j in range(2):
                        last = group(dst[:, j * n:(j + 1) * n], [(w[:, k, j * 128:(j + 1) * 128], rhs[:, k, :]) for k in range(kt)])
                last.then_inc(unit_used[s], 1)
                banks.full_when[names[-1]] = (unit_used[s], cnt)

            def mod_unit(u):
                s, cnt = unit("mod", u)
                dst = take(("mod_row", u))
                group(dst[0:2, 0:UNIT_COLS], [(silu_c[:, k, :], by_k(s)[:, k, :]) for k in range(KT)]).then_inc(unit_used[s], 1)
                banks.full_when[("mod_row", u)] = (unit_used[s], cnt)

            def mod_columns(a, b):
                emptied(pe, ("mod_row", b - 1))
                dst = take(("mod", a))
                for t in range(2 * (b - a)):
                    row = mod_rows[:, (a + t // 2) % MOD_SLOTS, (t % 2) * 128:(t % 2 + 1) * 128]
                    last = nc.tensor.transpose(dst[:, 2 * t:2 * t + 2], row, ident[0:2, 0:2])
                done(("mod", a), last)

            def feature_sum(name, src, n, drains=1):
                dst = take(name, drains)
                done(name, group(dst[:, 0:n], [(ones, src[:, k, :]) for k in range(KT)]))

            pe.wait_ge(sq_ready, 1)
            pe.wait_ge(ones_ready, 1)
            feature_sum("ss_in", vc[:, :, :], T)

            def l2_sum(i):
                n = T if i < 8 else 512
                pe.wait_ge(sq_ready, 2 + i)
                dst = take(("l2", i), 1)
                done(("l2", i), nc.tensor.matmul(dst[:, 0:n], ones, masked[:, i % 2, 0:n], start=True, stop=True))

            pe.wait_ge(nT_ready, 1)
            for t in range(0, 24, 2):
                kind = CONV_TILES[t][0]
                u = t % 8 // 2
                tiles_of_unit(kind, u, nT, T, [(kind, 2 * u), (kind, 2 * u + 1)])
                for i in range(12):
                    if L2_AFTER[i] in (t - 4, t - 3):
                        l2_sum(i)
            pe.wait_ge(ws_loaded, 16)
            gba = ws[:, 0:KT * 16].rearrange("p (k n) -> p k n", n=16)
            dst = take("gba", 2)
            for g, a in enumerate((0, META, META + CH)):
                last = group(dst[:, g * 16:(g + 1) * 16], [(nT[:, k, a:a + 128], gba[:, k, :]) for k in range(KT)])
            done("gba", last)

            l2_sum(10)
            l2_sum(11)
            pe.wait_ge(silu_ready, 1)
            for u in range(6):
                mod_unit(u)

            pe.wait_ge(c1_loaded, 16)
            pe.wait_ge(tri_ready, 1)
            dst = take("gct", 2)
            for ci in range(NCH):
                last = nc.tensor.matmul(dst[:, ci * 8:(ci + 1) * 8], upper, tok[:, 3, (1 + ci) * 8:(2 + ci) * 8], start=True, stop=True)
            done("gct", last)
            dst = take("metaGB", 1)
            nc.tensor.matmul(dst[:, 0:128], ones[0:META, :], metas[0:META, 0, :], start=True, stop=True)
            done("metaGB", nc.tensor.matmul(dst[:, 128:256], ones[0:META, :], metas[0:META, 1, :], start=True, stop=True))
            dst = take("metaK", 1)
            nc.tensor.matmul(dst[:, 0:128], metas[:, 2, :], metas[:, 2, :], start=True, stop=True)
            nc.tensor.transpose(dst[:, 128:256], metas[:, 2, :], ident)
            done("metaK", nc.tensor.transpose(dst[:, 256:384], metas[:, 3, :], ident))

            mod_columns(0, 6)

            for h in range(H):
                dst = take(("GB", h), 2)
                for ci in range(NCH):
                    sy = h * NCH + ci
                    nc.tensor.matmul(dst[:, ci * 128:(ci + 1) * 128], inv[:, sy, :], upper, start=True, stop=True)
                    last = nc.tensor.matmul(dst[:, 256 + ci * 128:384 + ci * 128], invT[:, sy, :], ident, start=True, stop=True)
                done(("GB", h), last)
                dst = take(("KQ", h), 1)
                for ci in range(NCH):
                    k_c, q_c = chunk(kc, h, ci), chunk(qc, h, ci)
                    nc.tensor.matmul(dst[:, ci * 128:(ci + 1) * 128], k_c, k_c, start=True, stop=True)
                    last = nc.tensor.matmul(dst[:, 256 + ci * 128:384 + ci * 128], k_c, q_c, start=True, stop=True)
                done(("KQ", h), last)
                dst = take(("TR", h), 1)
                for ci in range(NCH):
                    nc.tensor.transpose(dst[:, ci * 128:(ci + 1) * 128], chunk(kc, h, ci), ident)
                    last = nc.tensor.transpose(dst[:, 256 + ci * 128:384 + ci * 128], chunk(vc, h, ci), ident)
                done(("TR", h), last)

            def level_p(n):
                l, g = LEVEL_ITEMS[n]
                pe.wait_ge(masked_ready, n + 1)
                if l > 0:
                    emptied(pe, ("QT", LEVEL_ITEMS.index((l - 1, g))))
                dst = take(("P", n))
                for j, s in enumerate(systems(g)):
                    rhs = ident if l == 0 else sysview(inv, 8, s)
                    last = nc.tensor.matmul(dst[:, j * 128:(j + 1) * 128], masked[:, n % 2, j * 128:(j + 1) * 128], rhs, start=True, stop=True)
                done(("P", n), last)

            def level_q(n):
                l, g = LEVEL_ITEMS[n]
                emptied(pe, ("P", n))
                end = META_LEVELS - 1 if g == 4 else LEVELS - 1
                if 0 < l < end:
                    dst = take(("Q", n), 1)
                    for j, s in enumerate(systems(g)):
                        last = nc.tensor.matmul(dst[:, j * 128:(j + 1) * 128], sysview(invT, 9, s), prod[:, n % 2, j * 128:(j + 1) * 128], start=True, stop=True)
                    done(("Q", n), last)
                dst = take(("QT", n), 1)
                for j, s in enumerate(systems(g)):
                    rhs = ident if l == 0 else sysview(invT, 9, s)
                    last = nc.tensor.matmul(dst[:, j * 128:(j + 1) * 128], prod[:, n % 2, j * 128:(j + 1) * 128], rhs, start=True, stop=True)
                done(("QT", n), last)

            mod_unit(6)
            mod_unit(7)
            for n in range(len(LEVEL_ITEMS)):
                level_p(n)
                if n >= 1:
                    level_q(n - 1)
            level_q(len(LEVEL_ITEMS) - 1)
            assert ORDER[at[0]] == ("gz", 0), ORDER[at[0]]

            pe.wait_ge(scan_ready, 1)
            dst = take("meta_v", 1)
            emptied(pe, ("QT", LEVEL_ITEMS.index((META_LEVELS - 1, 4))))
            done("meta_v", nc.tensor.matmul(dst[:, 0:128], metas[:, 9, :], metas[:, 7, :], start=True, stop=True))
            emptied(pe, "meta_v")
            for hg in range(2):
                dst = take(("S0", hg), 1)
                for j in range(4):
                    h = hg * 4 + j
                    last = nc.tensor.matmul(dst[:, j * 128:(j + 1) * 128], scr[:, 0, h * 128:(h + 1) * 128], metas[:, 3, :], start=True, stop=True)
                done(("S0", hg), last)
            mod_columns(6, 8)
            emptied(pe, ("QT", len(LEVEL_ITEMS) - 1))
            for ci in range(NCH):
                for hg in range(2):
                    emptied(pe, ("S0", hg) if ci == 0 else ("dS", ci - 1, hg))
                    dst = take(("kS", ci, hg), 1)
                    for j in range(4):
                        h = hg * 4 + j
                        last = nc.tensor.matmul(dst[:, j * 128:(j + 1) * 128], chunk(kc, h, ci), state[:, ci, h * 128:(h + 1) * 128], start=True, stop=True)
                    done(("kS", ci, hg), last)
                for hg in range(2):
                    emptied(pe, ("kS", ci, hg))
                    dst = take(("vn", ci, hg), 1)
                    for j in range(4):
                        sy = (hg * 4 + j) * NCH + ci
                        last = nc.tensor.matmul(dst[:, j * 128:(j + 1) * 128], invT[:, sy, :], scr[:, hg, j * 128:(j + 1) * 128], start=True, stop=True)
                    done(("vn", ci, hg), last)
                for hg in range(2):
                    emptied(pe, ("vn", ci, hg))
                    if ci + 1 < NCH:
                        dst = take(("dS", ci, hg), 1)
                        for j in range(4):
                            sy = (hg * 4 + j) * NCH + ci
                            last = nc.tensor.matmul(dst[:, j * 128:(j + 1) * 128], k_tail[:, sy, :], scr[:, hg, 512 + j * 128:640 + j * 128], start=True, stop=True)
                        done(("dS", ci, hg), last)
                    dst = take(("o", ci, hg), 1)
                    for j in range(4):
                        h = hg * 4 + j
                        last = group(dst[:, j * 128:(j + 1) * 128],
                                     [(state[:, ci, h * 128:(h + 1) * 128], chunk(qc, h, ci)),
                                      (scr[:, hg, 512 + j * 128:640 + j * 128], attn[:, h * NCH + ci, :])])
                    done(("o", ci, hg), last)
            for u in range(4):
                tiles_of_unit("gz", u, nT[:, :, META:T], SEQ, [("gz", u)])
            pe.wait_ge(sq_ready, 14)
            for j in range(4):
                dst = take(("yss", j), 1)
                done(("yss", j), nc.tensor.matmul(dst[:, :], ones, low[:, 4 * j:4 * j + 4, :], start=True, stop=True))

            def rope(i):
                kind, j = ROPES[i]
                emptied(pe, "ik" if kind == "ik" else ROPES[i])
                dst = take(("rot", i), 1)
                src, n = raw_of(kind, j)
                r = "rot_att" if kind in ("aq", "ak") else "rot_idx"
                done(("rot", i), nc.tensor.matmul(dst[:, 0:n], cst(r), src, start=True, stop=True))

            real = nT[:, :, META:T]
            for u in range(4):
                tiles_of_unit("aq", u, real, SEQ, [("aq", u)])
                if u:
                    rope(u - 1)
            tiles_of_unit("ak", 0, nT, T, [("ak", 0), ("ak", 1)])
            rope(3)
            s, cnt = unit("av", 0)
            for g, (a, m) in enumerate(((0, 128), (128, 128), (256, META))):
                dst = take(("av", g), 1)
                last = group(dst[0:m, 0:256], [(nT[:, k, a:a + m], by_k(s)[:, k, :]) for k in range(KT)])
                if g < 2:
                    done(("av", g), last)
            last.then_inc(unit_used[s], 1)
            banks.full_when[("av", 2)] = (unit_used[s], cnt)
            rope(4)
            rope(5)
            tiles_of_unit("iq", 0, real, SEQ, [("iq", 0)])
            tiles_of_unit("iq", 1, real, SEQ, [("iq", 1)])
            rope(6)
            wik = ws[:, WS["ik"][0]:WS["ik"][0] + KT * 128].rearrange("p (k n) -> p k n", n=128)
            wiw = ws[:, WS["iw"][0]:WS["iw"][0] + KT * 8].rearrange("p (k n) -> p k n", n=8)
            dst = take("ik")
            done("ik", group(dst[:, 0:T], [(wik[:, k, :], nT[:, k, :]) for k in range(KT)]))
            dst = take("iw")
            for qt in range(2):
                a = META + qt * 128
                last = group(dst[:, qt * 8:(qt + 1) * 8], [(nT[:, k, a:a + 128], wiw[:, k, :]) for k in range(KT)])
            done("iw", last)
            rope(7)
            rope(8)

            pe.wait_ge(roped_ready, 9)
            for qt, h in ATT:
                a = 64 * (h % 2)
                dst = take(("ix", qt, h))
                done(("ix", qt, h), nc.tensor.matmul(dst[:, 0:nkeys(qt)], iq[a:a + 64, h // 2, qt * 128:(qt + 1) * 128],
                                                     ik[a:a + 64, 0:nkeys(qt)], start=True, stop=True))
            pe.wait_ge(y_ready, 1)
            for u in range(4):
                tiles_of_unit("gate_a", u, real, SEQ, [("gate_a", u)])
                tiles_of_unit("bg", u, y_gdn, SEQ, [("bg", u)])

            def att_logits(n):
                qt, h = ATT[n]
                dst = take(("lg", n))
                done(("lg", n), nc.tensor.matmul(dst[:, 0:nkeys(qt)], aq[:, h, qt * 128:(qt + 1) * 128],
                                                 ak[:, h // 4, 0:nkeys(qt)], start=True, stop=True))

            def att_transpose(n):
                qt, h = ATT[n]
                pe.wait_ge(prob_ready, n + 1)
                dst = take(("pt", n), 1)
                for i, (a, m) in enumerate(key_tiles(qt)):
                    last = nc.tensor.transpose(dst[0:m, i * 128:(i + 1) * 128], prob[:, n % 2, a:a + m], ident)
                done(("pt", n), last)

            def att_values(n):
                qt, h = ATT[n]
                emptied(pe, ("pt", n))
                dst = take(("ao", n), 1)
                g = h // 4
                done(("ao", n), group(dst[:, 0:128], [(av[0:m, i, g * 128:(g + 1) * 128], probT[0:m, n % 2, i * 128:(i + 1) * 128])
                                                      for i, (a, m) in enumerate(key_tiles(qt))]))

            att_logits(0)
            for n in range(len(ATT) + 3):
                if n + 1 < len(ATT):
                    att_logits(n + 1)
                if 1 <= n <= len(ATT):
                    att_transpose(n - 1)
                if n >= 3:
                    att_values(n - 3)
            for u in range(4):
                tiles_of_unit("gate_b", u, real, SEQ, [("gate_b", u)])
                if u == 0:
                    emptied(pe, ("ao", len(ATT) - 1))
                tiles_of_unit("bd", u, y_dsa, SEQ, [("bd", u)])
            pe.wait_ge(merged_ready, 4)
            for u in range(4):
                tiles_of_unit("wo", u, merged, SEQ, [("wo", u)])
            pe.wait_ge(sq_ready, 15)
            feature_sum("ss_mix", sq, SEQ)
            for u in range(8, 11):
                mod_unit(u)
            pe.wait_ge(sq_ready, 16)
            feature_sum("ss_h1", sq, SEQ)
            for u in range(11, 13):
                mod_unit(u)
            def mlp_unit(kind, u, m):
                s, cnt = unit(kind, u)
                pe.wait_ge(mlp_low_ready, m + 1)
                pe.wait_ge(mlp_low_ready_g, m + 1)
                return s, cnt, [mlp_parts[:, m % 2, i, :].rearrange("p (k n) -> p k n", n=UNIT_COLS) for i in range(2)]

            def three(high, low, x):
                return [(high, x[:, 0, :]), (high, x[:, 1, :]), (low, x[:, 0, :])]

            pe.wait_ge(nM_ready, 1)
            for u in range(16):
                s, cnt, (w_high, w_low) = mlp_unit("up", u, u)
                dst = take(("up", u), 1)
                for j in range(2):
                    c = slice(j * 128, (j + 1) * 128)
                    last = group(dst[:, j * SEQ:(j + 1) * SEQ],
                                 [p for k in range(KT) for p in three(w_high[:, k, c], w_low[:, k, c], nMs[:, k, :, :])])
                last.then_inc(unit_used[s], 1)
                banks.full_when[("up", u)] = (unit_used[s], cnt)
                if u == 0:
                    mod_columns(8, 13)
            for cp in range(4):
                dst = take(("down", cp))
                for kg in range(4):
                    if cp == 0:
                        pe.wait_ge(up_ready, 4 * kg + 4)
                    s, cnt, (w_high, w_low) = mlp_unit("down", cp * 4 + kg, 16 + cp * 4 + kg)
                    for j in range(2):
                        c = slice(j * 128, (j + 1) * 128)
                        for k in range(KT):
                            for i, (w, x) in enumerate(three(w_high[:, k, c], w_low[:, k, c], up[:, kg * KT + k, :, :])):
                                last = nc.tensor.matmul(dst[:, j * SEQ:(j + 1) * SEQ], w, x, start=(kg == 0 and j == 0 and k == 0 and i == 0),
                                                        stop=(kg == 3 and k == KT - 1 and i == 2), skip_group_check=True)
                    last.then_inc(unit_used[s], 1)
                banks.full_when[("down", cp)] = (unit_used[s], cnt)
                if cp == 0:
                    pe.wait_ge(sq_ready, 17)
                    feature_sum("ss_ctx", sq, CTX)
            pe.wait_ge(lamp_ready, 1)
            dst = take("lam")
            done("lam", nc.tensor.matmul(dst[:, 0:2], ones[0:64, :], lam[0:64, 4:6], start=True, stop=True))
            pe.wait_ge(sq_ready, 18)
            feature_sum("ss_mlp", sq, SEQ)
            for u in range(13, 16):
                mod_unit(u)

            pe.wait_ge(sq_ready, 19)
            feature_sum("ss_x", sq1, SEQ)
            for u in range(16, 18):
                mod_unit(u)
            pe.wait_ge(hcl_ready, 1)
            lat = hcl[:, :, CTX:CTX + SEQ]
            for u in range(4):
                tiles_of_unit("q2", u, lat, SEQ, [("q2", u)])
                if u == 0:
                    mod_columns(13, 18)

            def rope2(i):
                emptied(pe, ("q2", i) if i < 4 else ("k2", 2 * (i - 4) + 1))
                src = q2[:, 2 * i:2 * i + 2, :] if i < 4 else k2[:, 2 * (i - 4):2 * (i - 4) + 2, CTX:CTX + SEQ]
                dst = take(("rot2", i))
                done(("rot2", i), nc.tensor.matmul(dst[:, :], cst2("rot_ax"), src, start=True, stop=True))

            pe.wait_ge(c2_loaded, 16)
            for u in range(4):
                tiles_of_unit("k2", u, hcl, 512, [("k2", 2 * u), ("k2", 2 * u + 1)])
                rope2(u)
            for u in range(4):
                s, cnt = unit("v2", u)
                for tp in range(2):
                    dst = take(("v2", u, tp))
                    for j in range(2):
                        a = (2 * tp + j) * 128
                        last = group(dst[:, j * 256:(j + 1) * 256], [(hcl[:, k, a:a + 128], by_k(s)[:, k, :]) for k in range(KT)])
                    if tp == 0:
                        done(("v2", u, 0), last)
                last.then_inc(unit_used[s], 1)
                banks.full_when[("v2", u, 1)] = (unit_used[s], cnt)
                rope2(4 + u)
            for u in range(2):
                tiles_of_unit("f2", u, lat, SEQ, [("f2", u)])

            def scores2(n):
                qt, h = ATT[n]
                for i in range(2):
                    dst = take(("s2", n, i), 2)
                    done(("s2", n, i), nc.tensor.matmul(dst[:, :], q2[64 * i:64 * i + 64, h, qt * 128:(qt + 1) * 128],
                                                        k2[64 * i:64 * i + 64, h, :], start=True, stop=True))

            def transpose2(n):
                pe.wait_ge(prob_ready, len(ATT) + n + 1)
                dst = take(("at2", n))
                for i in range(4):
                    last = nc.tensor.transpose(dst[:, i * 128:(i + 1) * 128], esc[:, n % 2, 0, i * 128:(i + 1) * 128], ident)
                done(("at2", n), last)

            def values2(n):
                qt, h = ATT[n]
                emptied(pe, ("at2", n))
                dst = take(("o2", n))
                done(("o2", n), group(dst[:, 0:128], [(v2[:, i, h * 128:(h + 1) * 128], aT[:, n % 2, i * 128:(i + 1) * 128]) for i in range(4)]))

            dft_d, dft_n = cst2("dft_d"), cst2("dft_n")

            def dft_features(g):
                emptied(pe, ("f2", g // 2))
                dst = take(("z", g))
                for nt in range(2):
                    last = nc.tensor.matmul(dst[:, nt * 256:(nt + 1) * 256], f2[:, g, nt * 128:(nt + 1) * 128], dft_d, start=True, stop=True)
                done(("z", g), last)

            def dft_tokens(g):
                emptied(pe, ("z", g))
                dst = take(("four", g))
                done(("four", g), group(dst[:, 0:SEQ], [(zdft[:, g, nt, p * 128:(p + 1) * 128], dft_n[:, (2 * nt + p) * SEQ:(2 * nt + p + 1) * SEQ])
                                                        for nt in range(2) for p in range(2)]))

            pe.wait_ge(roped2_ready, 8)
            scores2(0)
            for n in range(len(ATT) + 3):
                if n + 1 < len(ATT):
                    scores2(n + 1)
                if 2 <= n < 6:
                    dft_features(n - 2)
                if 4 <= n < 8:
                    dft_tokens(n - 4)
                if 1 <= n <= len(ATT):
                    transpose2(n - 1)
                if n >= 3:
                    values2(n - 3)
            pe.wait_ge(sq_ready, 20)
            for j in range(4):
                dst = take(("hss", j))
                done(("hss", j), nc.tensor.matmul(dst[:, :], ones, sq1[:, 2 * j:2 * j + 2, :], start=True, stop=True))
            def four_out(u):
                s = four_slot[0]
                w = by_k(s[0], 512)
                dst = take(("fo", u))
                for j in range(2):
                    a = (u % 2) * 256 + j * 128
                    last = group(dst[:, j * SEQ:(j + 1) * SEQ], [(w[:, k, a:a + 128], four[:, k, :]) for k in range(4)])
                if u % 2:
                    last.then_inc(unit_used[s[0]], 1)
                    banks.full_when[("fo", u)] = (unit_used[s[0]], s[1])
                else:
                    done(("fo", u), last)

            four_slot = [None]
            for u in range(4):
                tiles_of_unit("gate2a", u, lat, SEQ, [("gate2a", u)])
                if u == 0:
                    mod_unit(18)
                    mod_unit(19)
                    pe.wait_ge(heads_ready, 1)
                    emptied(pe, ("four", 3))
                tiles_of_unit("ao", u, heads, SEQ, [("ao2", u)])
                if u == 0:
                    mod_columns(18, 20)
                tiles_of_unit("gate2f", u, lat, SEQ, [("gate2f", u)])
                if u % 2 == 0:
                    four_slot[0] = unit("fo", u // 2)
                four_out(u)
            pe.wait_ge(merged2_ready, 4)
            for u in range(4):
                tiles_of_unit("wo2", u, merged2, SEQ, [("wo2", u)])
            pe.wait_ge(sq_ready, 21)
            feature_sum("ss_x1", sq2, SEQ)
            for u in range(20, 24):
                mod_unit(u)
            pe.wait_ge(h2_ready, 1)
            pe.wait_ge(wr_loaded, 16)
            dst = take("router")
            for qt in range(2):
                last = group(dst[:, qt * 20:(qt + 1) * 20], [(h2[:, k, qt * 128:(qt + 1) * 128], wr[:, k, :]) for k in range(KT)])
            done("router", last)
            for qt in range(2):
                for i in range(2):
                    dst = take(("ht", qt, i))
                    for j in range(4):
                        last = nc.tensor.transpose(dst[:, j * 128:(j + 1) * 128], h2[:, 4 * i + j, qt * 128:(qt + 1) * 128], ident)
                    done(("ht", qt, i), last)
            mod_columns(20, 24)
            pe.wait_ge(routed_ready, 1)
            dst = take("rank")
            m0, m1, earlier = rt[:, 20, 0:N_EXP], rt[:, 21, 0:N_EXP], cst2("earlier")
            group(dst[:, 0:16], [(earlier, m0)])
            group(dst[:, 16:32], [(ones, m0), (earlier, m1)])
            done("rank", group(dst[:, 32:48], [(ones, m0), (ones, m1)]))

            for b in range(8):
                pe.wait_ge(banks.free[b], banks.freed[b])
            pe.wait_ge(ys_ready, 4)
            acc = psum[4:8]
            for b in range(4):
                last = nc.tensor.matmul(acc[b][:, :], yb[:, 0, 0:128], yb[:, 1, 0:512], start=True, stop=False, skip_group_check=True)
                last.then_inc(parts_used, 1)

            def unit_parts(n, i):
                pe.wait_ge(*low_part_of(n, i))
                return parts[:, i % SPLITS, 0, :], parts[:, i % SPLITS, 1, :]

            def up_product(n, j, units):
                into = ((1, 2), (0, 3))[j]
                for q in units:
                    high_low = [w.rearrange("p (k n) -> p k n", n=UNIT_COLS) for w in unit_parts(n, 4 * j + q)]
                    dst = psum[into[q // 2]][:, (q % 2) * 256:(q % 2 + 1) * 256]
                    group(dst, [(xs[:, k, j, :], w[:, k, :]) for k in range(KT) for w in high_low]).then_inc(parts_used, 1)

            def fold_rows(j):
                for t in range(8):
                    last = nc.tensor.matmul(psum[1 + j][:, t * CAP:(t + 1) * CAP], yb[:, j, t * 128:(t + 1) * 128], fold[:, :], start=True, stop=True)
                last.then_inc(folded[j], 1)

            def down_product(n, j):
                into = ((0, 3), (1, 2))[j]
                for q in range(2):
                    high_low = [w.rearrange("p (k n) -> p k n", n=512) for w in unit_parts(n, 8 + 2 * j + q)]
                    group(psum[into[q]][:, :], [(hids[:, j, k, :], w[:, k, :]) for k in range(4) for w in high_low]).then_inc(parts_used, 1)

            def scatter(j):
                for ft in range(KT):
                    last = nc.tensor.matmul(acc[ft // 2][:, (ft % 2) * SEQ:(ft % 2 + 1) * SEQ], yb[:, j, ft * 128:(ft + 1) * 128], spread[:, j, :],
                                            start=False, stop=False, skip_group_check=True)
                return last

            def expert_pass(pair, n):
                pe.wait_ge(pick_ready, n * 8 + 4)
                pe.wait_ge(ys_ready, n * 4 + 2)
                for ft in range(KT):
                    last = group(psum[0 if ft < 4 else 3][:, (ft % 4) * 2 * CAP:(ft % 4 + 1) * 2 * CAP],
                                 [(h2tok[:, qt, ft * 128:(ft + 1) * 128], pick[:, qt, :]) for qt in range(2)])
                last.then_inc(gathered, 1)
                scatter(0)
                pe.wait_ge(ys_ready, n * 4 + 4)
                scatter(1)
                pe.wait_ge(xs_ready, n + 1)
                pe.wait_ge(pick_ready, n * 8 + 8)
                for j in range(2):
                    for qt in range(2):
                        last = nc.tensor.transpose(psum[3][:, j * SEQ + qt * 128:j * SEQ + (qt + 1) * 128],
                                                   pick_gated[:, qt, j, :, :].rearrange("p a b -> p (a b)"), ident)
                last.then_inc(spread_full, 1)
                up_product(n, 0, range(4))
                pe.wait_ge(spread_ready, n + 1)
                up_product(n, 1, range(2))
                pe.wait_ge(yb_ready, n * 4 + 2)
                fold_rows(0)
                up_product(n, 1, range(2, 4))
                pe.wait_ge(yb_ready, n * 4 + 4)
                fold_rows(1)
                pe.wait_ge(hid_ready[0], n + 1)
                down_product(n, 0)
                pe.wait_ge(hid_ready[1], n + 1)
                down_product(n, 1)

            assert at[0] == FIRST_EXPERT
            total = each_pass(pe, expert_pass)
            pe.wait_ge(ys_ready, total * 4 + 4)
            scatter(0)
            scatter(1).then_inc(scattered, 1)
            pe.wait_ge(sq_ready, 22)
            dst = take("ss_out", bank=0)
            done("ss_out", group(dst[:, 0:SEQ], [(ones, sq2[:, k, :]) for k in range(KT)]))

        @block.sync
        def _(sp):
            sp.dma_start(qc[:, :, :], h_in).then_inc(h_loaded, 16)
            sp.dma_start(sm[:, :], sm_in).then_inc(sm_loaded, 16)
            for s in range(SLOTS):
                if s == 2:
                    sp.dma_start(c1[:, :], c1_in).then_inc(c1_loaded, 16)
                sp.dma_start(ring[:, s, :], stream[s]).then_inc(unit_loaded[s], 16)
            with sp.Fori(1, BASE + 1) as i:
                for s in range(SLOTS):
                    sp.wait_ge(unit_used[s], i)
                    sp.dma_start(ring[:, s, :], stream[i * SLOTS + s]).then_inc(unit_loaded[s], 16)
            for s in range(SLOTS):
                sp.wait_ge(*low_part_of(0, s))
                sp.dma_start(ring[:, s, :], stream[(BASE + 1) * SLOTS + s]).then_inc(unit_loaded[s], 16)
            sp.wait_ge(plan_ready, 1)
            total = sp.value_load(plan[0:1, MAX_PASSES:MAX_PASSES + 1], min_val=PAIRS, max_val=MAX_PASSES)
            with sp.Fori(1, total) as n:
                pair = sp.value_load(plan[0:1, bass.ds(n, 1)], min_val=0, max_val=PAIRS - 1)
                for half in range(2):
                    for s in range(SLOTS):
                        sp.wait_ge(*low_part_of(n - 1 + half, (1 - half) * SLOTS + s))
                        sp.dma_start(ring[:, s, :], stream[pair * EXPERT_UNITS + ((BASE + half) * SLOTS + s)]).then_inc(unit_loaded[s], 16)
            sp.wait_ge(out_ready, 1)
            sp.dma_start(out, mix2[:, :, :]).then_inc(out_stored, 16)
            sp.wait_ge(out_stored, 16)

        @block.gpsimd
        def _(pool):
            pool.dma_start(ws[:, :], ws_in).then_inc(ws_loaded, 16)
            pool.dma_start(hT[:, :, :], h_in[:, :, META:T]).then_inc(res_loaded, 16)
            pool.dma_start(wr[:, :, :], wr_in).then_inc(wr_loaded, 16)
            pool.dma_start(lam[0:64, 0:4], lam_in).then_inc(lam_loaded, 16)
            emptied(pool, ("GB", H - 1))
            for n, (l, g) in enumerate(LEVEL_ITEMS):
                if n >= 2:
                    pool.wait_ge(*banks.full_when[("P", n - 2)])
                a, _w = C1["levels"]
                m = c1[:, a + 128 * l:a + 128 * (l + 1)]
                if g == 4:
                    nc.gpsimd.tensor_tensor(masked[:, n % 2, 0:128], metas[:, 5, :], m, mul).then_inc(masked_ready, 1)
                else:
                    nc.gpsimd.tensor_tensor(masked[:, n % 2, :].rearrange("p (a b) -> p a b", b=128), low[:, 4 * g:4 * g + 4, :],
                                            m.unsqueeze(1).to_broadcast([128, 4, 128]), mul).then_inc(masked_ready, 1)
            pool.wait_ge(merged_ready, 4)
            pool.dma_start(ctxT[:, :, :], ctx_in).then_inc(ctx_loaded, 16)
            pool.dma_start(c2[:, :], c2_in).then_inc(c2_loaded, 16)
            for m in range(MLP_UNITS):
                pool.wait_ge(mlp_high_ready, m + 1)
                a = KT * UNIT_COLS - G_COLS
                nc.gpsimd.tensor_tensor(mlp_parts[:, m % 2, 1, a:], ring[:, (MLP_FIRST + m) % SLOTS, a:],
                                        mlp_parts[:, m % 2, 0, a:], sub).then_inc(mlp_low_ready_g, 1)

            def expert_pass(pair, n):
                for i in range(G_FIRST, EXPERT_UNITS, G_EVERY):
                    pool.wait_ge(high_ready, n * EXPERT_UNITS + (i + 1))
                    nc.gpsimd.tensor_tensor(parts[:, i % SPLITS, 1, :], ring[:, i % SLOTS, :], parts[:, i % SPLITS, 0, :], sub).then_inc(low_ready_g, 1)

            each_pass(pool, expert_pass)

        @block.scalar
        def _(act):
            step = Steps(act, act_step)
            A = nc.scalar.activation

            def evac(name, dst, width, scale=1.0):
                src = full(act, name)[0:dst.shape[0], 0:width]
                if len(dst.shape) == 3:
                    src = src.rearrange("p (a b) -> p a b", b=dst.shape[2])
                A(dst, src, ACT.Copy, scale=scale).then_inc(free(name), 1)

            def evac_mod(u):
                evac(("mod_row", u), mod_rows[:, u % MOD_SLOTS, :], UNIT_COLS)

            def mod_columns(a, b):
                evac(("mod", a), modT[:, 2 * a:2 * b, :], 4 * (b - a))

            def rms_root(name, n, dst, width=D):
                A(dst, full(act, name)[:, 0:n], ACT.Sqrt, bias=eps, scale=1.0 / width).then_inc(free(name), 1)

            act.wait_ge(sm_loaded, 16)
            A(a1[:, :, :], small("c").rearrange("p (k n) -> p k n", n=2), ACT.Sigmoid).then_inc(sig_ready, 1)
            act.wait_ge(h_loaded, 16)
            A(vc[:, :, :], qc[:, :, :], ACT.Square).then_inc(sq_ready, 1)
            act.wait_ge(ones_ready, 1)
            rms_root("ss_in", T, root[:, :])
            def l2_square(i):
                n = T if i < 8 else 512
                act.wait_ge(silu_ready, L2_AFTER[i] % 8 + 2 if i < 8 else L2_AFTER[i] + 2)
                src = kc[:, i, :] if i < 8 else qc[:, 2 * (i - 8):2 * (i - 8) + 2, META:T]
                dst = masked[:, i % 2, 0:n]
                if i >= 2:
                    act.wait_ge(*banks.full_when[("l2", i - 2)])
                A(dst if i < 8 else dst.rearrange("p (a b) -> p a b", b=SEQ), src, ACT.Square).then_inc(sq_ready, 1)

            def l2_root(i):
                n = T if i < 8 else 512
                if i >= 2:
                    act.wait_ge(normed_ready, i - 1)
                A(prod[:, i % 2, 0:n], full(act, ("l2", i))[:, 0:n], ACT.Sqrt, bias=eps).then_inc(free(("l2", i)), 1)

            for t in range(24):
                kind, j = CONV_TILES[t]
                emptied(act, (kind, j))
                if t >= 2:
                    act.wait_ge(silu_ready, t)
                A(scr[:, t % 2, 0:T], conv_dst(t), ACT.Sigmoid).then_inc(sig_ready, 1)
                for i in range(12):
                    if L2_AFTER[i] == t - 1:
                        l2_square(i)
                    if L2_AFTER[i] == t - 6:
                        l2_root(i)
            l2_square(11)
            l2_root(9)
            bank = full(act, "gba")
            A(tok[:, 0, :].rearrange("p (g n) -> p g n", n=8), bank[:, 0:48].rearrange("p (g n) -> p g n", n=16)[:, :, 0:8],
              ACT.Sigmoid).then_inc(free("gba"), 1)
            l2_root(10)
            l2_root(11)
            for u in range(6):
                evac_mod(u)
            act.wait_ge(absx_ready, 1)
            step(A(tok[:, 2, :], tok[:, 2, :], ACT.Exp, scale=-1.0))
            step(A(tok[:, 7, 0:8], small("a_log"), ACT.Exp))
            step.settle()
            A(tok[:, 2, :], tok[:, 2, :], ACT.Ln, bias=1.0).then_inc(softplus_ready, 1)
            A(tok[:, 5, 0:16], full(act, "gct")[:, 0:16], ACT.Exp).then_inc(free("gct"), 1)
            act.wait_ge(meta_arg_ready, 1)
            A(metas[:, 4, :], metas[:, 4, :], ACT.Exp).then_inc(meta_exp_ready, 1)
            mod_columns(0, 6)
            for h in range(H + 1):
                if h < H:
                    act.wait_ge(decay_arg_ready, h + 1)
                    A(scr[:, h % 2, 256:512], full(act, ("GB", h))[:, 0:256], ACT.Exp).then_inc(free(("GB", h)), 1)
                    A(scr[:, h % 2, 0:256], scr[:, h % 2, 0:256], ACT.Exp).then_inc(decay_exp_ready, 1)
                if h >= 1:
                    g = h - 1
                    emptied(act, ("KQ", g))
                    bank = full(act, ("TR", g))
                    for ci in range(NCH):
                        sy = g * NCH + ci
                        step(A(k_tail[:, sy, :], bank[:, ci * 128:(ci + 1) * 128], ACT.Copy, scale=scr[:, g % 2, ci * 128 + 127:ci * 128 + 128]))
                        ins = A(v_beta[:, sy, :], bank[:, 256 + ci * 128:384 + ci * 128], ACT.Copy, scale=tok[:, 0, 8 + 8 * ci + g:9 + 8 * ci + g])
                        if ci == NCH - 1:
                            ins.then_inc(free(("TR", g)), 1)
            evac_mod(6)
            evac_mod(7)
            for n, (l, g) in enumerate(LEVEL_ITEMS):
                w = 512 if g < 4 else 128
                if n >= 2:
                    act.wait_ge(*banks.full_when[("QT", n - 2)])
                    if LEVEL_ITEMS[n - 2][0] == 0:
                        emptied(act, ("QT", n - 2))
                evac(("P", n), prod[:, n % 2, 0:w], w)
            evac("meta_v", metas[:, 3, :], 128)
            for hg in range(2):
                evac(("S0", hg), state[:, 0, hg * 512:(hg + 1) * 512], 512)
            mod_columns(6, 8)
            for ci in range(NCH):
                for hg in range(2):
                    evac(("vn", ci, hg), scr[:, hg, 512:1024], 512)
                for hg in range(2):
                    evac(("o", ci, hg), y_gdn[:, hg * 4:hg * 4 + 4, ci * 128:(ci + 1) * 128], 512)
            for u in range(4):
                A(inv[:, 4 * u:4 * u + 4, :], full(act, ("gz", u))[:, :].rearrange("p (a b) -> p a b", b=128), ACT.Sigmoid).then_inc(sig_ready, 1)
                act.wait_ge(sig_ready, 26 + u)
                A(k_tail[:, 4 * u:4 * u + 4, :], full(act, ("gz", u))[:, :].rearrange("p (a b) -> p a b", b=128), ACT.Copy).then_inc(free(("gz", u)), 1)
            emptied(act, ("o", NCH - 1, 1))
            A(low[:, :, :], y_gdn[:, :, :].rearrange("p h (c s) -> p (h c) s", s=128), ACT.Square).then_inc(sq_ready, 1)
            for j in range(4):
                rms_root(("yss", j), 512, attn[:, 4 * j:4 * j + 4, :].rearrange("p a b -> p (a b)"), 128)
            act.wait_ge(y_ready, 1)
            for u in range(4):
                evac(("aq", u), aq[:, 2 * u:2 * u + 2, :], 512)
            for j in range(2):
                evac(("ak", j), ak[:, j, :], T)
            for g, m in enumerate((128, 128, META)):
                evac(("av", g), av[0:m, g, :], 256)
            for u in range(2):
                evac(("iq", u), iq[:, 2 * u:2 * u + 2, :], 512)
            evac("ik", ik[:, :], T)
            evac("iw", iw[:, :, :], 16, float(H * 64) ** -0.5)
            for n, (qt, h) in enumerate(ATT):
                if n >= 2:
                    act.wait_ge(score_ready, n - 1)
                A(relu[:, n % 2, 0:nkeys(qt)], full(act, ("ix", qt, h))[:, 0:nkeys(qt)], ACT.Relu).then_inc(free(("ix", qt, h)), 1)
            for u in range(4):
                if u >= 2:
                    emptied(act, ("bg", u - 2))
                A(gate[:, u % 2, :], full(act, ("gate_a", u))[:, :], ACT.Sigmoid).then_inc(free(("gate_a", u)), 1)
            for n in range(len(ATT) + 4):
                if n < len(ATT):
                    qt, h = ATT[n]
                    act.wait_ge(nmax_ready, n + 1)
                    if n >= 2:
                        act.wait_ge(*banks.full_when[("pt", n - 2)])
                    A(prob[:, n % 2, 0:nkeys(qt)], lmask[:, n % 2, 0:nkeys(qt)], ACT.Exp, bias=stat[:, n % 2, 0:1],
                      accum_out=stat[:, n % 2, 1:2]).then_inc(pexp_ready, 1)
                if 2 <= n < len(ATT) + 2:
                    k = n - 2
                    qt, h = ATT[k]
                    bank = full(act, ("pt", k))
                    if k >= 2:
                        act.wait_ge(*banks.full_when[("ao", k - 2)])
                    nt = len(key_tiles(qt)) - 1
                    step(A(probT[:, k % 2, 0:nt * 128], bank[:, 0:nt * 128], ACT.Copy))
                    A(probT[0:META, k % 2, nt * 128:(nt + 1) * 128], bank[0:META, nt * 128:(nt + 1) * 128], ACT.Copy).then_inc(free(("pt", k)), 1)
                if n >= 4:
                    qt, h = ATT[n - 4]
                    evac(("ao", n - 4), y_dsa[:, h, qt * 128:(qt + 1) * 128], 128)
            for u in range(4):
                if u >= 2:
                    emptied(act, ("bd", u - 2))
                A(gate[:, u % 2, :], full(act, ("gate_b", u))[:, :], ACT.Sigmoid).then_inc(free(("gate_b", u)), 1)
            for u in range(4):
                bank = full(act, ("wo", u))[:, :].rearrange("p (a b) -> p a b", b=SEQ)
                ins = A(sq[:, 2 * u:2 * u + 2, :], bank, ACT.Square)
                if u == 3:
                    ins.then_inc(sq_ready, 1)
                evac(("wo", u), mix[:, 2 * u:2 * u + 2, :], 512)
            rms_root("ss_mix", SEQ, root[:, 0:SEQ])
            for u in range(8, 11):
                evac_mod(u)
            act.wait_ge(h1_ready, 1)
            A(sq[:, :, :], hT[:, :, :], ACT.Square).then_inc(sq_ready, 1)
            rms_root("ss_h1", SEQ, root[:, 0:SEQ])
            for u in range(11, 13):
                evac_mod(u)
            def mlp_high(m):
                s, n = ring_unit(MLP_FIRST + m)
                act.wait_ge(unit_loaded[s], 16 * n)
                if m >= 2:
                    mlp_unit_used(act, m - 2)
                A(mlp_parts[:, m % 2, 0, :], ring[:, s, :], ACT.Copy).then_inc(mlp_high_ready, 1)

            act.wait_ge(ctx_loaded, 16)
            mlp_high(0)
            mlp_high(1)
            for u in range(16):
                mlp_high(u + 2)
                if u >= 2:
                    act.wait_ge(up_ready, u - 1)
                A(hidden_now[:, u % 2, :], full(act, ("up", u))[:, :], ACT.Relu).then_inc(free(("up", u)), 1)
                emptied(act, ("up", u))
                A(up[:, 2 * u:2 * u + 2, 0, :], hidden_now[:, u % 2, :].rearrange("p (a b) -> p a b", b=SEQ), ACT.Square).then_inc(hid_high_ready, 1)
                if u == 0:
                    mod_columns(8, 13)
            A(sq[:, :, :], ctxT[:, :, :], ACT.Square).then_inc(sq_ready, 1)
            for m in range(16, 32):
                if m + 2 < MLP_UNITS:
                    mlp_high(m + 2)
                if m == 19:
                    rms_root("ss_ctx", CTX, root[:, 0:CTX])
                if m % 4 == 3:
                    cp = (m - 16) // 4
                    bank = full(act, ("down", cp))[:, :].rearrange("p (a b) -> p a b", b=SEQ)
                    ins = A(sq[:, 2 * cp:2 * cp + 2, :], bank, ACT.Square)
                    if cp == 3:
                        ins.then_inc(sq_ready, 1)
                    evac(("down", cp), mix[:, 2 * cp:2 * cp + 2, :], 512)
            A(lam[:, 6:8], full(act, "lam")[:, 0:2], ACT.Exp).then_inc(free("lam"), 1)
            act.wait_ge(h1_ready, 2)
            rms_root("ss_mlp", SEQ, root[:, 0:SEQ])
            for u in range(13, 16):
                evac_mod(u)

            act.wait_ge(h1_ready, 3)
            A(sq1[:, :, :], hT[:, :, :], ACT.Square).then_inc(sq_ready, 1)
            rms_root("ss_x", SEQ, root[:, 0:SEQ])
            for u in range(16, 18):
                evac_mod(u)
            for u in range(4):
                evac(("q2", u), q2[:, 2 * u:2 * u + 2, :], 512)
                if u == 0:
                    mod_columns(13, 18)
            for u in range(4):
                evac(("k2", 2 * u), k2[:, 2 * u, :], 512)
                evac(("k2", 2 * u + 1), k2[:, 2 * u + 1, :], 512)
            for u in range(4):
                for tp in range(2):
                    evac(("v2", u, tp), v2[:, 2 * tp:2 * tp + 2, u * 256:(u + 1) * 256], 512)
            for u in range(2):
                evac(("f2", u), f2[:, 2 * u:2 * u + 2, :], 512)
            for n in range(len(ATT) + 4):
                if n < len(ATT):
                    act.wait_ge(nmax_ready, len(ATT) + n + 1)
                    if n >= 2:
                        act.wait_ge(*banks.full_when[("at2", n - 2)])
                    for i in range(2):
                        A(esc[:, n % 2, i, :], full(act, ("s2", n, i))[:, :], ACT.Exp, bias=stat2[:, n % 2, 2 + i:3 + i], scale=0.125,
                          accum_out=stat2[:, n % 2, 4 + i:5 + i]).then_inc(free(("s2", n, i)), 1)
                if 2 <= n < 6:
                    evac(("z", n - 2), zdft[:, n - 2, :, :], 512)
                if 4 <= n < 8:
                    evac(("four", n - 4), four[:, n - 4, :], SEQ)
                if 2 <= n < len(ATT) + 2:
                    k = n - 2
                    if k >= 2:
                        act.wait_ge(*banks.full_when[("o2", k - 2)])
                    evac(("at2", k), aT[:, k % 2, :], 512)
                if n >= 4:
                    qt, h = ATT[n - 4]
                    evac(("o2", n - 4), heads[:, h, qt * 128:(qt + 1) * 128], 128)
            emptied(act, ("o2", len(ATT) - 1))
            A(sq1[:, :, :], heads[:, :, :], ACT.Square).then_inc(sq_ready, 1)
            for j in range(4):
                rms_root(("hss", j), 512, q2[:, 2 * j:2 * j + 2, :].rearrange("p a b -> p (a b)"), 128)
            for u in range(4):
                if u >= 1:
                    act.wait_ge(merged2_ready, u)
                A(gate2[:, 0, :], full(act, ("gate2a", u))[:, :], ACT.Sigmoid).then_inc(free(("gate2a", u)), 1)
                if u == 0:
                    evac_mod(18)
                    evac_mod(19)
                    mod_columns(18, 20)
                A(gate2[:, 1, :], full(act, ("gate2f", u))[:, :], ACT.Sigmoid).then_inc(free(("gate2f", u)), 1)
            emptied(act, ("wo2", 3))
            A(sq2[:, :, :], hT[:, :, :], ACT.Square).then_inc(sq_ready, 1)
            rms_root("ss_x1", SEQ, root[:, 0:SEQ])
            for u in range(20, 24):
                evac_mod(u)
            act.wait_ge(rexp_arg_ready, 1)
            A(rflat(80, 8), rflat(80, 8), ACT.Exp).then_inc(rexp_ready, 1)
            act.wait_ge(rexp_arg_ready, 2)
            A(rflat(180, 2), rflat(180, 2), ACT.Exp).then_inc(rexp_ready, 1)
            for qt in range(2):
                for i in range(2):
                    evac(("ht", qt, i), h2tok[:, qt, i * 512:(i + 1) * 512], 512)
            mod_columns(20, 24)

            def expert_pass(pair, n):
                def high(i):
                    act.wait_ge(unit_loaded[i % SLOTS], n * 32 + 16 * (BASE + 1 + i // SLOTS))
                    act.wait_ge(parts_used, n * EXPERT_UNITS + (i + 1))
                    A(parts[:, i % SPLITS, 0, :], ring[:, i % SLOTS, :], ACT.Copy).then_inc(high_ready, 1)

                def products(j):
                    act.wait_ge(parts_used, n * EXPERT_UNITS + (SPLITS + 4 * j + 4))
                    for i, b in enumerate(((1, 2), (0, 3))[j]):
                        A(yb[:, j, i * 512:(i + 1) * 512], psum[b][:, :], ACT.Copy).then_inc(yb_ready, 1)

                def sigmoid(j):
                    act.wait_ge(folded[j], n + 1)
                    A(sg[:, j, :], psum[1 + j][:, 0:4 * CAP], ACT.Sigmoid).then_inc(sig_w1_ready[j], 1)

                def outputs(j):
                    act.wait_ge(parts_used, n * EXPERT_UNITS + (SPLITS + 8 + 2 * j + 2))
                    for i, b in enumerate(((0, 3), (1, 2))[j]):
                        A(yb[:, j, i * 512:(i + 1) * 512], psum[b][:, :], ACT.Copy).then_inc(ys_ready, 1)

                high(0)
                high(1)
                high(2)
                act.wait_ge(spread_full, n + 1)
                A(spread[:, :, :], psum[3][:, :].rearrange("p (a b) -> p a b", b=SEQ), ACT.Copy).then_inc(spread_ready, 1)
                high(3)
                high(4)
                high(5)
                high(6)
                products(0)
                high(7)
                high(8)
                sigmoid(0)
                high(9)
                high(10)
                products(1)
                high(11)
                sigmoid(1)
                outputs(0)
                outputs(1)

            each_pass(act, expert_pass)
            act.wait_ge(h1_ready, 4)
            A(sq2[:, :, :], hT[:, :, :], ACT.Square).then_inc(sq_ready, 1)
            rms_root("ss_out", SEQ, root[:, 0:SEQ])

        @block.vector
        def _(dve):
            step = Steps(dve, dve_step)
            TT, TS, STT, CP = nc.vector.tensor_tensor, nc.vector.tensor_scalar, nc.vector.scalar_tensor_tensor, nc.vector.tensor_copy

            def split(ap, b):
                return ap.rearrange("p (a b) -> p a b", b=b)

            def over(ap, n):
                return ap.unsqueeze(1).to_broadcast([ap.shape[0], n, ap.shape[1]])

            def each(ap, n):
                return ap.unsqueeze(2).to_broadcast([ap.shape[0], ap.shape[1], n])

            def inv_rms(name, n):
                emptied(dve, name)
                step(nc.vector.reciprocal(rB[:, 0:n], root[:, 0:n]))
                step.settle()

            def scaled(dst, src, gains, n, last_sem=None):
                for k in range(KT):
                    ins = STT(dst[:, k, :], src[:, k, :], gains[:, k:k + 1], rB[:, 0:n], mul, mul)
                    if k == KT - 1 and last_sem is not None:
                        ins.then_inc(last_sem, 1)
                    else:
                        step(ins)

            step(nc.vector.memset(ones[:, :], 1.0))
            nc.vector.memset(eps, EPS).then_inc(ones_ready, 1)
            dve.wait_ge(sm_loaded, 16)
            dve.wait_ge(sig_ready, 1)
            TT(silu_c[:, :, :], small("c").rearrange("p (k n) -> p k n", n=2), a1[:, :, :], mul).then_inc(silu_ready, 1)
            inv_rms("ss_in", T)
            scaled(nT, qc, small("g_pre_mix"), T, nT_ready)
            def silu(t):
                dve.wait_ge(sig_ready, t + 2)
                TT(conv_dst(t), conv_dst(t), scr[:, t % 2, 0:T], mul).then_inc(silu_ready, 1)

            def l2_norm(i):
                n = T if i < 8 else 512
                emptied(dve, ("l2", i))
                r = prod[:, i % 2, 0:n]
                step(nc.vector.reciprocal(r, r))
                step.settle()
                if i < 8:
                    TT(kc[:, i, :], kc[:, i, :], r, mul).then_inc(normed_ready, 1)
                else:
                    q = qc[:, 2 * (i - 8):2 * (i - 8) + 2, META:T]
                    STT(q, q, 128.0 ** -0.5, split(r, SEQ), mul, mul).then_inc(normed_ready, 1)

            for t in range(24):
                kind, j = CONV_TILES[t]
                bank = full(dve, (kind, j))
                dst = conv_dst(t)
                a = SM["conv"][0] + 4 * ({"gq": 0, "gk": 8, "gv": 16}[kind] + j)
                step(TS(dst, bank[:, 0:T], sm[:, a + 3:a + 4], None, mul))
                for back in (1, 2, 3):
                    step.settle()
                    ins = STT(dst[:, back:T], bank[:, 0:T - back], sm[:, a + 3 - back:a + 4 - back], dst[:, back:T], mul, add)
                    if back < 3:
                        step(ins)
                    else:
                        ins.then_inc(free((kind, j)), 1)
                if t >= 1:
                    silu(t - 1)
                for i in range(12):
                    if L2_AFTER[i] == t - 7:
                        l2_norm(i)
            silu(23)
            l2_norm(8)
            l2_norm(9)
            emptied(dve, "gba", 1)
            bank = psum[banks.at["gba"]]
            TT(tok[:, 1, :].rearrange("p (g n) -> p g n", n=8), bank[:, 0:48].rearrange("p (g n) -> p g n", n=16)[:, :, 8:16],
               over(small("dt_bias"), 3), add).then_inc(free("gba"), 1)
            emptied(dve, "gba")
            step(TS(tok[:, 3, :], tok[:, 1, :], -1.0, None, mul))
            step.settle()
            TT(tok[:, 2, :], tok[:, 1, :], tok[:, 3, :], ALU.max).then_inc(absx_ready, 1)

            l2_norm(10)
            l2_norm(11)
            dve.wait_ge(softplus_ready, 1)
            step(STT(tok[:, 4, :], tok[:, 1, :], 0.0, tok[:, 2, :], ALU.max, add))
            step.settle()
            step(STT(split(tok[:, 3, :], 8), split(tok[:, 4, :], 8), -1.0, over(tok[:, 7, 0:8], 3), mul, mul))
            step.settle()
            dve.wait_ge(normed_ready, 12)
            for ci in range(NCH):
                a = 8 * (1 + ci)
                step(CP(inv[:, :, :].rearrange("p (h c) m -> p c h m", c=NCH)[:, ci], each(tok[:, 3, a:a + 8], 128)))
                step(CP(invT[:, :, :].rearrange("p (h c) m -> p c h m", c=NCH)[:, ci], each(tok[:, 0, a:a + 8], 128)))
            step(TT(split(metas[0:META, 0, :], META), each(tok[0:META, 3, 0:8], META), over(upper[0:META, 0:META], 8), mul))
            step(TT(split(metas[0:META, 1, :], META), each(tok[0:META, 0, 0:8], META), over(ident[0:META, 0:META], 8), mul))
            step(CP(split(metas[:, 2, :], META), kc[:, :, 0:META]))
            CP(split(metas[:, 3, :], META), vc[:, :, 0:META]).then_inc(tri_ready, 1)
            emptied(dve, "gct", 1)
            TS(tok[:, 6, 0:16], psum[banks.at["gct"]][:, 0:16], -1.0, None, mul).then_inc(free("gct"), 1)
            emptied(dve, "gct")
            step(STT(tok[:, 7, 8:24], tok[:, 5, 0:16], -1.0, tok[:, 0, 8:24], mul, mul))
            bank = full(dve, "metaGB")
            step(STT(metas[:, 5, :], bank[:, 0:128], 1.0, ident, mul, mul, accum_out=mcol[:, 0:1]))
            step(STT(metas[:, 6, :], bank[:, 128:256], 1.0, ident, mul, mul, accum_out=mcol[:, 1:2]))
            step.settle()
            TS(metas[:, 4, :], bank[:, 0:128], mcol[:, 0:1], 0.0, sub, ALU.min).then_inc(meta_arg_ready, 1)
            dve.wait_ge(meta_exp_ready, 1)
            step(TT(metas[:, 4, :], metas[:, 4, :], cst("meta_upper"), mul))
            step.settle()
            kbank = full(dve, "metaK")
            step(STT(metas[:, 6, :], metas[:, 4, :], 1.0, cst("meta_last"), mul, mul, accum_out=mcol[:, 2:3]))
            step(TT(metas[:, 5, :], kbank[:, 0:128], metas[:, 4, :], mul))
            step.settle()
            TT(metas[:, 5, :], metas[:, 5, :], bank[:, 128:256], mul).then_inc(free("metaGB"), 1)
            step(TS(metas[:, 6, :], kbank[:, 128:256], mcol[:, 2:3], None, mul))
            TS(metas[:, 7, :], kbank[:, 256:384], mcol[:, 1:2], None, mul).then_inc(free("metaK"), 1)

            def decay_args(h):
                if h >= 2:
                    emptied(dve, ("TR", h - 2))
                bank = full(dve, ("GB", h))
                for ci in range(NCH):
                    ins = TS(scr[:, h % 2, ci * 128:(ci + 1) * 128], bank[:, ci * 128:(ci + 1) * 128],
                             tok[:, 6, 8 * ci + h:8 * ci + h + 1], 0.0, add, ALU.min)
                    if ci == NCH - 1:
                        ins.then_inc(decay_arg_ready, 1)
                    else:
                        step(ins)

            def decay_use(h):
                dve.wait_ge(decay_exp_ready, h + 1)
                dt = scr[:, h % 2, 0:256]
                step(TT(split(dt, 128), split(dt, 128), over(upper, 2), mul))
                step(CP(egl[:, 2 * h:2 * h + 2], split(scr[:, h % 2, 256:512], 128)[:, :, 127]))
                step.settle()
                bank = full(dve, ("KQ", h))
                step(TT(attn[:, 2 * h:2 * h + 2, :], split(bank[:, 256:512], 128), split(dt, 128), mul))
                TT(low[:, 2 * h:2 * h + 2, :], split(bank[:, 0:256], 128), split(dt, 128), mul).then_inc(free(("KQ", h)), 1)
                step(TT(qc[:, h, META:T], qc[:, h, META:T], scr[:, h % 2, 256:512], mul))
                emptied(dve, ("KQ", h))
                TT(low[:, 2 * h:2 * h + 2, :], low[:, 2 * h:2 * h + 2, :], split(full(dve, ("GB", h))[:, 256:512], 128), mul).then_inc(free(("GB", h)), 1)

            for h in range(H + 1):
                if h < H:
                    decay_args(h)
                if h >= 1:
                    decay_use(h - 1)
            emptied(dve, ("TR", H - 1))
            TT(split(scr[:, 0, :], 128), over(metas[:, 6, :], H), each(cst("head_rows"), 128), mul).then_inc(scan_ready, 1)

            def update_inverse(n):
                l, g = LEVEL_ITEMS[n]
                x = metas[:, 8:9, :] if g == 4 else inv[:, 4 * g:4 * g + 4, :]
                xt = metas[:, 9:10, :] if g == 4 else invT[:, 4 * g:4 * g + 4, :]
                w = 1 if g == 4 else 4
                if l == 0:
                    emptied(dve, ("P", n))
                    step(TT(x, over(ident, w), split(prod[:, n % 2, 0:w * 128], 128), sub))
                    TT(xt, over(ident, w), split(full(dve, ("QT", n))[:, 0:w * 128], 128), sub).then_inc(free(("QT", n)), 1)
                    return
                if ("Q", n) in banks.at:
                    TT(x, x, split(full(dve, ("Q", n))[:, 0:w * 128], 128), sub).then_inc(free(("Q", n)), 1)
                TT(xt, xt, split(full(dve, ("QT", n))[:, 0:w * 128], 128), sub).then_inc(free(("QT", n)), 1)

            for n in range(len(LEVEL_ITEMS)):
                update_inverse(n)
            for ci in range(NCH):
                for hg in range(2):
                    bank = full(dve, ("kS", ci, hg))
                    for j in range(4):
                        h = hg * 4 + j
                        ins = STT(scr[:, hg, j * 128:(j + 1) * 128], bank[:, j * 128:(j + 1) * 128], tok[:, 7, 8 + 8 * ci + h:9 + 8 * ci + h],
                                  v_beta[:, h * NCH + ci, :], mul, add)
                        if j == 3:
                            ins.then_inc(free(("kS", ci, hg)), 1)
                if ci + 1 < NCH:
                    for hg in range(2):
                        bank = full(dve, ("dS", ci, hg))
                        for j in range(4):
                            h = hg * 4 + j
                            sy = h * NCH + ci
                            ins = STT(state[:, ci + 1, h * 128:(h + 1) * 128], state[:, ci, h * 128:(h + 1) * 128], egl[:, sy:sy + 1],
                                      bank[:, j * 128:(j + 1) * 128], mul, add)
                            if j == 3:
                                ins.then_inc(free(("dS", ci, hg)), 1)
            for u in range(4):
                emptied(dve, ("gz", u))
                step(TT(inv[:, 4 * u:4 * u + 4, :], inv[:, 4 * u:4 * u + 4, :], k_tail[:, 4 * u:4 * u + 4, :], mul))
            for j in range(4):
                emptied(dve, ("yss", j))
                r = attn[:, 4 * j:4 * j + 4, :].rearrange("p a b -> p (a b)")
                yj = y_gdn[:, 2 * j:2 * j + 2, :].rearrange("p a b -> p (a b)")
                step(nc.vector.reciprocal(r, r))
                step.settle()
                step(STT(yj, yj, small("gdn_norm"), r, mul, mul))
                step.settle()
                ins = TT(yj, yj, inv[:, 4 * j:4 * j + 4, :].rearrange("p a b -> p (a b)"), mul)
                if j == 3:
                    ins.then_inc(y_ready, 1)
                else:
                    step(ins)
            for i, (kind, j) in enumerate(ROPES):
                bank = full(dve, ("rot", i))
                raw, _n = raw_of(kind, j)
                w, n = (2, SEQ) if kind in ("aq", "iq") else (1, T)
                tab = "att" if kind in ("aq", "ak") else "idx"
                if i:
                    dve.wait_ge(roped_ready, i)
                cos, sin = cst("cos_" + tab)[:, T - n:T], cst("sin_" + tab)[:, T - n:T]
                TT(split(rot1[:, 0:w * n], n), split(bank[:, 0:w * n], n), over(sin, w), mul).then_inc(free(("rot", i)), 1)
                step(TT(split(rot2[:, 0:w * n], n), raw, over(cos, w), mul))
                step.settle()
                emptied(dve, ("rot", i))
                TT(raw, split(rot1[:, 0:w * n], n), split(rot2[:, 0:w * n], n), add).then_inc(roped_ready, 1)
            emptied(dve, "iw")
            for n, (qt, h) in enumerate(ATT):
                emptied(dve, ("ix", qt, h))
                sc = score[:, qt, 0:nkeys(qt)]
                if h == 0:
                    TS(sc, relu[:, n % 2, 0:nkeys(qt)], iw[:, qt, h:h + 1], None, mul).then_inc(score_ready, 1)
                else:
                    dve.wait_ge(score_ready, n)
                    STT(sc, relu[:, n % 2, 0:nkeys(qt)], iw[:, qt, h:h + 1], sc, mul, add).then_inc(score_ready, 1)
            dve.wait_ge(score_ready, len(ATT))

            def choose(qt):
                n = nkeys(qt)
                causal = cst("causal")[:, qt * T:qt * T + n]
                step(TT(work[:, 0, 0:n], score[:, qt, 0:n], causal, add))
                for i in range(TOPK // 8):
                    step.settle()
                    step(nc.vector.max(best[:, :], work[:, i % 2, 0:n]))
                    step.settle()
                    step(nc.vector.match_replace(work[:, (i + 1) % 2, 0:n], best[:, :], work[:, i % 2, 0:n], TAKEN))
                step(TS(lmask[:, 0, 0:n], causal, 0.0, None, ALU.is_equal))
                step.settle()
                step(STT(lmask[:, 1, 0:n], work[:, (TOPK // 8) % 2, 0:n], (NEG + TAKEN) / 2, lmask[:, 0, 0:n], ALU.is_le, mul))
                step.settle()
                step(TS(bias[:, qt, 0:n], lmask[:, 1, 0:n], 1.0, 1.0e30, sub, mul))

            def merge_a(u):
                emptied(dve, ("gate_a", u))
                TT(merged[:, 2 * u:2 * u + 2, :], split(gate[:, u % 2, :], SEQ), split(full(dve, ("bg", u))[:, :], SEQ), mul).then_inc(free(("bg", u)), 1)

            choose(0)
            merge_a(0)
            merge_a(1)
            choose(1)
            merge_a(2)
            merge_a(3)
            step.settle()
            for n in range(len(ATT) + 1):
                if n < len(ATT):
                    qt, h = ATT[n]
                    w = nkeys(qt)
                    if n >= 2:
                        dve.wait_ge(pexp_ready, n - 1)
                    STT(lmask[:, n % 2, 0:w], full(dve, ("lg", n))[:, 0:w], 128.0 ** -0.5, bias[:, qt, 0:w], mul, add).then_inc(free(("lg", n)), 1)
                    emptied(dve, ("lg", n))
                    nc.vector.tensor_reduce(stat[:, n % 2, 0:1], lmask[:, n % 2, 0:w], AX, ALU.max, negate=True).then_inc(nmax_ready, 1)
                if n >= 1:
                    k = n - 1
                    w = nkeys(ATT[k][0])
                    dve.wait_ge(pexp_ready, k + 1)
                    step(nc.vector.reciprocal(stat[:, k % 2, 2:3], stat[:, k % 2, 1:2]))
                    step.settle()
                    TS(prob[:, k % 2, 0:w], prob[:, k % 2, 0:w], stat[:, k % 2, 2:3], None, mul).then_inc(prob_ready, 1)
            for u in range(4):
                emptied(dve, ("gate_b", u))
                gated = (rot1, rot2)[u % 2]
                TT(gated[:, :], gate[:, u % 2, :], full(dve, ("bd", u))[:, :], mul).then_inc(free(("bd", u)), 1)
                emptied(dve, ("bd", u))
                TT(merged[:, 2 * u:2 * u + 2, :], merged[:, 2 * u:2 * u + 2, :], split(gated[:, :], SEQ), add).then_inc(merged_ready, 1)
            dve.wait_ge(res_loaded, 16)
            inv_rms("ss_mix", SEQ)
            scaled(mix, mix, small("g_post_mix"), SEQ)
            step.settle()
            TT(hT[:, :, :], hT[:, :, :], mix[:, :, :], add).then_inc(h1_ready, 1)
            inv_rms("ss_h1", SEQ)
            dve.wait_ge(h1_ready, 1)
            scaled(nM, hT, small("g_pre_mlp"), SEQ)
            step.settle()
            step(CP(nMs[:, :, 0, :], nM[:, :, :]))
            step.settle()
            TT(nMs[:, :, 1, :], nM[:, :, :], nMs[:, :, 0, :], sub).then_inc(nM_ready, 1)
            dve.wait_ge(lam_loaded, 16)
            step(TT(lam[0:64, 4:5], lam[0:64, 0:1], lam[0:64, 1:2], mul))
            TT(lam[0:64, 5:6], lam[0:64, 2:3], lam[0:64, 3:4], mul).then_inc(lamp_ready, 1)
            def mlp_low(m):
                dve.wait_ge(mlp_high_ready, m + 1)
                a = KT * UNIT_COLS - G_COLS
                TT(mlp_parts[:, m % 2, 1, 0:a], ring[:, (MLP_FIRST + m) % SLOTS, 0:a], mlp_parts[:, m % 2, 0, 0:a], sub).then_inc(mlp_low_ready, 1)

            mlp_low(0)
            mlp_low(1)
            for u in range(16):
                mlp_low(u + 2)
                dve.wait_ge(hid_high_ready, u + 1)
                v = hidden_now[:, u % 2, :]
                step(TT(v, v, v, mul))
                step.settle()
                TT(up[:, 2 * u:2 * u + 2, 1, :], split(v, SEQ), up[:, 2 * u:2 * u + 2, 0, :], sub).then_inc(up_ready, 1)
            for m in range(18, MLP_UNITS):
                mlp_low(m)
                if m == 22:
                    inv_rms("ss_ctx", CTX)
                    dve.wait_ge(ctx_loaded, 16)
                    TT(ctxT[:, :, :], ctxT[:, :, :], over(rB[:, 0:CTX], KT), mul).then_inc(h1_ready, 1)
            inv_rms("ss_mlp", SEQ)
            emptied(dve, ("down", 3))
            scaled(mix, mix, small("g_post_mlp"), SEQ)
            step.settle()
            TT(hT[:, :, :], hT[:, :, :], mix[:, :, :], add).then_inc(h1_ready, 1)

            def mod_bias(a, b):
                emptied(dve, ("mod", {16: 6, 40: 18, 48: 20}[b]))
                step(TT(modT[:, a:b, :], modT[:, a:b, :], each(small("b_mod")[:, a:b], 2), add))

            mod_bias(0, 16)
            emptied(dve, "lam")
            step(TT(lam[:, 4:5], lam[:, 7:8], lam[:, 6:7], sub))
            step(TS(small("subln"), small("subln"), 1.0 - LAM_INIT, None, mul))
            step.settle()
            step(TS(lam[:, 5:6], lam[:, 4:5], -LAM_INIT, None, add))
            step(STT(a1[:, :, :], modT[:, 8:16, :], 1.0, each(small("g_n1"), 2), add, mul))
            step.settle()
            for k in range(KT):
                step(TS(hcl[:, k, 0:CTX], ctxT[:, k, :], a1[:, k, 1:2], modT[:, k, 1:2], mul, add))
            inv_rms("ss_x", SEQ)
            for k in range(KT):
                step(STT(hcl[:, k, CTX:CTX + SEQ], hT[:, k, :], a1[:, k, 0:1], rB[:, 0:SEQ], mul, mul))
            step.settle()
            for k in range(KT):
                ins = TS(hcl[:, k, CTX:CTX + SEQ], hcl[:, k, CTX:CTX + SEQ], modT[:, k, 0:1], None, add)
                if k == KT - 1:
                    ins.then_inc(hcl_ready, 1)
                else:
                    step(ins)
            dve.wait_ge(c2_loaded, 16)
            for i in range(8):
                bank = full(dve, ("rot2", i))
                raw = q2[:, 2 * i:2 * i + 2, :] if i < 4 else k2[:, 2 * (i - 4):2 * (i - 4) + 2, CTX:CTX + SEQ]
                if i:
                    dve.wait_ge(roped2_ready, i)
                TT(split(rot3[:, 0, :], SEQ), split(bank[:, :], SEQ), over(cst2("sin_ax"), 2), mul).then_inc(free(("rot2", i)), 1)
                step(TT(split(rot3[:, 1, :], SEQ), raw, over(cst2("cos_ax"), 2), mul))
                step.settle()
                emptied(dve, ("rot2", i))
                TT(raw, split(rot3[:, 0, :], SEQ), split(rot3[:, 1, :], SEQ), add).then_inc(roped2_ready, 1)
            for n in range(len(ATT) + 1):
                if n < len(ATT):
                    st = stat2[:, n % 2, :]
                    for i in range(2):
                        nc.vector.tensor_reduce(st[:, i:i + 1], full(dve, ("s2", n, i))[:, :], AX, ALU.max, negate=True).then_inc(free(("s2", n, i)), 1)
                    dve.wait_ge(banks.free[banks.at[("s2", n, 1)]], banks.free_when[("s2", n, 1)] - 1)
                    TS(st[:, 2:4], st[:, 0:2], 0.125, None, mul).then_inc(nmax_ready, 1)
                if n >= 1:
                    k = n - 1
                    st = stat2[:, k % 2, :]
                    emptied(dve, ("s2", k, 0))
                    emptied(dve, ("s2", k, 1))
                    step(nc.vector.reciprocal(st[:, 6:8], st[:, 4:6]))
                    step.settle()
                    step(TT(st[:, 7:8], st[:, 7:8], lam[:, 5:6], mul))
                    step(TS(esc[:, k % 2, 0, :], esc[:, k % 2, 0, :], st[:, 6:7], None, mul))
                    step.settle()
                    STT(esc[:, k % 2, 0, :], esc[:, k % 2, 1, :], st[:, 7:8], esc[:, k % 2, 0, :], mul, add).then_inc(prob_ready, 1)
            for j in range(4):
                emptied(dve, ("hss", j))
                r = q2[:, 2 * j:2 * j + 2, :].rearrange("p a b -> p (a b)")
                hj = heads[:, 2 * j:2 * j + 2, :].rearrange("p a b -> p (a b)")
                step(nc.vector.reciprocal(r, r))
                step.settle()
                ins = STT(hj, hj, small("subln"), r, mul, mul)
                if j == 3:
                    ins.then_inc(heads_ready, 1)
                else:
                    step(ins)
            for u in range(4):
                emptied(dve, ("gate2a", u))
                m = merged2[:, 2 * u:2 * u + 2, :].rearrange("p a b -> p (a b)")
                TT(m, gate2[:, 0, :], full(dve, ("ao2", u))[:, :], mul).then_inc(free(("ao2", u)), 1)
                emptied(dve, ("gate2f", u))
                TT(rot3[:, u % 2, :], gate2[:, 1, :], full(dve, ("fo", u))[:, :], mul).then_inc(free(("fo", u)), 1)
                emptied(dve, ("ao2", u))
                emptied(dve, ("fo", u))
                TT(m, m, rot3[:, u % 2, :], add).then_inc(merged2_ready, 1)
            mod_bias(16, 40)
            step.settle()
            step(STT(a2[:, :], modT[:, 32:40, 0], 1.0, small("g_n2"), add, mul))
            for u in range(4):
                bank = full(dve, ("wo2", u))
                for j in range(2):
                    k = 2 * u + j
                    ins = STT(hT[:, k, :], bank[:, j * SEQ:(j + 1) * SEQ], modT[:, 16 + k, 0:1], hT[:, k, :], mul, add)
                    if j == 1:
                        ins.then_inc(free(("wo2", u)), 1)
            emptied(dve, ("wo2", 3))
            inv_rms("ss_x1", SEQ)
            scaled(h2, hT, a2, SEQ)
            step.settle()
            for k in range(KT):
                ins = TS(h2[:, k, :], h2[:, k, :], modT[:, 24 + k, 0:1], None, add)
                if k == KT - 1:
                    ins.then_inc(h2_ready, 1)
                else:
                    step(ins)
            step(nc.vector.memset(spread[:, :, :], 0.0))
            for i in range(4):
                nc.vector.memset(yb[:, i // 2, i % 2 * 512:(i % 2 + 1) * 512], 0.0).then_inc(ys_ready, 1)
            step(TT(fold[:, :], ident[:, 0:CAP], ident[:, CAP:2 * CAP], add))
            for j in range(4):
                step(nc.vector.memset(rflat(300 + j, 1), float(4 - j)))
            rank = over(rflat(300, 4), 2)

            def r2(a, n=4):
                return rflat(a, 2 * n).rearrange("p (q n) -> p q n", n=n)

            def one(a):
                return each(rflat(a, 2), 4)

            def now(ins):
                step(ins)
                step.settle()

            def first_of(dst, src, best_at, tmp, tmp2):
                now(nc.vector.tensor_reduce(rflat(best_at, 2), src, AX, ALU.max))
                now(TT(r2(tmp), src, one(best_at), ALU.is_equal))
                now(TT(r2(tmp), r2(tmp), rank, mul))
                now(nc.vector.tensor_reduce(rflat(tmp2, 2), r2(tmp), AX, ALU.max))
                now(TT(r2(dst), r2(tmp), one(tmp2), ALU.is_equal))

            bank = full(dve, "router")
            logits = rflat(0, 40).rearrange("p (q n) -> p q n", n=20)
            TT(logits, bank[:, 0:40].rearrange("p (q n) -> p q n", n=20), over(small("b_router"), 2), add).then_inc(free("router"), 1)
            emptied(dve, "router")
            lg = logits[:, :, 0:4]
            first_of(72, lg, 40, 48, 64)
            TT(r2(80), lg, one(40), sub).then_inc(rexp_arg_ready, 1)
            for g in range(4):
                chosen = rflat(72, 8).rearrange("p (q n) -> p q n", n=4)[:, :, g:g + 1].to_broadcast([128, 2, 4])
                if g == 0:
                    now(TT(r2(96), logits[:, :, 4:8], chosen, mul))
                else:
                    now(TT(r2(104), logits[:, :, 4 + 4 * g:8 + 4 * g], chosen, mul))
                    now(TT(r2(96), r2(96), r2(104), add))
            first_of(112, r2(96), 120, 128, 136)
            now(STT(r2(144), r2(112), -1.0e30, r2(96), mul, add))
            first_of(152, r2(144), 160, 168, 176)
            TT(rflat(180, 2), rflat(160, 2), rflat(120, 2), sub).then_inc(rexp_arg_ready, 1)
            dve.wait_ge(rexp_ready, 2)
            now(nc.vector.tensor_reduce(rflat(190, 2), r2(80), AX, add))
            now(nc.vector.reciprocal(rflat(192, 2), rflat(190, 2)))
            now(TS(rflat(194, 2), rflat(180, 2), 1.0, None, add))
            now(nc.vector.reciprocal(rflat(196, 2), rflat(194, 2)))
            now(TT(rflat(198, 2), rflat(196, 2), rflat(192, 2), mul))
            now(TT(rflat(202, 2), rflat(198, 2), rflat(180, 2), mul))
            now(TT(r2(208), r2(112), one(198), mul))
            now(TT(r2(216), r2(152), one(202), mul))
            now(TT(r2(208), r2(208), r2(216), add))
            for qt in range(2):
                ins = TT(rt[:, 18 + qt, 0:16].rearrange("p (g j) -> p g j", j=4), each(rflat(72 + 4 * qt, 4), 4), over(rflat(208 + 4 * qt, 4), 4), mul)
                step(ins)
            now(TT(r2(224), r2(112), r2(152), add))
            for qt in range(2):
                ins = TT(rt[:, 20 + qt, 0:16].rearrange("p (g j) -> p g j", j=4), each(rflat(72 + 4 * qt, 4), 4), over(rflat(224 + 4 * qt, 4), 4), mul)
                if qt == 1:
                    ins.then_inc(routed_ready, 1)
                else:
                    step(ins)
            step.settle()
            dve.wait_ge(routed_ready, 1)
            bank = full(dve, "rank")
            for qt in range(2):
                m = rt[:, 20 + qt, 0:16]
                place = rt[:, 16 + qt, 0:16]
                now(TS(place, bank[:, qt * 16:(qt + 1) * 16], float(1 + CAP), None, add))
                now(TT(place, place, m, mul))
                now(TS(place, place, 1.0, None, sub))
            CP(rt[:, 22, 0:16], bank[:, 32:48]).then_inc(free("rank"), 1)
            emptied(dve, "rank")
            now(nc.vector.tensor_reduce(rt[:, 23, 0:8], rt[:, 22, 0:16].rearrange("p (a b) -> p a b", b=2), AX, ALU.max))
            now(TS(rt[:, 23, 8:16], rt[:, 23, 0:8], float(CAP), 1.0, ALU.is_gt, add))
            for i in range(2, SEQ // CAP):
                now(STT(rt[:, 23, 8:16], rt[:, 23, 0:8], float(CAP * i), rt[:, 23, 8:16], ALU.is_gt, add))
            CP(passes[:, :], rt[:, 23, 8:16]).then_inc(passes_ready, 1)

            mod_bias(40, 48)
            now(CP(rt[:, 22, 0:1], rt[:, 23, 8:9]))
            for p in range(1, PAIRS):
                now(TT(rt[:, 22, p:p + 1], rt[:, 22, p - 1:p], rt[:, 23, 8 + p:9 + p], add))
            of = rt[:, 15, 0:MAX_PASSES]
            now(TS(of, cst2("iota")[:, 0:MAX_PASSES], rt[:, 22, 0:1], None, ALU.is_ge))
            for p in range(1, PAIRS - 1):
                now(STT(of, cst2("iota")[:, 0:MAX_PASSES], rt[:, 22, p:p + 1], of, ALU.is_ge, add))
            step(CP(plan[:, 0:MAX_PASSES], of))
            CP(plan[:, MAX_PASSES:MAX_PASSES + 1], rt[:, 22, PAIRS - 1:PAIRS]).then_inc(plan_ready, 1)

            STEPS = 10

            def start_pair(pair):
                for qt in range(2):
                    CP(slot_of[:, qt, :], rt[:, 16 + qt, bass.ds(pair * 2, 2)]).then_inc(slots_loaded, 1)
                    CP(gate_of[:, qt, :], rt[:, 18 + qt, bass.ds(pair * 2, 2)]).then_inc(slots_loaded, 1)
                dve.wait_ge(slots_loaded, 4 * pair + 4)

            def expert_pass(pair, n):
                taken = [0]

                def stp(ins, wait=True):
                    taken[0] += 1
                    ins.then_inc(moe_step, 1)
                    if wait:
                        dve.wait_ge(moe_step, n * STEPS + taken[0])

                lows = [0]

                def low_part(i):
                    dve.wait_ge(high_ready, n * EXPERT_UNITS + (i + 1))
                    TT(parts[:, i % SPLITS, 1, :], ring[:, i % SLOTS, :], parts[:, i % SPLITS, 0, :], sub).then_inc(low_ready, 1)
                    lows[0] += 1

                def hidden(j):
                    dve.wait_ge(sig_w1_ready[j], n + 1)
                    stp(TT(sg[:, j, :], sg[:, j, :], psum[1 + j][:, 0:4 * CAP], mul))
                    stp(TT(hid[:, j, :], sg[:, j, :], psum[1 + j][:, 4 * CAP:8 * CAP], mul))
                    stp(CP(hids[:, j, :, 0:CAP], split(hid[:, j, :], CAP)))
                    TT(hids[:, j, :, CAP:2 * CAP], split(hid[:, j, :], CAP), hids[:, j, :, 0:CAP], sub).then_inc(hid_ready[j], 1)

                stp(TS(slot_of[:, :, :], slot_of[:, :, :], float(CAP), None, sub))
                for j in range(2):
                    for qt in range(2):
                        TS(pick[:, qt, j * CAP:(j + 1) * CAP], cst2("iota"), slot_of[:, qt, j:j + 1], None, ALU.is_equal).then_inc(pick_ready, 1)
                for j in range(2):
                    for qt in range(2):
                        TS(pick_gated[:, qt, j, :, :], over(cst2("iota"), 2), slot_of[:, qt, j:j + 1], gate_of[:, qt, j:j + 1], ALU.is_equal, mul).then_inc(pick_ready, 1)
                low_part(0)
                dve.wait_ge(gathered, n + 1)
                for i, b in enumerate((0, 3)):
                    x = psum[b][:, :].rearrange("p (k j c) -> p k j c", j=2, c=CAP)
                    stp(CP(xs[:, 4 * i:4 * i + 4, :, 0:CAP], x), False)
                dve.wait_ge(moe_step, n * STEPS + taken[0])
                for i, b in enumerate((0, 3)):
                    x = psum[b][:, :].rearrange("p (k j c) -> p k j c", j=2, c=CAP)
                    ins = TT(xs[:, 4 * i:4 * i + 4, :, CAP:2 * CAP], x, xs[:, 4 * i:4 * i + 4, :, 0:CAP], sub)
                    if i == 1:
                        ins.then_inc(xs_ready, 1)
                    else:
                        stp(ins, False)
                for i in (2, 3, 5, 6, 8):
                    low_part(i)
                hidden(0)
                low_part(9)
                hidden(1)
                low_part(11)
                assert taken[0] == STEPS and lows[0] == 8, taken

            total = each_pass(dve, expert_pass, start_pair)
            dve.wait_ge(scattered, 1)
            for k in range(KT):
                ins = STT(hT[:, k, :], psum[4 + k // 2][:, (k % 2) * SEQ:(k % 2 + 1) * SEQ], modT[:, 40 + k, 0:1], hT[:, k, :], mul, add)
                if k == KT - 1:
                    ins.then_inc(h1_ready, 1)
                else:
                    step(ins)
            step.settle()
            inv_rms("ss_out", SEQ)
            scaled(mix2, hT, small("g_final"), SEQ, out_ready)


def _freqs(dim):
    return (10000.0 ** (-(np.arange(0, dim, 2) / dim))).astype(np.float32)


def _rotation(block):
    r = np.zeros((128, 128), np.float32)
    for p in range(128):
        q = p % block
        if q < block // 2:
            r[p, p + block // 2] = -1.0
        else:
            r[p, p - block // 2] = 1.0
    return r.T


def _constants_one():
    c = np.zeros((128, C1_W), np.float32)

    def put(name, a):
        at, w = C1[name]
        c[:, at:at + w] = np.asarray(a).reshape(128, w)

    p, f = np.arange(128)[:, None], np.arange(128)[None, :]
    put("ident", p == f)
    put("upper", p <= f)
    put("rot_att", _rotation(128))
    put("rot_idx", _rotation(64))
    for name, dim in (("att", 128), ("idx", 64)):
        inv = _freqs(dim)
        ang = (np.arange(T, dtype=np.float32)[None, :] * inv[np.arange(128) % (dim // 2)][:, None]).astype(np.float64)
        put("cos_" + name, np.cos(ang))
        put("sin_" + name, np.sin(ang))
    put("meta_upper", (p // META == f // META) & (p <= f))
    put("meta_last", f == p // META * META + META - 1)
    put("levels", np.concatenate([(p >> (l + 1) == f >> (l + 1)) & ((p >> l) % 2 == 0) & ((f >> l) % 2 == 1) for l in range(LEVELS)], 1))
    key = np.arange(T)[None, :]
    put("causal", np.concatenate([np.where(key <= META + qt * 128 + p, 0.0, NEG) for qt in range(2)], 1))
    put("head_rows", p // META == np.arange(H)[None, :])
    return c


def _constants_two():
    c = np.zeros((128, C2_W), np.float32)

    def put(name, a):
        at, w = C2[name]
        c[:, at:at + w] = np.asarray(a).reshape(128, w)

    put("rot_ax", _rotation(32))
    p, n = np.arange(128), np.arange(SEQ)
    inv = (1.0 / (10000.0 ** (np.arange(16) / 16))).astype(np.float32)
    pos = np.where((p % 64 // 32 == 0)[:, None], (n // 64)[None, :], (n % 64)[None, :]).astype(np.float32)
    ang = (pos * inv[p % 16][:, None]).astype(np.float64)
    put("cos_ax", np.cos(ang))
    put("sin_ax", np.sin(ang))
    d = 2 * np.pi * np.outer(p, p) / 128
    put("dft_d", np.concatenate([np.cos(d), np.sin(d)], 1) / np.sqrt(128))
    t = 2 * np.pi * np.outer(n, n) / SEQ
    put("earlier", p[:, None] < p[None, :])
    put("iota", np.broadcast_to(np.arange(CAP), (128, CAP)))
    put("dft_n", np.concatenate([m[nt * 128:(nt + 1) * 128] for nt in range(2) for m in (np.cos(t), -np.sin(t))], 1) / np.sqrt(SEQ))
    return c


def _unit(w, rows, cols):
    return w[rows, cols].reshape(-1, 128, cols.stop - cols.start).transpose(1, 0, 2).reshape(128, -1)


def _stream(x):
    w_in, w_in2 = x["w_in"][0], x["w_in_2"][0]
    every = slice(0, D)
    offsets = {"gq": 0, "gk": 1024, "gv": 2048, "gz": 3072, "aq": 4112, "ak": 5136, "av": 5392, "iq": 5648, "gate_a": 6232, "gate_b": 7256}
    offsets2 = {"q2": 0, "k2": 1024, "v2": 2048, "f2": 3072, "gate2a": 3584, "gate2f": 4608}
    whole = {"mod": x["w_mod_2"][0], "bg": x["w_branch_gdn"][0], "bd": x["w_branch_dsa"][0], "wo": x["w_out"][0], "up": x["w_up"][0],
             "ao": x["w_attn_out_2"][0], "wo2": x["w_out_2"][0]}
    s = np.empty((len(ORDER), 128, KT * UNIT_COLS), np.float32)
    for i, (kind, u) in enumerate(ORDER):
        c = slice(u * 256, (u + 1) * 256)
        if kind in offsets:
            s[i] = _unit(w_in, every, slice(offsets[kind] + c.start, offsets[kind] + c.stop))
        elif kind in offsets2:
            s[i] = _unit(w_in2, every, slice(offsets2[kind] + c.start, offsets2[kind] + c.stop))
        elif kind in whole:
            s[i] = _unit(whole[kind], every, c)
        elif kind == "down":
            cp, kg = divmod(u, 4)
            s[i] = _unit(x["w_down"][0], slice(kg * D, (kg + 1) * D), slice(cp * 256, (cp + 1) * 256))
        elif kind == "fo":
            s[i] = _unit(x["w_four_out_2"][0], slice(0, 512), slice(u * 512, (u + 1) * 512))
        elif kind == "e_up":
            e, q = divmod(u, 4)
            w = x["w_exp_gate_2" if q < 2 else "w_exp_up_2"][0, e]
            s[i] = _unit(w, every, slice(q % 2 * 256, (q % 2 + 1) * 256))
        else:
            e, q = divmod(u, 2)
            s[i] = _unit(x["w_exp_down_2"][0, e], slice(0, EH), slice(q * 512, (q + 1) * 512))
    return s


def _smalls(x):
    c = np.zeros((128, SM_W), np.float32)

    def put(name, a):
        at, w = SM[name]
        c[:, at:at + w] = a.reshape(128, w)

    def cols(v):
        return v.reshape(-1, 128).T

    for name, v in (("g_pre_mix", x["pre_mix_norm"]), ("g_post_mix", x["post_mix_norm"]), ("g_pre_mlp", x["pre_mlp_norm"]),
                    ("g_post_mlp", x["post_mlp_norm"]), ("g_n1", x["norm1_g_2"]), ("g_n2", x["norm2_g_2"]), ("g_final", x["final_g_2"]),
                    ("gdn_norm", x["gdn_norm"]), ("subln", x["subln_g_2"]), ("b_mod", x["b_mod_2"])):
        put(name, cols(v))
    put("conv", x["conv_w"][0].reshape(4, 24, 128).transpose(2, 1, 0))
    put("c", np.stack([cols(x["c_2"]), cols(x["c_ctx_2"])], 2))
    put("dt_bias", np.broadcast_to(x["dt_bias"], (128, H)))
    put("a_log", np.broadcast_to(x["a_log"], (128, H)))
    put("b_router", np.broadcast_to(np.concatenate([x["b_router_group_2"][0], x["b_router_expert_2"][0]]), (128, 20)))
    return c


def _small_weights(x):
    w = x["w_in"][0]

    def cols(a, b):
        return w[:, a:b].reshape(KT, 128, b - a).transpose(1, 0, 2)

    ik = cols(6160, 6224)
    return np.concatenate([cols(4096, 4112).reshape(128, -1), np.concatenate([ik, ik], 2).reshape(128, -1),
                           cols(6224, 6232).reshape(128, -1)], 1)


def _columns(a):
    return np.ascontiguousarray(a.T.reshape(KT, 128, -1).transpose(1, 0, 2))


def kernel(**inputs):
    import concourse.bacc as bacc
    from concourse.bass_utils import run_bass_kernel_spmd

    x = {name: np.asarray(a) for name, a in inputs.items()}
    router = np.concatenate([x["w_router_group_2"][0], x["w_router_expert_2"][0]], 1)
    arrays = {
        "stream": _stream(x),
        "h_in": _columns(np.concatenate([x["meta_tokens"], x["x"][0]])),
        "ctx_in": _columns(x["ctx_2"][0]),
        "constants_one": _constants_one(),
        "constants_two": _constants_two(),
        "smalls": _smalls(x),
        "small_weights": _small_weights(x),
        "router": np.ascontiguousarray(router.reshape(KT, 128, 20).transpose(1, 0, 2)),
        "lambdas": np.stack([x["lam_q1_2"][0], x["lam_k1_2"][0], x["lam_q2_2"][0], x["lam_k2_2"][0]], 1),
    }
    nc = bacc.Bacc("TRN2", target_bir_lowering=False, num_devices=1)
    args = [nc.dram_tensor(name, a.shape, mybir.dt.float32, kind="ExternalInput").ap() for name, a in arrays.items()]
    args.append(nc.dram_tensor("result", (128, KT, SEQ), mybir.dt.float32, kind="ExternalOutput").ap())
    build(nc, *args)
    r = run_bass_kernel_spmd(nc, [arrays], core_ids=[0])
    return np.ascontiguousarray(r.results[0]["result"].transpose(2, 1, 0)).reshape(1, SEQ, D)
```
